# Optimizing a Trainium2 kernel written in Bass

```python
import jax, jax.numpy as jnp
from jax import lax
import numpy as np
import jax
import jax.numpy as jnp

D_MODEL = 1024
BATCH = 1
SEQ = 256
DEPTH = 1

N_HEADS = 16
HEAD_DIM = 64
ATTN_WIDTH = N_HEADS * HEAD_DIM
KV_LATENT = 128
IDX_HEADS = 8
IDX_DIM = 64
TOPK_MAX = 256
Q_BLOCK = 128
RNN_WIDTH = 1024
RNN_BLOCKS = 16
RNN_BLOCK_DIM = RNN_WIDTH // RNN_BLOCKS
CONV_WIDTH = 4
LRU_C = 8.0
NORM_EPS = 1e-6
SPLITS = (ATTN_WIDTH, KV_LATENT, IDX_HEADS * IDX_DIM, IDX_DIM, IDX_HEADS, ATTN_WIDTH, RNN_WIDTH, RNN_WIDTH, 2 * D_MODEL)
IN_WIDTH = sum(SPLITS)


def rms_norm(x, g):
    xf = x.astype(jnp.float32)
    y = xf * lax.rsqrt(jnp.mean(xf * xf, axis=-1, keepdims=True) + NORM_EPS)
    return (y * g.astype(jnp.float32)).astype(x.dtype)

def layer_norm(x, g, b):
    xf = x.astype(jnp.float32)
    mu = jnp.mean(xf, axis=-1, keepdims=True)
    xc = xf - mu
    y = xc * lax.rsqrt(jnp.mean(xc * xc, axis=-1, keepdims=True) + NORM_EPS)
    return (y * g.astype(jnp.float32) + b.astype(jnp.float32)).astype(x.dtype)

def alibi_slopes(n):
    return jnp.exp2(-8.0 * jnp.arange(1, n + 1, dtype=jnp.float32) / n)

def split_cols(z):
    offsets = np.cumsum(np.array(SPLITS))[:-1].tolist()
    return jnp.split(z, offsets, axis=-1)

def sparse_mla_attention(q, c_kv, q_idx, k_idx, w_idx, w_uk, w_uv):
    B, S = q.shape[0], q.shape[1]
    topk = min(TOPK_MAX, S // 4)
    tb = min(Q_BLOCK, S)
    nblk = S // tb
    f32 = jnp.float32
    q_lat = jnp.einsum('bshd,hcd->bshc', q, w_uk) * (HEAD_DIM ** -0.5)
    slopes = alibi_slopes(N_HEADS)
    key_pos = jnp.arange(S, dtype=jnp.int32)
    k_idx_f = k_idx.astype(f32)

    def to_blocks(a):
        return a.reshape((B, nblk, tb) + a.shape[2:]).swapaxes(0, 1)

    def block_fn(args):
        ql, qi, wi, t0 = args
        t = t0 + jnp.arange(tb, dtype=jnp.int32)
        s_idx = jax.nn.relu(jnp.einsum('btjd,bsd->btjs', qi.astype(f32), k_idx_f))
        s_idx = jnp.einsum('btjs,btj->bts', s_idx, wi.astype(f32))
        causal = key_pos[None, :] <= t[:, None]
        s_idx = jnp.where(causal[None], s_idx, -jnp.inf)
        _, idx = lax.top_k(s_idx, topk)
        c_sel = jax.vmap(lambda c, i: c[i])(c_kv, idx).astype(f32)
        logits = jnp.einsum('bthc,btkc->bthk', ql.astype(f32), c_sel)
        dist = (t[None, :, None] - idx).astype(f32)
        logits = logits - slopes[None, None, :, None] * dist[:, :, None, :]
        valid = idx <= t[None, :, None]
        logits = jnp.where(valid[:, :, None, :], logits, -jnp.inf)
        p = jax.nn.softmax(logits, axis=-1)
        o = jnp.einsum('bthk,btkc->bthc', p, c_sel)
        return o.astype(ql.dtype)

    t0s = jnp.arange(nblk, dtype=jnp.int32) * tb
    o_lat = lax.map(block_fn, (to_blocks(q_lat), to_blocks(q_idx), to_blocks(w_idx), t0s))
    o_lat = o_lat.swapaxes(0, 1).reshape(B, S, N_HEADS, KV_LATENT)
    return jnp.einsum('bshc,hcd->bshd', o_lat, w_uv)

def causal_depthwise_conv(x, w, b):
    S = x.shape[1]
    xp = jnp.pad(x, ((0, 0), (CONV_WIDTH - 1, 0), (0, 0)))
    out = b
    for k in range(CONV_WIDTH):
        out = out + xp[:, k:k + S] * w[k]
    return out

def rg_lru(x, w_a, b_a, w_x, b_x, lam):
    B, S, C = x.shape
    f32 = jnp.float32
    xb = x.reshape(B, S, RNN_BLOCKS, RNN_BLOCK_DIM)
    r = jax.nn.sigmoid(jnp.einsum('bsgi,gij->bsgj', xb, w_a).reshape(B, S, C) + b_a).astype(f32)
    i = jax.nn.sigmoid(jnp.einsum('bsgi,gij->bsgj', xb, w_x).reshape(B, S, C) + b_x).astype(f32)
    log_a = -LRU_C * r * jax.nn.softplus(-lam.astype(f32))
    a = jnp.exp(log_a)
    b_in = jnp.sqrt(-jnp.expm1(2.0 * log_a)) * (i * x.astype(f32))

    def combine(left, right):
        a1, b1 = left
        a2, b2 = right
        return a1 * a2, a2 * b1 + b2

    _, h = lax.associative_scan(combine, (a, b_in), axis=1)
    return h.astype(x.dtype)

def hybrid_layer(x, norm_g, w_in, b_merge, kv_norm_g, w_uk, w_uv, idx_ln_g, idx_ln_b,
                 w_attn_proj, conv_w, conv_b, w_rg_a, b_rg_a, w_rg_x, b_rg_x, lru_lambda,
                 w_rnn_proj, w_out):
    B, S, _ = x.shape
    xn = rms_norm(x, norm_g)
    z = xn @ w_in
    q, c_kv, q_idx, k_idx, w_idx, g_attn, x_rnn, g_rnn, merge = split_cols(z)
    q = q.reshape(B, S, N_HEADS, HEAD_DIM)
    c_kv = rms_norm(c_kv, kv_norm_g)
    q_idx = q_idx.reshape(B, S, IDX_HEADS, IDX_DIM) * (IDX_DIM ** -0.5)
    k_idx = layer_norm(k_idx, idx_ln_g, idx_ln_b)
    w_idx = w_idx * (IDX_HEADS ** -0.5)
    o = sparse_mla_attention(q, c_kv, q_idx, k_idx, w_idx, w_uk, w_uv).reshape(B, S, ATTN_WIDTH)
    y_attn = (o * jax.nn.silu(g_attn)) @ w_attn_proj
    h = rg_lru(causal_depthwise_conv(x_rnn, conv_w, conv_b), w_rg_a, b_rg_a, w_rg_x, b_rg_x, lru_lambda)
    y_rnn = (h * jax.nn.silu(g_rnn)) @ w_rnn_proj
    gates = jax.nn.sigmoid(merge + b_merge)
    g_a, g_r = gates[..., :D_MODEL], gates[..., D_MODEL:]
    mixed = g_a * y_attn + g_r * y_rnn
    return x + mixed @ w_out

def first_inputs(seed: int = 0) -> dict:
    key = jax.random.key(seed)
    ks = jax.random.split(key, 24)
    f32 = jnp.float32

    def nrm(k, shape, scale):
        return jax.random.normal(k, shape, f32) * scale

    u = jax.random.uniform(ks[20], (DEPTH, RNN_WIDTH), f32, minval=0.9, maxval=0.999)
    return {
        'x': jax.random.normal(ks[0], (BATCH, SEQ, D_MODEL), f32),
        'norm_gain': 1.0 + nrm(ks[1], (DEPTH, D_MODEL), 0.01),
        'w_in': nrm(ks[2], (DEPTH, D_MODEL, IN_WIDTH), D_MODEL ** -0.5),
        'b_merge': nrm(ks[3], (DEPTH, 2 * D_MODEL), 0.01),
        'kv_norm_gain': 1.0 + nrm(ks[4], (DEPTH, KV_LATENT), 0.01),
        'w_uk': nrm(ks[5], (DEPTH, N_HEADS, KV_LATENT, HEAD_DIM), KV_LATENT ** -0.5),
        'w_uv': nrm(ks[6], (DEPTH, N_HEADS, KV_LATENT, HEAD_DIM), KV_LATENT ** -0.5),
        'idx_ln_gain': 1.0 + nrm(ks[7], (DEPTH, IDX_DIM), 0.01),
        'idx_ln_bias': nrm(ks[8], (DEPTH, IDX_DIM), 0.01),
        'w_attn_proj': nrm(ks[9], (DEPTH, ATTN_WIDTH, D_MODEL), ATTN_WIDTH ** -0.5),
        'conv_w': nrm(ks[10], (DEPTH, CONV_WIDTH, RNN_WIDTH), CONV_WIDTH ** -0.5),
        'conv_b': nrm(ks[11], (DEPTH, RNN_WIDTH), 0.01),
        'w_rg_a': nrm(ks[12], (DEPTH, RNN_BLOCKS, RNN_BLOCK_DIM, RNN_BLOCK_DIM), RNN_BLOCK_DIM ** -0.5),
        'b_rg_a': nrm(ks[13], (DEPTH, RNN_WIDTH), 0.01),
        'w_rg_x': nrm(ks[14], (DEPTH, RNN_BLOCKS, RNN_BLOCK_DIM, RNN_BLOCK_DIM), RNN_BLOCK_DIM ** -0.5),
        'b_rg_x': nrm(ks[15], (DEPTH, RNN_WIDTH), 0.01),
        'lru_lambda': jnp.log(u) - jnp.log1p(-u),
        'w_rnn_proj': nrm(ks[16], (DEPTH, RNN_WIDTH, D_MODEL), RNN_WIDTH ** -0.5),
        'w_out': nrm(ks[17], (DEPTH, D_MODEL, D_MODEL), D_MODEL ** -0.5),
        'final_norm_gain': 1.0 + nrm(ks[18], (D_MODEL,), 0.01),
    }

def first_block(x, norm_gain, w_in, b_merge, kv_norm_gain, w_uk, w_uv, idx_ln_gain, idx_ln_bias,
              w_attn_proj, conv_w, conv_b, w_rg_a, b_rg_a, w_rg_x, b_rg_x, lru_lambda,
              w_rnn_proj, w_out, final_norm_gain):
    for l in range(DEPTH):
        x = hybrid_layer(x, norm_gain[l], w_in[l], b_merge[l], kv_norm_gain[l], w_uk[l], w_uv[l],
                         idx_ln_gain[l], idx_ln_bias[l], w_attn_proj[l], conv_w[l], conv_b[l],
                         w_rg_a[l], b_rg_a[l], w_rg_x[l], b_rg_x[l], lru_lambda[l],
                         w_rnn_proj[l], w_out[l])
    return rms_norm(x, final_norm_gain)


ROPE_THETA = 500000.0
MLA_HEADS = 8
MLA_NOPE = 64
MLA_ROPE = 32
MLA_V = 64
KV_LORA = 4 * MLA_V
Q_LORA = 3 * KV_LORA
ATTN_Q_BLOCK = 128
MOBA_HEADS = 8
MOBA_HD = 64
MOBA_ROT = MOBA_HD // 4
MOBA_BLOCK = 256
MOBA_TOPK = 3
MOBA_Q_CHUNK = 32
N_GROUPS = 4
EXPERTS_PER_GROUP = 8
N_EXPERTS = N_GROUPS * EXPERTS_PER_GROUP
EXPERT_TOPK = 2
EXPERT_FF = 256
EXPERT_BLOCK = 256
IN_SPLITS = (Q_LORA, KV_LORA, MLA_ROPE,
             MOBA_HEADS * MOBA_HD, MOBA_HEADS * MOBA_HD, MOBA_HEADS * MOBA_HD,
             D_MODEL, D_MODEL)
IN_WIDTH_2 = sum(IN_SPLITS)


def rmsnorm(x, g):
    xf = x.astype(jnp.float32)
    y = xf * lax.rsqrt(jnp.mean(xf * xf, axis=-1, keepdims=True) + NORM_EPS)
    return (y * g.astype(jnp.float32)).astype(x.dtype)

def rope_tables(seq, rot_dim):
    half = rot_dim // 2
    inv_freq = jnp.power(ROPE_THETA, -jnp.arange(half, dtype=jnp.float32) / half)
    ang = jnp.arange(seq, dtype=jnp.float32)[:, None] * inv_freq[None, :]
    return jnp.cos(ang), jnp.sin(ang)

def apply_rope(x, cos, sin):
    half = x.shape[-1] // 2
    xf = x.astype(jnp.float32)
    x1, x2 = xf[..., :half], xf[..., half:]
    c = cos[None, :, None, :]
    s = sin[None, :, None, :]
    return jnp.concatenate([x1 * c - x2 * s, x2 * c + x1 * s], axis=-1).astype(x.dtype)

def causal_dense_attention(q, k, v):
    B, S, H, Dq = q.shape
    Dv = v.shape[-1]
    scale = Dq ** -0.5
    nqb = S // ATTN_Q_BLOCK
    q_blocks = q.reshape(B, nqb, ATTN_Q_BLOCK, H, Dq).transpose(1, 0, 2, 3, 4)
    kpos = jnp.arange(S)

    def block(args):
        qi, i = args
        s = jnp.einsum('bqhd,bkhd->bhqk', qi, k).astype(jnp.float32) * scale
        qpos = i * ATTN_Q_BLOCK + jnp.arange(ATTN_Q_BLOCK)
        s = jnp.where(kpos[None, :] <= qpos[:, None], s, -jnp.inf)
        p = jax.nn.softmax(s, axis=-1).astype(v.dtype)
        return jnp.einsum('bhqk,bkhd->bqhd', p, v)

    o = lax.map(block, (q_blocks, jnp.arange(nqb)))
    return o.transpose(1, 0, 2, 3, 4).reshape(B, S, H * Dv)

def mla_attention(c_q, c_kv, k_r, q_norm, w_uq, kv_norm, w_ukv, cos, sin):
    B, S, _ = c_q.shape
    q = (rmsnorm(c_q, q_norm) @ w_uq).reshape(B, S, MLA_HEADS, MLA_NOPE + MLA_ROPE)
    q = jnp.concatenate([q[..., :MLA_NOPE], apply_rope(q[..., MLA_NOPE:], cos, sin)], axis=-1)
    kv = (rmsnorm(c_kv, kv_norm) @ w_ukv).reshape(B, S, MLA_HEADS, MLA_NOPE + MLA_V)
    k_nope, v = kv[..., :MLA_NOPE], kv[..., MLA_NOPE:]
    k_rope = apply_rope(k_r[:, :, None, :], cos, sin)
    k = jnp.concatenate([k_nope, jnp.broadcast_to(k_rope, (B, S, MLA_HEADS, MLA_ROPE))], axis=-1)
    return causal_dense_attention(q, k, v)

def moba_attention(q, k, v, cos, sin):
    B, S, H, dh = q.shape
    scale = dh ** -0.5
    q = jnp.concatenate([apply_rope(q[..., :MOBA_ROT], cos, sin), q[..., MOBA_ROT:]], axis=-1)
    k = jnp.concatenate([apply_rope(k[..., :MOBA_ROT], cos, sin), k[..., MOBA_ROT:]], axis=-1)
    nb = -(-S // MOBA_BLOCK)
    pad = nb * MOBA_BLOCK - S
    kp = jnp.pad(k, ((0, 0), (0, pad), (0, 0), (0, 0)))
    vp = jnp.pad(v, ((0, 0), (0, pad), (0, 0), (0, 0)))
    k_blocks = kp.reshape(B, nb, MOBA_BLOCK, H, dh).transpose(0, 3, 1, 2, 4)
    v_blocks = vp.reshape(B, nb, MOBA_BLOCK, H, dh).transpose(0, 3, 1, 2, 4)
    k_mean = jnp.mean(k_blocks.astype(jnp.float32), axis=3)
    n_sel = min(MOBA_TOPK, nb)
    gather = jax.vmap(jax.vmap(lambda blocks, idx: blocks[idx]))
    nqc = S // MOBA_Q_CHUNK
    q_chunks = q.reshape(B, nqc, MOBA_Q_CHUNK, H, dh).transpose(1, 0, 3, 2, 4)
    blk_ids = jnp.arange(nb)
    sel_ids = jnp.arange(n_sel)

    def chunk(args):
        qc, c = args
        q0 = c * MOBA_Q_CHUNK
        own = q0 // MOBA_BLOCK
        qpos = q0 + jnp.arange(MOBA_Q_CHUNK)
        gate = jnp.einsum('bhqd,bhnd->bhqn', qc.astype(jnp.float32), k_mean)
        gate = jnp.where(blk_ids < own, gate, -jnp.inf)
        _, idx = lax.top_k(gate, n_sel)
        valid = sel_ids < own
        k_sel = gather(k_blocks, idx)
        v_sel = gather(v_blocks, idx)
        s_sel = jnp.einsum('bhqd,bhqjkd->bhqjk', qc, k_sel).astype(jnp.float32) * scale
        s_sel = jnp.where(valid[:, None], s_sel, -jnp.inf).reshape(B, H, MOBA_Q_CHUNK, n_sel * MOBA_BLOCK)
        k_own = lax.dynamic_index_in_dim(k_blocks, own, axis=2, keepdims=False)
        v_own = lax.dynamic_index_in_dim(v_blocks, own, axis=2, keepdims=False)
        kpos = own * MOBA_BLOCK + jnp.arange(MOBA_BLOCK)
        s_own = jnp.einsum('bhqd,bhkd->bhqk', qc, k_own).astype(jnp.float32) * scale
        s_own = jnp.where(kpos[None, :] <= qpos[:, None], s_own, -jnp.inf)
        p = jax.nn.softmax(jnp.concatenate([s_own, s_sel], axis=-1), axis=-1).astype(v.dtype)
        p_own = p[..., :MOBA_BLOCK]
        p_sel = p[..., MOBA_BLOCK:].reshape(B, H, MOBA_Q_CHUNK, n_sel, MOBA_BLOCK)
        return (jnp.einsum('bhqk,bhkd->bhqd', p_own, v_own)
                + jnp.einsum('bhqjk,bhqjkd->bhqd', p_sel, v_sel))

    o = lax.map(chunk, (q_chunks, jnp.arange(nqc)))
    return o.transpose(1, 0, 3, 2, 4).reshape(B, S, H * dh)

def hierarchical_moe(h, w_rg, b_rg, w_re, b_re, w_g, w_u, w_d):
    B, S, D = h.shape
    T = B * S
    hf = h.reshape(T, D)
    g_logits = (hf @ w_rg + b_rg).astype(jnp.float32)
    g_sel = jnp.argmax(g_logits, axis=-1).astype(jnp.int32)
    p_group = jnp.take_along_axis(jax.nn.softmax(g_logits, axis=-1), g_sel[:, None], axis=1)
    e_logits = (jnp.einsum('td,gde->tge', hf, w_re) + b_re).astype(jnp.float32)
    e_in = jnp.take_along_axis(e_logits, g_sel[:, None, None], axis=1)[:, 0]
    top_vals, top_idx = lax.top_k(e_in, EXPERT_TOPK)
    weight = p_group * jax.nn.softmax(top_vals, axis=-1)
    expert_id = g_sel[:, None] * EXPERTS_PER_GROUP + top_idx.astype(jnp.int32)

    A = T * EXPERT_TOPK
    eid = expert_id.reshape(A)
    w_flat = weight.reshape(A)
    tok = jnp.repeat(jnp.arange(T, dtype=jnp.int32), EXPERT_TOPK)
    order = jnp.argsort(eid, stable=True)
    se = eid[order]
    counts = jnp.bincount(eid, length=N_EXPERTS).astype(jnp.int32)
    padded = (counts + EXPERT_BLOCK - 1) // EXPERT_BLOCK * EXPERT_BLOCK
    start = jnp.cumsum(counts) - counts
    pend = jnp.cumsum(padded)
    pstart = pend - padded
    dest = pstart[se] + jnp.arange(A, dtype=jnp.int32) - start[se]
    n_slots = (-(-A // EXPERT_BLOCK) + N_EXPERTS) * EXPERT_BLOCK
    slot_tok = jnp.zeros((n_slots,), jnp.int32).at[dest].set(tok[order])
    slot_w = jnp.zeros((n_slots,), h.dtype).at[dest].set(w_flat[order].astype(h.dtype))
    n_blocks = n_slots // EXPERT_BLOCK
    blk_e = jnp.minimum(jnp.searchsorted(pend, jnp.arange(n_blocks, dtype=jnp.int32) * EXPERT_BLOCK,
                                         side='right'), N_EXPERTS - 1)
    xs = hf[slot_tok].reshape(n_blocks, EXPERT_BLOCK, D)

    def expert_block(args):
        xb, e = args
        return (jax.nn.silu(xb @ w_g[e]) * (xb @ w_u[e])) @ w_d[e]

    ys = lax.map(expert_block, (xs, blk_e)).reshape(n_slots, D)
    out = jnp.zeros((T, D), h.dtype).at[slot_tok].add(ys * slot_w[:, None])
    return out.reshape(B, S, D)

def second_inputs(seed: int = 0) -> dict:
    key = jax.random.key(seed)
    ks = jax.random.split(key, 20)
    f32 = jnp.float32
    L = DEPTH

    def dense(k, shape, fan_in):
        return jax.random.normal(k, shape, f32) * fan_in ** -0.5

    def gain(k, shape):
        return 1.0 + 0.02 * jax.random.normal(k, shape, f32)

    return {
        'x': jax.random.normal(ks[0], (BATCH, SEQ, D_MODEL), f32),
        'attn_norm': gain(ks[1], (L, D_MODEL)),
        'w_in': dense(ks[2], (L, D_MODEL, IN_WIDTH_2), D_MODEL),
        'q_norm': gain(ks[3], (L, Q_LORA)),
        'w_uq': dense(ks[4], (L, Q_LORA, MLA_HEADS * (MLA_NOPE + MLA_ROPE)), Q_LORA),
        'kv_norm': gain(ks[5], (L, KV_LORA)),
        'w_ukv': dense(ks[6], (L, KV_LORA, MLA_HEADS * (MLA_NOPE + MLA_V)), KV_LORA),
        'w_o_mla': dense(ks[7], (L, MLA_HEADS * MLA_V, D_MODEL), MLA_HEADS * MLA_V),
        'w_o_moba': dense(ks[8], (L, MOBA_HEADS * MOBA_HD, D_MODEL), MOBA_HEADS * MOBA_HD),
        'w_out': dense(ks[9], (L, D_MODEL, D_MODEL), D_MODEL),
        'ffn_norm': gain(ks[10], (L, D_MODEL)),
        'w_router_group': dense(ks[11], (L, D_MODEL, N_GROUPS), D_MODEL),
        'b_router_group': 0.01 * jax.random.normal(ks[12], (L, N_GROUPS), f32),
        'w_router_expert': dense(ks[13], (L, N_GROUPS, D_MODEL, EXPERTS_PER_GROUP), D_MODEL),
        'b_router_expert': 0.01 * jax.random.normal(ks[14], (L, N_GROUPS, EXPERTS_PER_GROUP), f32),
        'w_exp_gate': dense(ks[15], (L, N_EXPERTS, D_MODEL, EXPERT_FF), D_MODEL),
        'w_exp_up': dense(ks[16], (L, N_EXPERTS, D_MODEL, EXPERT_FF), D_MODEL),
        'w_exp_down': dense(ks[17], (L, N_EXPERTS, EXPERT_FF, D_MODEL), EXPERT_FF),
        'final_norm': gain(ks[18], (D_MODEL,)),
    }

def second_block(x, attn_norm, w_in, q_norm, w_uq, kv_norm, w_ukv, w_o_mla, w_o_moba, w_out,
              ffn_norm, w_router_group, b_router_group, w_router_expert, b_router_expert,
              w_exp_gate, w_exp_up, w_exp_down, final_norm):
    B, S, _ = x.shape
    cos_mla, sin_mla = rope_tables(S, MLA_ROPE)
    cos_moba, sin_moba = rope_tables(S, MOBA_ROT)
    split_at = [int(i) for i in np.cumsum(IN_SPLITS)[:-1]]
    for l in range(DEPTH):
        h = rmsnorm(x, attn_norm[l])
        proj = h @ w_in[l]
        c_q, c_kv, k_r, q_b, k_b, v_b, gate_a, gate_b = jnp.split(proj, split_at, axis=-1)
        o_a = mla_attention(c_q, c_kv, k_r, q_norm[l], w_uq[l], kv_norm[l], w_ukv[l], cos_mla, sin_mla)
        o_b = moba_attention(q_b.reshape(B, S, MOBA_HEADS, MOBA_HD),
                             k_b.reshape(B, S, MOBA_HEADS, MOBA_HD),
                             v_b.reshape(B, S, MOBA_HEADS, MOBA_HD), cos_moba, sin_moba)
        mixed = (jax.nn.sigmoid(gate_a) * (o_a @ w_o_mla[l])
                 + jax.nn.sigmoid(gate_b) * (o_b @ w_o_moba[l]))
        x = x + mixed @ w_out[l]
        x = x + hierarchical_moe(rmsnorm(x, ffn_norm[l]), w_router_group[l], b_router_group[l],
                                 w_router_expert[l], b_router_expert[l],
                                 w_exp_gate[l], w_exp_up[l], w_exp_down[l])
    return rmsnorm(x, final_norm)


def setup_inputs(seed=0):
    out = dict(first_inputs(seed))
    for name, value in second_inputs(seed + 1).items():
        if name != "x":
            out[name + "_2"] = value
    return out


def reference(
    x, norm_gain, w_in, b_merge, kv_norm_gain, w_uk, w_uv, idx_ln_gain, idx_ln_bias,
    w_attn_proj, conv_w, conv_b, w_rg_a, b_rg_a, w_rg_x, b_rg_x, lru_lambda, w_rnn_proj, w_out,
    final_norm_gain, attn_norm_2, w_in_2, q_norm_2, w_uq_2, kv_norm_2, w_ukv_2, w_o_mla_2,
    w_o_moba_2, w_out_2, ffn_norm_2, w_router_group_2, b_router_group_2, w_router_expert_2,
    b_router_expert_2, w_exp_gate_2, w_exp_up_2, w_exp_down_2, final_norm_2,
):
    x = first_block(
        x, norm_gain, w_in, b_merge, kv_norm_gain, w_uk, w_uv, idx_ln_gain, idx_ln_bias,
        w_attn_proj, conv_w, conv_b, w_rg_a, b_rg_a, w_rg_x, b_rg_x, lru_lambda, w_rnn_proj,
        w_out, final_norm_gain,
    )
    return second_block(
        x, attn_norm_2, w_in_2, q_norm_2, w_uq_2, kv_norm_2, w_ukv_2, w_o_mla_2, w_o_moba_2,
        w_out_2, ffn_norm_2, w_router_group_2, b_router_group_2, w_router_expert_2,
        b_router_expert_2, w_exp_gate_2, w_exp_up_2, w_exp_down_2, final_norm_2,
    )


_drawn_inputs = setup_inputs


def setup_inputs(seed=0):
    import zlib

    import numpy as np

    out = dict(_drawn_inputs(seed))
    spreads = {}
    factors = {'b_merge': 8.0,
     'kv_norm_gain': 8.0,
     'idx_ln_bias': 3.736,
     'conv_b': 2.815,
     'b_rg_a': 30.679,
     'b_rg_x': 8.0,
     'attn_norm_2': 7.525,
     'q_norm_2': 8.0,
     'kv_norm_2': 6.637,
     'b_router_group_2': 64.0,
     'final_norm_2': 21.599,
     'ffn_norm_2': 8.0,
     'b_router_expert_2': 21.76}
    for name, (base, spread) in spreads.items():
        noise = np.random.default_rng([zlib.crc32(name.encode()), seed]).standard_normal(out[name].shape)
        drawn = base * np.exp(spread * noise) if base else spread * noise
        out[name] = jnp.asarray(drawn.astype(out[name].dtype))
    for name, factor in factors.items():
        out[name] = (out[name] * factor).astype(out[name].dtype)
    return out
```

```python
import numpy as np
import concourse.bass as bass
from concourse import mybir
from contextlib import ExitStack

F32 = mybir.dt.float32
I32 = mybir.dt.int32
U32 = mybir.dt.uint32
ACT = mybir.ActivationFunctionType
ALU = mybir.AluOpType
AX = mybir.AxisListType

P = 128
T = 256
NT = T // P
D = 1024
DC = D // P
EPS = 1e-6
BIG = 1e30
TAKEN = -3e38

H1, HD1, LAT = 16, 64, 128
IDXH, IDXD = 8, 64
TOPK = min(256, T // 4)
CONV = 4
LRU_C = 8.0
H2, HD2 = 8, 64
ROPE, MROT = 32, 16
QL, KL = 768, 256
QC, KC = QL // P, KL // P
MLA_SCALE = float((HD2 + ROPE) ** -0.5)
MOBA_SCALE = float(HD2 ** -0.5)
NG, EPG = 4, 8
NE = NG * EPG
FF = 256
SLOTS = 2 * T
WIN = 64
CAUSAL = P + T

UNIT = 1024
RING = 6

PLAN = [
    ("ckv_kidx", [2], "act"), ("qidx", [2, 4], "act"), ("xrnn", [2, 4, 6, 8], "act"),
    ("q", [2, 4, 6, 8], "act"), ("gattn", [2, 4, 6, 8], "dve"), ("grnn", [2, 4, 6, 8], "dve"),
    ("merge", [2, 4, 6, 8, 10, 12, 14, 16], "act"), ("rproj", [2, 4, 6, 8], "dve"),
    ("aproj", [2, 4, 6, 8], "dve"), ("out1", [2, 4, 6, 8], "dve"),
    ("cq", [2, 4, 6], "act"), ("ckv2", [2], "act"), ("qb", [2, 4], "act"), ("kb", [2, 4], "act"),
    ("vb", [4, 4], "act"), ("uq", [2, 4, 6, 8], "dve"), ("ukvk", [1, 1], "act"),
    ("ukvv", [1, 1], "act"), ("gates", [2, 4, 6, 8, 10, 12, 14, 16], "act"),
    ("omla", [1, 2, 3, 4], "dve"), ("omoba", [1, 2, 3, 4], "dve"), ("out2", [2, 4, 6, 8], "dve"),
]
FILL0, UNIT0, UNITS_AT, RELEASE = {}, {}, [], []
_u = 0
for _name, _ends, _eng in PLAN:
    FILL0[_name], UNIT0[_name] = len(UNITS_AT), _u
    for _e in _ends:
        UNITS_AT.append(_u + _e)
        RELEASE.append(_eng)
    _u += _ends[-1]
DENSE_UNITS = _u
DENSE_PANELS = DENSE_UNITS // 2
EXPERT_PANELS = 3
PAIR = 2 * EXPERT_PANELS
RELEASED = [RELEASE[:f + 1].count(RELEASE[f]) for f in range(len(RELEASE))]

NORMS = [(8, D), (1, LAT), (1, 1), (8, D), (8, D), (6, QL), (2, KL), (8, D), (8, D)]
N_X, N_CKV, N_KIDX, N_FIN1, N_ATT2, N_CQ, N_CKV2, N_FFN, N_OUT = range(9)
SQ0 = [sum((c + 1) // 2 for c, _ in NORMS[:k]) for k in range(10)]
NM0 = [sum(c for c, _ in NORMS[:k]) for k in range(10)]

VEC = {}
_c = 0
for _name, _n in [("norm_gain", 8), ("b_merge", 16), ("b_rg_a", 8), ("b_rg_x", 8), ("kv_norm_gain", 1),
                  ("idx_ln_gain", 1), ("idx_ln_bias", 1), ("conv_w", 32), ("conv_b", 8), ("lru_lambda", 8),
                  ("final_norm_gain", 8), ("attn_norm_2", 8), ("q_norm_2", 6), ("kv_norm_2", 2),
                  ("ffn_norm_2", 8), ("final_norm_2", 8)]:
    VEC[_name] = _c
    _c += _n
NVEC = _c
CST = {}
_c = 0
for _name, _n in [("ident", P), ("ones", P), ("mean64", P), ("swap", P), ("before", P), ("dist", CAUSAL),
                  ("causal", CAUSAL), ("cos_mla", T), ("sin_mla", T), ("cos_moba", T), ("sin_moba", T),
                  ("iota", SLOTS)]:
    CST[_name] = _c
    _c += _n
NCST = _c


def build(nc, x_t, vecs, consts, w_widx, w_rg, w_uk, w_uv, w_kr, w_router, b_router, w_dense, w_expert, out):
    ctx = ExitStack()
    with ctx:
        def sb(name, shape, dt=F32):
            return ctx.enter_context(nc.sbuf_tensor(name, shape, dt))

        def sem(name):
            return ctx.enter_context(nc.semaphore(name))

        ring = sb("ring", [P, RING, 2 * UNIT])
        vec = sb("vec", [P, NVEC])
        cst = sb("cst", [P, NCST])
        xT = sb("xT", [P, DC, T])
        hT = sb("hT", [P, DC, T])
        scr = sb("scr", [P, DC, T])
        widx_w = sb("widx_w", [P, DC, IDXH])
        wkr = sb("wkr", [P, DC, 2 * ROPE])
        wrt = sb("wrt", [P, DC, NG + NE])
        brt = sb("brt", [1, NG + NE])
        wuk = sb("wuk", [P, H1 // 2, LAT])
        wuv = sb("wuv", [P, H1, HD1])
        root = sb("root", [P, T])
        rinv = sb("rinv", [P, T])
        halfb = sb("halfb", [P, 32])
        sp = sb("sp", [P, 10, 8])
        S = sb("S", [P, 2, CAUSAL])
        E = sb("E", [P, 2, CAUSAL])
        PT = sb("PT", [P, 2, CAUSAL])
        stat = sb("stat", [P, 2, 3, 2])
        th = sb("th", [P, 2, 2 * T])
        big = sb("big", [P, 19 * 1024])
        small = sb("small", [P, 5 * 1024])

        def at(region, off, *dims):
            n = 1
            for d in dims:
                n *= d
            v = region[:, off:off + n]
            if len(dims) == 2:
                v = v.rearrange("p (a b) -> p a b", a=dims[0])
            if len(dims) == 3:
                v = v.rearrange("p (a b c) -> p a b c", a=dims[0], b=dims[1])
            return v

        K = 1024
        qT = at(big, 0, 8, T)
        oT = qT
        xr = at(big, 2 * K, 8, T + CONV)
        la = at(big, 2 * K, 8, T)
        u = at(big, 5 * K - 512, 8, T)
        ra = at(big, 7 * K - 512, 8, T)
        ib = at(big, 9 * K - 512, 8, T)
        sg = at(big, 11 * K - 512, 8, T)
        sr = at(big, 13 * K - 512, 8, T)
        tm = at(big, 15 * K - 512, 16, T)
        wrg = at(big, 15 * K - 512, 2, 8, P)
        qi = at(small, 0, 4, T)
        zc = at(small, K, 2, T)
        kiT = at(small, K + 512, T)
        cT = at(small, K + 768, T)
        ctok = at(small, 2 * K, 2, LAT)
        widx = at(small, 2 * K + 256, 2, IDXH)
        qlat = at(small, 2 * K + 512, 2, T)
        olat = at(small, 3 * K, 2, T)
        score = at(small, 3 * K + 512, CAUSAL)
        Dm = at(small, 4 * K, CAUSAL)
        top8 = at(small, 4 * K + 512, 2, 8)
        cqT = at(big, 0, QC, T)
        ckT = at(big, 6 * 256, KC, T)
        qb = at(big, 2 * K, 4, T)
        kb = at(big, 3 * K, 4, T)
        vb = at(big, 4 * K, 2, 512)
        qh = at(big, 5 * K, H2, T)
        kh = at(big, 7 * K, H2, T)
        vh = at(big, 9 * K, 2, 512)
        tg2 = at(big, 10 * K, 16, T)
        oA = at(big, 14 * K, 4, T)
        oB = at(big, 15 * K, 4, T)
        krT = at(big, 16 * K, T)
        rot = at(big, 16 * K + 256, 2, 512)
        xs = at(big, 0, DC, SLOTS + T)
        ys = at(big, 6 * K, DC, SLOTS + T)
        ysm = at(big, 12 * K, SLOTS // P, D)
        SWT = at(big, 16 * K, SLOTS // P, T)
        sel = at(big, 17 * K, 2, SLOTS)
        sw = at(big, 18 * K, 2, SLOTS)
        htok = at(big, 12 * K, 2, D)
        actT = at(small, 0, 2, 2 * T)
        rt = at(small, K, 2048)

        def V(name, i=0, n=1):
            return vec[:, VEC[name] + i:VEC[name] + i + n]

        def C(name, n, i=0):
            return cst[:, CST[name] + i:CST[name] + i + n]

        ident, ones = C("ident", P), C("ones", P)

        D0, D1, L0, L1, TB, QB, OB, UB = [ctx.enter_context(nc.psum_tensor(n, [P, 512], F32))
                                          for n in ("D0", "D1", "L0", "L1", "TB", "QB", "OB", "UB")]
        DB, LB = [D0, D1], [L0, L1]

        arrived = [sem(f"panel_arrived_{i}") for i in range(RING)]
        s_in = {n: sem(f"in_{n}") for n in ("x", "vec", "cst", "widx", "wrg", "wuk", "wuv", "wkr", "wrt", "brt")}
        unit_done, moe_used = sem("unit_done"), sem("moe_used")
        rel = {"act": sem("bank_released_by_act"), "dve": sem("bank_released_by_dve")}
        sq, ssq, rooted, rinvd, normed = [sem(n) for n in ("squared", "sumsq_ready", "rooted", "rinv_ready", "normed")]
        tanhd = sem("tanh_ready")
        vstep, astep = sem("vector_step"), sem("scalar_step")
        mean_ready, centered, kidx_ready, widx_mm, widx_ready = [sem(n) for n in (
            "mean_ready", "centered", "kidx_ready", "widx_matmul", "widx_ready")]
        ctok_mm, ctok_ready = sem("ctok_transposed"), sem("ctok_ready")
        idx_mm, idx_relu, idx_acc = sem("idx_scores"), sem("idx_relu"), sem("idx_accumulated")
        mask_ready = sem("mask_ready")
        padded, conv_done, gate_mm, gates, decay, sq_a, m_ready, rt_m, h_ready = [sem(n) for n in (
            "conv_padded", "conv_done", "rg_gates_matmul", "rg_gates_ready", "decay_ready", "decay_squared",
            "m_ready", "m_rooted", "gated_h_ready")]
        sp_step, sp_act, sp_ready = sem("softplus_step"), sem("softplus_act"), sem("softplus_ready")
        qlat_mm, qlat_ready = sem("qlat_matmul"), sem("qlat_ready")
        logits, biased, maxed, expd, probs = [sem(n) for n in ("logits", "biased", "maxed", "expd", "probs")]
        pt_mm, pt_ready, pv_mm, olat_ready, o_mm, o_ready = [sem(n) for n in (
            "probs_transposed", "pt_ready", "pv_matmul", "olat_ready", "o_matmul", "o_ready")]
        mixed = sem("mixed_ready")
        kr_mm, kr_ready = sem("krope_matmul"), sem("krope_ready")
        swap_mm, rotated = sem("swap_matmul"), sem("moba_rotated")
        rlog_mm, rlog, gate_neg, expg, topd, expt, onehot, cnt_mm, selected, offs = [sem(n) for n in (
            "router_matmul", "router_logits", "group_max", "group_exp", "top2", "top2_exp", "onehot_ready",
            "rank_matmul", "selection_ready", "offsets_ready")]
        htok_mm, htok_ready, swt_mm, swt_ready, xs_mm, xs_ready, xs_ready2 = [sem(n) for n in (
            "htok_transposed", "htok_ready", "swt_transposed", "swt_ready", "gathered", "xs_by_act", "xs_by_dve")]
        padz = sem("pads_zero")
        gate_t, silu_e, act_ready, ys_done = sem("expert_gate_tanh"), sem("expert_silu"), sem("expert_act_ready"), sem("expert_out_kept")
        ysm_mm, ysm_ready, ysm_ready2, comb_mm, comb = [sem(n) for n in (
            "ys_transposed", "ysm_by_act", "ysm_by_dve", "combined_matmul", "combined")]
        stored = sem("stored")

        def freed(eng, f):
            eng.wait_ge(rel[RELEASE[f]], RELEASED[f])

        def kept(eng, stage, i):
            freed(eng, FILL0[stage] + i)

        def filled(eng, stage, i):
            f = FILL0[stage] + i
            eng.wait_ge(unit_done, UNITS_AT[f])
            return DB[f % 2]

        def kept_all(eng):
            eng.wait_ge(ys_done, 2 + NE)

        def x1_src(eng, stage):
            def src(c, w):
                kept(eng, stage, c // 2)
                return xT[:, c:c + w, :]
            return src

        def x3_src(eng):
            def src(c, w):
                eng.wait_ge(comb, c // 2 + 1)
                return xT[:, c:c + w, :]
            return src

        block = ctx.enter_context(nc.Block())

        @block.sync
        def _(sp_):
            def panel(slot, src):
                return sp_.dma_start(ring[:, slot, :], src).then_inc(arrived[slot], 16)

            sp_.dma_start(xT[:], x_t.rearrange("p (c t) -> p c t", c=DC)).then_inc(s_in["x"], 16)
            sp_.dma_start(vec[:], vecs).then_inc(s_in["vec"], 16)
            sp_.dma_start(cst[:, 0:NCST], consts).then_inc(s_in["cst"], 16)
            panel(0, w_dense[0])
            sp_.dma_start(widx_w[:], w_widx.rearrange("p (c t) -> p c t", c=DC)).then_inc(s_in["widx"], 16)
            for p in range(1, RING):
                panel(p, w_dense[p])
            sp_.dma_start(wrg, w_rg.rearrange("p (a c t) -> p a c t", a=2, c=8)).then_inc(s_in["wrg"], 16)
            sp_.dma_start(wuk[:], w_uk.rearrange("p (c t) -> p c t", c=8)).then_inc(s_in["wuk"], 16)
            sp_.dma_start(wuv[:], w_uv.rearrange("p (c t) -> p c t", c=16)).then_inc(s_in["wuv"], 16)
            sp_.dma_start(wkr[:], w_kr.rearrange("p (c t) -> p c t", c=DC)).then_inc(s_in["wkr"], 16)
            sp_.dma_start(wrt[:], w_router.rearrange("p (c t) -> p c t", c=DC)).then_inc(s_in["wrt"], 16)
            sp_.dma_start(brt[:], b_router).then_inc(s_in["brt"], 16)
            laps = DENSE_PANELS // RING
            with sp_.Fori(1, laps) as lap:
                for slot in range(RING):
                    sp_.wait_ge(unit_done, lap * (2 * RING) + (2 * slot + 2 - 2 * RING))
                    sp_.dma_start(ring[:, slot, :], w_dense[bass.ds(lap * RING + slot, 1)].rearrange(
                        "a p n -> p (a n)")).then_inc(arrived[slot], 16)
            for p in range(laps * RING, DENSE_PANELS):
                sp_.wait_ge(unit_done, 2 * (p - RING) + 2)
                panel(p % RING, w_dense[p])
            for p in range(PAIR):
                sp_.wait_ge(unit_done, 2 * (DENSE_PANELS + p - RING) + 2)
                panel((DENSE_PANELS + p) % RING, w_expert[p])
            with sp_.Fori(1, NE // 2) as lap:
                for j in range(PAIR):
                    sp_.wait_ge(moe_used, lap * PAIR + (j + 1 - PAIR))
                    sp_.dma_start(ring[:, (DENSE_PANELS + j) % RING, :],
                                  w_expert[bass.ds(lap * PAIR + j, 1)].rearrange("a p n -> p (a n)")
                                  ).then_inc(arrived[(DENSE_PANELS + j) % RING], 16)
            for c in range(0, DC, 2):
                sp_.wait_ge(normed, NM0[N_OUT] + c + 2)
                sp_.dma_start(out[:, c * T:(c + 2) * T].rearrange("p (c t) -> p c t", c=2),
                              hT[:, c:c + 2, :]).then_inc(stored, 16)
            sp_.wait_ge(stored, 16 * (DC // 2))

        @block.tensor
        def _(pe):
            mm = nc.tensor.matmul
            seen = [0]

            def unit(n):
                p = n // 2
                if p >= seen[0]:
                    pe.wait_ge(arrived[p % RING], 16 * (p // RING + 1))
                    seen[0] = p + 1
                return ring[:, p % RING, (n % 2) * UNIT:(n % 2 + 1) * UNIT]

            def open_bank(stage, i):
                f = FILL0[stage] + i
                if f >= 2:
                    freed(pe, f - 2)
                return DB[f % 2]

            def chunk(stage, c, src, kc=DC, ready=None):
                bank = open_bank(stage, c // 2) if c % 2 == 0 else DB[(FILL0[stage] + c // 2) % 2]
                w = unit(UNIT0[stage] + c)
                for k in range(kc):
                    if ready is not None:
                        pe.wait_ge(normed, ready + k + 1)
                    last = mm(bank[:, (c % 2) * T:(c % 2 + 1) * T], w[:, k * P:(k + 1) * P], src[:, k, :],
                              start=(k == 0), stop=(k == kc - 1))
                last.then_inc(unit_done, 1)

            def sumsq(n, lhs=None):
                nch = NORMS[n][0]
                if n:
                    pe.wait_ge(rooted, n)
                for c in range(nch):
                    pe.wait_ge(sq, SQ0[n] + c // 2 + 1)
                    last = mm(UB[:, 0:T], ones if lhs is None else lhs, scr[:, c, :],
                              start=(c == 0), stop=(c == nch - 1))
                last.then_inc(ssq, 1)

            pe.wait_ge(s_in["cst"], 16)
            sumsq(N_X)
            for c in range(2):
                chunk("ckv_kidx", c, hT, ready=NM0[N_X] if c == 0 else None)
            chunk("qidx", 0, hT)
            kept(pe, "ckv_kidx", 0)
            mm(OB[:, 0:T], C("mean64", P), zc[:, 1, :], start=True, stop=True).then_inc(mean_ready, 1)
            chunk("qidx", 1, hT)
            sumsq(N_CKV)
            pe.wait_ge(s_in["widx"], 16)
            for tt in range(NT):
                for k in range(DC):
                    last = mm(QB[:, tt * IDXH:(tt + 1) * IDXH], hT[:, k, tt * P:(tt + 1) * P], widx_w[:, k, :],
                              start=(k == 0), stop=(k == DC - 1))
            last.then_inc(widx_mm, 1)
            chunk("qidx", 2, hT)
            sumsq(N_KIDX, C("mean64", P))
            chunk("qidx", 3, hT)
            chunk("xrnn", 0, hT)
            pe.wait_ge(kidx_ready, 1)
            kept(pe, "qidx", 1)
            for j in range(IDXH):
                if j >= 2:
                    pe.wait_ge(idx_relu, j - 1)
                lo = IDXD * (j % 2)
                mm(LB[j % 2][:, 0:P], qi[lo:lo + IDXD, j // 2, 0:P], kiT[lo:lo + IDXD, 0:P], start=True, stop=True)
                mm(LB[j % 2][:, P:CAUSAL], qi[lo:lo + IDXD, j // 2, P:T], kiT[lo:lo + IDXD, 0:T],
                   start=True, stop=True).then_inc(idx_mm, 1)
            pe.wait_ge(normed, NM0[N_CKV] + 1)
            for s in range(2):
                last = nc.tensor.transpose(OB[:, 256 + s * P:256 + (s + 1) * P], cT[:, s * P:(s + 1) * P], ident)
            last.then_inc(ctok_mm, 1)
            for c in range(1, 8):
                chunk("xrnn", c, hT)
            for c in range(8):
                chunk("q", c, hT)
            pe.wait_ge(s_in["wrg"], 16)
            for c in range(8):
                pe.wait_ge(conv_done, c + 1)
                pe.wait_ge(idx_relu, IDXH)
                if c >= 2:
                    pe.wait_ge(gates, c - 1)
                for g in range(2):
                    last = mm(LB[c % 2][:, g * T:(g + 1) * T], wrg[:, g, c, :], u[:, c, :], start=True, stop=True)
                last.then_inc(gate_mm, 1)

            def scores(a, q_of, k_of):
                pe.wait_ge(biased, a - 1) if a >= 2 else pe.wait_ge(gates, 8)
                for tt in range(NT):
                    c0, n = (0, P) if tt == 0 else (P, T)
                    last = mm(LB[a % 2][:, c0:c0 + n], q_of(tt), k_of(n), start=True, stop=True)
                last.then_inc(logits, 1)

            def transposes(a):
                pe.wait_ge(probs, a + 1)
                if a >= 1:
                    pe.wait_ge(pt_ready, a)
                for b in range(3):
                    last = nc.tensor.transpose(TB[:, b * P:(b + 1) * P], E[:, a % 2, b * P:(b + 1) * P], ident)
                last.then_inc(pt_mm, 1)

            def pv(a, dst, v_of):
                pe.wait_ge(pt_ready, a + 1)
                mm(dst[:, 0:T], v_of(0), PT[:, a % 2, 0:T], start=True, stop=False, skip_group_check=True)
                return mm(dst[:, P:T], v_of(1), PT[:, a % 2, T:CAUSAL], start=False, stop=True, skip_group_check=True)

            todo = [("gattn", c) for c in range(8)] + [("grnn", c) for c in range(8)] + [("merge", c) for c in range(16)]

            def fill():
                if todo:
                    chunk(*todo.pop(0), hT)

            pe.wait_ge(s_in["wuk"], 16)
            pe.wait_ge(s_in["wuv"], 16)
            kept(pe, "q", 3)
            pe.wait_ge(ctok_ready, 1)
            pe.wait_ge(widx_ready, 1)
            for i in range(H1 + 2):
                if i < H1:
                    lo = HD1 * (i % 2)
                    if i >= 1:
                        pe.wait_ge(qlat_ready, i)
                    mm(QB[:, 0:T], wuk[lo:lo + HD1, i // 2, :], qT[lo:lo + HD1, i // 2, :],
                       start=True, stop=True).then_inc(qlat_mm, 1)
                fill()
                if i < H1:
                    pe.wait_ge(qlat_ready, i + 1)
                    scores(i, lambda tt: qlat[:, i % 2, tt * P:(tt + 1) * P], lambda n: cT[:, 0:n])
                if 1 <= i <= H1:
                    transposes(i - 1)
                fill()
                if 1 <= i <= H1:
                    if i >= 2:
                        pe.wait_ge(olat_ready, i - 1)
                    pv(i - 1, OB, lambda s: ctok[:, s, :]).then_inc(pv_mm, 1)
                if i >= 2:
                    a = i - 2
                    pe.wait_ge(olat_ready, a + 1)
                    if a % 2 == 0 and a >= 2:
                        pe.wait_ge(o_ready, a // 2)
                    lo = HD1 * (a % 2)
                    mm(UB[lo:lo + HD1, 0:T], wuv[:, a, :], olat[:, a % 2, :], start=True, stop=True).then_inc(o_mm, 1)
            while todo:
                fill()
            pe.wait_ge(h_ready, 4)
            for c in range(8):
                chunk("rproj", c, u)
            pe.wait_ge(o_ready, 8)
            for c in range(8):
                chunk("aproj", c, oT)
            pe.wait_ge(mixed, 4)
            for c in range(8):
                chunk("out1", c, tm)
            sumsq(N_FIN1)
            sumsq(N_ATT2)

            for c in range(6):
                chunk("cq", c, hT, ready=NM0[N_ATT2] if c == 0 else None)
            for c in range(2):
                chunk("ckv2", c, hT)
            for c in range(4):
                chunk("qb", c, hT)
            for c in range(4):
                chunk("kb", c, hT)
            for i in range(2):
                bank = open_bank("vb", i)
            vb_banks = [DB[(FILL0["vb"] + i) % 2] for i in range(2)]
            for k in range(DC):
                w = unit(UNIT0["vb"] + k // 2)[:, (k % 2) * 512:(k % 2 + 1) * 512]
                for tt in range(NT):
                    last = mm(vb_banks[tt][:, 0:512], hT[:, k, tt * P:(tt + 1) * P], w, start=(k == 0), stop=(k == DC - 1))
                if k % 2:
                    last.then_inc(unit_done, 1)
            sumsq(N_CQ)
            pe.wait_ge(s_in["wkr"], 16)
            for k in range(DC):
                last = mm(QB[0:2 * ROPE, 0:T], wkr[:, k, :], hT[:, k, :], start=(k == 0), stop=(k == DC - 1))
            last.then_inc(kr_mm, 1)
            sumsq(N_CKV2)
            kept(pe, "kb", 1)
            for i in range(4):
                if i >= 2:
                    pe.wait_ge(rotated, i - 1)
                src = (qb if i < 2 else kb)[:, (i % 2) * 2:(i % 2) * 2 + 2, :]
                mm(LB[i % 2][:, :], C("swap", P), src, start=True, stop=True).then_inc(swap_mm, 1)
            pe.wait_ge(normed, NM0[N_CQ] + 6)
            for h in range(H2):
                chunk("uq", h, cqT, kc=QC)
            pe.wait_ge(normed, NM0[N_CKV2] + 2)
            w = unit(UNIT0["ukvk"])
            for m in range(4):
                bank = open_bank("ukvk", m // 2) if m % 2 == 0 else DB[(FILL0["ukvk"] + m // 2) % 2]
                for k in range(KC):
                    last = mm(bank[:, (m % 2) * T:(m % 2 + 1) * T], w[:, (m * KC + k) * P:(m * KC + k + 1) * P],
                              ckT[:, k, :], start=(k == 0), stop=(k == KC - 1))
            last.then_inc(unit_done, 1)
            w = unit(UNIT0["ukvv"])
            for tt in range(NT):
                bank = open_bank("ukvv", tt)
                for k in range(KC):
                    last = mm(bank[:, 0:512], ckT[:, k, tt * P:(tt + 1) * P], w[:, k * 512:(k + 1) * 512],
                              start=(k == 0), stop=(k == KC - 1))
            last.then_inc(unit_done, 1)

            todo = [("gates", c) for c in range(16)]
            pe.wait_ge(rotated, 4)
            kept(pe, "vb", 1)
            for i in range(2 * H2 + 1):
                a = H1 + i
                if i < H2:
                    lo = HD2 * (i % 2)
                    scores(a, lambda tt: qb[lo:lo + HD2, i // 2, tt * P:(tt + 1) * P],
                           lambda n: kb[lo:lo + HD2, i // 2, 0:n])
                elif i < 2 * H2:
                    j = i - H2
                    if j == 0:
                        kept(pe, "uq", 3)
                        kept(pe, "ukvk", 1)
                        kept(pe, "ukvv", 1)
                        pe.wait_ge(kr_ready, 1)
                    scores(a, lambda tt: qh[0:HD2 + ROPE, j, tt * P:(tt + 1) * P], lambda n: kh[0:HD2 + ROPE, j, 0:n])
                if i >= 1:
                    transposes(a - 1)
                if todo:
                    chunk(*todo.pop(0), hT)
                if i >= 1:
                    j, v = ((i - 1) % H2), (vb if i - 1 < H2 else vh)
                    if (i - 1) % 2 == 0:
                        pe.wait_ge(o_ready, 8 + (i - 1) // 2)
                        pe.wait_ge(rooted, N_CKV2 + 1)
                    lo = HD2 * (j % 2)
                    pv(a - 1, UB[lo:lo + HD2], lambda s: v[:, s, j * HD2:(j + 1) * HD2]).then_inc(o_mm, 1)
            pe.wait_ge(o_ready, 16)

            def half_chunks(stage, src):
                for i in range(4):
                    bank, w = open_bank(stage, i), unit(UNIT0[stage] + i)
                    for m in range(2):
                        for k in range(4):
                            last = mm(bank[:, m * T:(m + 1) * T], w[:, (m * 4 + k) * P:(m * 4 + k + 1) * P],
                                      src[:, k, :], start=(k == 0), stop=(k == 3))
                    last.then_inc(unit_done, 1)

            half_chunks("omla", oA)
            half_chunks("omoba", oB)
            pe.wait_ge(mixed, 8)
            for c in range(8):
                chunk("out2", c, tg2[:, 8:16, :])
            sumsq(N_FFN)

            pe.wait_ge(s_in["wrt"], 16)
            pe.wait_ge(s_in["brt"], 16)
            pe.wait_ge(normed, NM0[N_FFN] + 8)
            for tt in range(NT):
                for k in range(DC):
                    mm(QB[:, tt * 64:tt * 64 + NG + NE], hT[:, k, tt * P:(tt + 1) * P], wrt[:, k, :],
                       start=(k == 0), stop=False)
                last = mm(QB[:, tt * 64:tt * 64 + NG + NE], ones[0:1, :], brt[0:1, :], start=False, stop=True)
            last.then_inc(rlog_mm, 1)
            for n in range(4):
                tt, half = n // 2, n % 2
                if n >= 2:
                    pe.wait_ge(htok_ready, n - 1)
                for c in range(4):
                    last = nc.tensor.transpose(LB[n % 2][:, c * P:(c + 1) * P],
                                               hT[:, half * 4 + c, tt * P:(tt + 1) * P], ident)
                last.then_inc(htok_mm, 1)
            pe.wait_ge(onehot, 2)
            A = rt[:, 0:64].rearrange("p (a b) -> p a b", a=2)
            before = C("before", P)
            mm(OB[:, 0:NE], before, A[:, 0, :], start=True, stop=True)
            mm(OB[:, NE:2 * NE], ones, A[:, 0, :], start=True, stop=False)
            mm(OB[:, NE:2 * NE], before, A[:, 1, :], start=False, stop=True)
            mm(OB[:, 2 * NE:3 * NE], ones, A[:, 0, :], start=True, stop=False)
            mm(OB[:, 2 * NE:3 * NE], ones, A[:, 1, :], start=False, stop=True).then_inc(cnt_mm, 1)
            pe.wait_ge(selected, 2)
            pe.wait_ge(htok_ready, 4)
            for c in range(DC):
                if c >= 2:
                    pe.wait_ge((xs_ready, xs_ready2)[c % 2], c // 2)
                elif c == 0:
                    kept(pe, "out2", 3)
                for tt in range(NT):
                    last = mm(DB[c % 2][:, :], htok[:, tt, c * P:(c + 1) * P], sel[:, tt, :],
                              start=(tt == 0), stop=(tt == NT - 1))
                last.then_inc(xs_mm, 1)
            for s2 in range(2):
                for b in range(4):
                    s, tt = s2 * 2 + b // 2, b % 2
                    last = nc.tensor.transpose(LB[s2][:, b * P:(b + 1) * P], sw[:, tt, s * P:(s + 1) * P], ident)
                last.then_inc(swt_mm, 1)

            pe.wait_ge(offs, 1)
            pe.wait_ge(swt_ready, 2)
            pe.wait_ge(padz, 1)
            pe.wait_ge(xs_ready, 4)
            pe.wait_ge(xs_ready2, 4)
            offi, flag = rt[0:1, 512:544].bitcast(I32), rt[0:1, 544:545].bitcast(I32)

            def experts(n, gu_banks, y_banks):
                with pe.Fori(0, NE // 2) as it:
                    for b in range(2):
                        off = pe.value_load(offi[0:1, bass.ds(it * 2 + b, 1)], min_val=0, max_val=SLOTS)
                        gu, y = gu_banks[b], y_banks[b]
                        pe.wait_ge(act_ready, it * 2 + (b + 1))
                        for m in range(4):
                            pn = EXPERT_PANELS * b + m // 2
                            slot = (DENSE_PANELS + pn) % RING
                            if m % 2 == 0:
                                pe.wait_ge(arrived[slot], it * 16 + 16 * ((DENSE_PANELS + pn) // RING + 1))
                            w = ring[:, slot, (m % 2) * UNIT:(m % 2 + 1) * UNIT]
                            for k in range(DC):
                                last = mm(gu(m), w[:, k * P:(k + 1) * P], xs[:, k, bass.ds(off, n)],
                                          start=(k == 0), stop=(k == DC - 1))
                            if m % 2:
                                last.then_inc(moe_used, 1)
                        pn = EXPERT_PANELS * b + 2
                        slot = (DENSE_PANELS + pn) % RING
                        pe.wait_ge(arrived[slot], it * 16 + 16 * ((DENSE_PANELS + pn) // RING + 1))
                        pe.wait_ge(ys_done, it * 2 + (b + 1))
                        pe.wait_ge(act_ready, it * 2 + (b + 3))
                        for c in range(DC):
                            for k in range(2):
                                last = mm(y(c), ring[:, slot, k * UNIT + c * P:k * UNIT + (c + 1) * P],
                                          actT[:, b, k * n:(k + 1) * n], start=(k == 0), stop=(k == 1))
                        last.then_inc(moe_used, 1)

            def fast(f):
                gu = [lambda m, b=b: (DB, LB)[m // 2][b][:, (m % 2) * WIN:(m % 2 + 1) * WIN] for b in range(2)]
                y = [lambda c, bank=bank: bank[:, c * WIN:(c + 1) * WIN] for bank in (QB, OB)]
                f(WIN, gu, y)

            def slow(f):
                gu = [lambda m: LB[m // 2][:, (m % 2) * T:(m % 2 + 1) * T]] * 2
                y = [lambda c: (QB, OB, TB, UB)[c // 2][:, (c % 2) * T:(c % 2 + 1) * T]] * 2
                f(T, gu, y)

            crowded = pe.value_load(flag, min_val=0, max_val=1)
            with pe.If(crowded):
                slow(experts)
            with pe.Else():
                fast(experts)

            kept_all(pe)
            for n in range(8):
                s, half = n // 2, n % 2
                if n >= 2:
                    pe.wait_ge((ysm_ready, ysm_ready2)[n % 2], n // 2)
                for c in range(4):
                    last = nc.tensor.transpose(LB[n % 2][:, c * P:(c + 1) * P],
                                               ys[:, half * 4 + c, s * P:(s + 1) * P], ident)
                last.then_inc(ysm_mm, 1)
            pe.wait_ge(ysm_ready, 4)
            pe.wait_ge(ysm_ready2, 4)
            for c in range(DC):
                if c % 2 == 0 and c >= 4:
                    pe.wait_ge(comb, c // 2 - 1)
                for s in range(SLOTS // P):
                    last = mm(DB[(c // 2) % 2][:, (c % 2) * T:(c % 2 + 1) * T], ysm[:, s, c * P:(c + 1) * P],
                              SWT[:, s, :], start=(s == 0), stop=(s == SLOTS // P - 1))
                if c % 2:
                    last.then_inc(comb_mm, 1)
            sumsq(N_OUT)

        @block.scalar
        def _(act):
            A_ = nc.scalar.activation

            def squares(n, src):
                nch = NORMS[n][0]
                if n:
                    act.wait_ge(ssq, n)
                for c in range(0, nch, 2):
                    w = min(2, nch - c)
                    A_(scr[:, c:c + w, :], src(c, w), ACT.Square).then_inc(sq, 1)

            def rootmean(n):
                act.wait_ge(ssq, n + 1)
                if n:
                    act.wait_ge(rinvd, n)
                act.wait_ge(vstep, 1)
                A_(root[:], UB[:, 0:T], ACT.Sqrt, bias=sp[:, 9, 0:1], scale=1.0 / NORMS[n][1]).then_inc(rooted, 1)

            act.wait_ge(s_in["x"], 16)
            squares(N_X, lambda c, w: xT[:, c:c + w, :])
            rootmean(N_X)
            act.wait_ge(sp_step, 2)
            A_(sp[:, 2, :], sp[:, 1, :], ACT.Exp, scale=-1.0).then_inc(sp_act, 1)
            act.wait_ge(sp_step, 3)
            A_(sp[:, 4, :], sp[:, 3, :], ACT.Ln).then_inc(sp_act, 1)
            bank = filled(act, "ckv_kidx", 0)
            A_(zc, bank[:, :].rearrange("p (a b) -> p a b", a=2), ACT.Copy).then_inc(rel["act"], 1)
            act.wait_ge(rel["act"], 1)
            squares(N_CKV, lambda c, w: zc[:, 0:1, :])
            rootmean(N_CKV)
            act.wait_ge(centered, 1)
            squares(N_KIDX, lambda c, w: zc[:, 1:2, :])
            act.wait_ge(widx_mm, 1)
            A_(widx, QB[:, 0:2 * IDXH].rearrange("p (a b) -> p a b", a=2), ACT.Copy,
               scale=float(IDXH ** -0.5)).then_inc(widx_ready, 1)
            rootmean(N_KIDX)
            for i in range(2):
                bank = filled(act, "qidx", i)
                A_(qi[:, 2 * i:2 * i + 2, :], bank[:, :].rearrange("p (a b) -> p a b", a=2), ACT.Copy,
                   scale=float(IDXD ** -0.5)).then_inc(rel["act"], 1)

            def conv_in(i):
                bank = filled(act, "xrnn", i)
                A_(xr[:, 2 * i:2 * i + 2, CONV:CONV + T], bank[:, :].rearrange("p (a b) -> p a b", a=2),
                   ACT.Copy).then_inc(rel["act"], 1)

            for j in range(IDXH):
                act.wait_ge(idx_mm, j + 1)
                if j >= 2:
                    act.wait_ge(idx_acc, j - 1)
                A_(S[:, j % 2, :], LB[j % 2][:, 0:CAUSAL], ACT.Relu).then_inc(idx_relu, 1)
            conv_in(0)
            act.wait_ge(ctok_mm, 1)
            A_(ctok, OB[:, 256:512].rearrange("p (a b) -> p a b", a=2), ACT.Copy).then_inc(ctok_ready, 1)
            for i in range(1, 4):
                conv_in(i)
            for i in range(4):
                bank = filled(act, "q", i)
                A_(qT[:, 2 * i:2 * i + 2, :], bank[:, :].rearrange("p (a b) -> p a b", a=2), ACT.Copy,
                   scale=float(HD1 ** -0.5)).then_inc(rel["act"], 1)
            for c in range(8):
                act.wait_ge(gate_mm, c + 1)
                A_(ra[:, c, :], LB[c % 2][:, 0:T], ACT.Tanh, bias=halfb[:, 16 + c:17 + c], scale=0.5)
                A_(ib[:, c, :], LB[c % 2][:, T:2 * T], ACT.Tanh, bias=halfb[:, 24 + c:25 + c],
                   scale=0.5).then_inc(gates, 1)
            act.wait_ge(gates, 8)
            act.wait_ge(sp_ready, 1)
            act.wait_ge(conv_done, 8)
            for c in range(8):
                A_(la[:, c, :], ra[:, c, :], ACT.Exp, bias=sp[:, 8, c:c + 1], scale=sp[:, 8, c:c + 1]).then_inc(decay, 1)
                act.wait_ge(decay, 2 * c + 1)
                A_(ra[:, c, :], ra[:, c, :], ACT.Tanh, bias=sp[:, 7, c:c + 1], scale=sp[:, 7, c:c + 1]).then_inc(decay, 1)
            act.wait_ge(ssq, 3)
            for i in range(4):
                A_(scr[:, 2 * i:2 * i + 2, :], la[:, 2 * i:2 * i + 2, :], ACT.Square).then_inc(sq_a, 1)
            def exps(a):
                act.wait_ge(maxed, a + 1)
                if a >= 2:
                    act.wait_ge(pt_mm, a - 1)
                for tt in range(NT):
                    c0, n = (0, P) if tt == 0 else (P, T)
                    last = A_(E[:, a % 2, c0:c0 + n], S[:, a % 2, c0:c0 + n], ACT.Exp,
                              bias=stat[:, a % 2, 0, tt:tt + 1], accum_out=stat[:, a % 2, 1, tt:tt + 1])
                last.then_inc(expd, 1)

            def ptcopy(a):
                act.wait_ge(pt_mm, a + 1)
                if a >= 2 and a <= H1:
                    act.wait_ge(pv_mm, a - 1)
                elif a > H1:
                    act.wait_ge(o_mm, a - 1)
                A_(PT[:, a % 2, :], TB[:, 0:CAUSAL], ACT.Copy).then_inc(pt_ready, 1)

            def half_tanh(f, stage, i):
                bank = filled(act, stage, i)
                if f >= 2:
                    act.wait_ge(rel["dve"], f - 1)
                A_(th[:, f % 2, :], bank[:, :], ACT.Tanh, scale=0.5).then_inc(tanhd, 1)

            def merge_gate(i):
                bank = filled(act, "merge", i)
                if i == 0:
                    act.wait_ge(gate_mm, 8)
                for m in range(2):
                    c = 2 * i + m
                    last = A_(tm[:, c, :], bank[:, m * T:(m + 1) * T], ACT.Tanh, bias=halfb[:, c:c + 1], scale=0.5)
                last.then_inc(rel["act"], 1)

            for i in range(H1 + 2):
                if i < H1:
                    act.wait_ge(qlat_mm, i + 1)
                    if i >= 2:
                        act.wait_ge(logits, i - 1)
                    A_(qlat[:, i % 2, :], QB[:, 0:T], ACT.Copy).then_inc(qlat_ready, 1)
                if 1 <= i <= H1:
                    ptcopy(i - 1)
                if i < H1:
                    exps(i)
                    if i == 1:
                        act.wait_ge(m_ready, 1)
                        A_(scr[:], scr[:], ACT.Sqrt).then_inc(rt_m, 1)
                    if i < 8:
                        half_tanh(i, "gattn" if i < 4 else "grnn", i % 4)
                    else:
                        merge_gate(i - 8)
            squares(N_FIN1, x1_src(act, "out1"))
            rootmean(N_FIN1)
            act.wait_ge(normed, NM0[N_FIN1] + 8)
            squares(N_ATT2, lambda c, w: xT[:, c:c + w, :])
            rootmean(N_ATT2)

            def keep(stage, i, dst, n=2):
                bank = filled(act, stage, i)
                A_(dst, bank[:, :].rearrange("p (a b) -> p a b", a=n), ACT.Copy).then_inc(rel["act"], 1)

            act.wait_ge(unit_done, UNITS_AT[FILL0["aproj"] + 3])
            for i in range(3):
                keep("cq", i, cqT[:, 2 * i:2 * i + 2, :])
            keep("ckv2", 0, ckT)
            for i in range(2):
                keep("qb", i, qb[:, 2 * i:2 * i + 2, :])
            act.wait_ge(rel["act"], RELEASED[FILL0["ckv2"]])
            squares(N_CQ, lambda c, w: cqT[:, c:c + w, :])
            for i in range(2):
                keep("kb", i, kb[:, 2 * i:2 * i + 2, :])
            rootmean(N_CQ)
            squares(N_CKV2, lambda c, w: ckT)
            rootmean(N_CKV2)
            for i in range(2):
                bank = filled(act, "vb", i)
                A_(vb[:, i, :], bank[:, :], ACT.Copy).then_inc(rel["act"], 1)
            for i in range(2):
                bank = filled(act, "ukvk", i)
                v = bank[:, :].rearrange("p (a b) -> p a b", a=2)
                A_(kh[0:64, 4 * i:4 * i + 4:2, :], v[0:64], ACT.Copy)
                A_(kh[0:64, 4 * i + 1:4 * i + 4:2, :], v[64:128], ACT.Copy).then_inc(rel["act"], 1)
            for i in range(2):
                bank = filled(act, "ukvv", i)
                A_(vh[:, i, :], bank[:, :], ACT.Copy).then_inc(rel["act"], 1)
            for i in range(2 * H2 + 1):
                a = H1 + i
                if i >= 1:
                    ptcopy(a - 1)
                if i < 2 * H2:
                    exps(a)
                    if i % 2:
                        g = i // 2
                        bank = filled(act, "gates", g)
                        A_(tg2[:, 2 * g:2 * g + 2, :], bank[:, :].rearrange("p (a b) -> p a b", a=2), ACT.Tanh,
                           scale=0.5).then_inc(rel["act"], 1)
            squares(N_FFN, x1_src(act, "out2"))
            rootmean(N_FFN)
            act.wait_ge(rlog_mm, 1)
            lg = rt[:, 64:192].rearrange("p (a b) -> p a b", a=2)
            A_(lg[:, :, 0:NG + NE], QB[:, 0:128].rearrange("p (a b) -> p a b", a=2)[:, :, 0:NG + NE],
               ACT.Copy).then_inc(rlog, 1)
            for n in range(4):
                act.wait_ge(htok_mm, n + 1)
                A_(htok[:, n // 2, (n % 2) * 512:(n % 2 + 1) * 512], LB[n % 2][:, :], ACT.Copy).then_inc(htok_ready, 1)
            for tt in range(NT):
                act.wait_ge(gate_neg, tt + 1)
                A_(rt[:, 256 + 8 * tt:260 + 8 * tt], lg[:, tt, 0:NG], ACT.Exp, bias=rt[:, 272 + tt:273 + tt],
                   accum_out=rt[:, 274 + tt:275 + tt]).then_inc(expg, 1)
            act.wait_ge(topd, 2)
            A_(rt[:, 278:280], rt[:, 276:278], ACT.Exp).then_inc(expt, 1)
            for c in range(0, DC, 2):
                act.wait_ge(xs_mm, c + 1)
                A_(xs[:, c, 0:SLOTS], DB[0][:, :], ACT.Copy).then_inc(xs_ready, 1)
            for s2 in range(2):
                act.wait_ge(swt_mm, s2 + 1)
                A_(SWT[:, 2 * s2:2 * s2 + 2, :], LB[s2][:, :].rearrange("p (a b) -> p a b", a=2),
                   ACT.Copy).then_inc(swt_ready, 1)
            act.wait_ge(offs, 1)
            act.wait_ge(padz, 1)
            act.wait_ge(htok_ready, 4)
            offi, flag = rt[0:1, 512:544].bitcast(I32), rt[0:1, 544:545].bitcast(I32)

            def experts(n, slow):
                with act.Fori(0, NE // 2) as it:
                    for b in range(2):
                        off = act.value_load(offi[0:1, bass.ds(it * 2 + b, 1)], min_val=0, max_val=SLOTS)
                        act.wait_ge(moe_used, it * PAIR + (EXPERT_PANELS * b + 1))
                        act.wait_ge(act_ready, it * 2 + (b + 1))
                        A_(th[:, b, 0:2 * n], (L0 if slow else DB[b])[:, 0:2 * n], ACT.Tanh, scale=0.5).then_inc(gate_t, 1)
                        act.wait_ge(moe_used, it * PAIR + (EXPERT_PANELS * b + 3))
                        if slow:
                            for q, bank in enumerate((QB, OB, TB, UB)):
                                last = A_(ys[:, 2 * q:2 * q + 2, bass.ds(off, n)],
                                          bank[:, :].rearrange("p (a b) -> p a b", a=2), ACT.Copy)
                        else:
                            last = A_(ys[:, :, bass.ds(off, n)],
                                      (QB, OB)[b][:, :].rearrange("p (a b) -> p a b", a=DC), ACT.Copy)
                        last.then_inc(ys_done, 1)

            crowded = act.value_load(flag, min_val=0, max_val=1)
            with act.If(crowded):
                experts(T, True)
            with act.Else():
                experts(WIN, False)
            kept_all(act)
            for n in range(0, 8, 2):
                act.wait_ge(ysm_mm, n + 1)
                A_(ysm[:, n // 2, 0:512], L0[:, :], ACT.Copy).then_inc(ysm_ready, 1)
            squares(N_OUT, x3_src(act))
            rootmean(N_OUT)

        @block.vector
        def _(dve):
            v = nc.vector
            count = [0]

            def step(ins):
                count[0] += 1
                ins.then_inc(vstep, 1)
                dve.wait_ge(vstep, count[0])

            def stt(out_, in0, scalar, in1, op0=ALU.mult, op1=ALU.mult):
                return v.scalar_tensor_tensor(out=out_, in0=in0, scalar=scalar, in1=in1, op0=op0, op1=op1)

            def norm(n, src, dst, gain):
                nch = NORMS[n][0]
                dve.wait_ge(rooted, n + 1)
                if n:
                    dve.wait_ge(normed, NM0[n])
                v.reciprocal(rinv[:], root[:]).then_inc(rinvd, 1)
                dve.wait_ge(rinvd, n + 1)
                for c in range(nch):
                    stt(dst(c), src(c), V(gain, c), rinv[:]).then_inc(normed, 1)

            step(v.memset(sp[:, 9, :], EPS))
            dve.wait_ge(s_in["vec"], 16)
            dve.wait_ge(s_in["x"], 16)
            norm(N_X, lambda c: xT[:, c, :], lambda c: hT[:, c, :], "norm_gain")
            v.memset(xr[:, :, 0:CONV], 0.0).then_inc(padded, 1)
            step(v.tensor_scalar(halfb[:], V("b_merge", 0, 32), 0.5, None, ALU.mult))
            v.tensor_scalar(sp[:, 0, :], V("lru_lambda", 0, 8), -1.0, None, ALU.mult).then_inc(sp_step, 1)
            dve.wait_ge(sp_step, 1)
            v.tensor_tensor(sp[:, 1, :], sp[:, 0, :], V("lru_lambda", 0, 8), ALU.max).then_inc(sp_step, 1)
            dve.wait_ge(sp_act, 1)
            v.tensor_scalar(sp[:, 3, :], sp[:, 2, :], 1.0, None, ALU.add).then_inc(sp_step, 1)
            dve.wait_ge(sp_step, 3)
            step(v.tensor_scalar(sp[:, 5, :], sp[:, 3, :], 1.0, None, ALU.is_equal))
            step(stt(sp[:, 6, :], sp[:, 3, :], -1.0, sp[:, 5, :], ALU.add, ALU.add))
            step(v.reciprocal(sp[:, 7, :], sp[:, 6, :]))
            dve.wait_ge(sp_act, 2)
            step(v.tensor_tensor(sp[:, 6, :], sp[:, 4, :], sp[:, 5, :], ALU.add))
            step(v.tensor_tensor(sp[:, 6, :], sp[:, 6, :], sp[:, 2, :], ALU.mult))
            step(v.tensor_tensor(sp[:, 6, :], sp[:, 6, :], sp[:, 7, :], ALU.mult))
            step(stt(sp[:, 6, :], sp[:, 0, :], 0.0, sp[:, 6, :], ALU.max, ALU.add))
            step(v.tensor_scalar(sp[:, 7, :], sp[:, 6, :], LRU_C / 2, None, ALU.mult))
            v.tensor_scalar(sp[:, 8, :], sp[:, 6, :], -LRU_C / 2, None, ALU.mult).then_inc(sp_ready, 1)

            dve.wait_ge(mean_ready, 1)
            v.tensor_tensor(zc[:, 1, :], zc[:, 1, :], OB[:, 0:T], ALU.subtract).then_inc(centered, 1)
            norm(N_CKV, lambda c: zc[:, 0, :], lambda c: cT, "kv_norm_gain")
            dve.wait_ge(centered, 1)
            norm(N_KIDX, lambda c: zc[:, 1, :], lambda c: kiT, "idx_ln_gain")
            dve.wait_ge(normed, NM0[N_KIDX] + 1)
            v.tensor_scalar(kiT, kiT, V("idx_ln_bias"), None, ALU.add).then_inc(kidx_ready, 1)
            dve.wait_ge(widx_ready, 1)
            dve.wait_ge(s_in["cst"], 16)
            tiles = [(0, P), (P, T)]
            for j in range(IDXH):
                dve.wait_ge(idx_relu, j + 1)
                if j:
                    dve.wait_ge(idx_acc, j)
                for tt, (c0, n) in enumerate(tiles):
                    acc = score[:, c0:c0 + n]
                    last = stt(acc, S[:, j % 2, c0:c0 + n], widx[:, tt, j:j + 1],
                               acc if j else C("causal", n, c0), ALU.mult, ALU.add)
                last.then_inc(idx_acc, 1)
            dve.wait_ge(idx_acc, IDXH)
            for tt, (c0, n) in enumerate(tiles):
                s = score[:, c0:c0 + n]
                for r in range(TOPK // 8):
                    step(v.max(out=top8[:, tt, :], in_=s))
                    step(v.match_replace(out=s, in_to_replace=top8[:, tt, :], in_values=s, imm_value=TAKEN))
            step(v.tensor_scalar(score, score, TAKEN / 2, -BIG, ALU.is_gt, ALU.mult))
            v.tensor_tensor(Dm, score, C("dist", CAUSAL), ALU.add).then_inc(mask_ready, 1)
            dve.wait_ge(padded, 1)
            for c in range(8):
                kept(dve, "xrnn", c // 2)
                step(v.tensor_scalar(u[:, c, :], xr[:, c, 4:4 + T], V("conv_w", 3 * 8 + c), V("conv_b", c),
                                     ALU.mult, ALU.add))
                for t in (2, 1, 0):
                    ins = stt(u[:, c, :], xr[:, c, 1 + t:1 + t + T], V("conv_w", t * 8 + c), u[:, c, :],
                              ALU.mult, ALU.add)
                    if t:
                        step(ins)
                ins.then_inc(conv_done, 1)

            def bias_max(a):
                kind = 0 if a < H1 else 1
                dve.wait_ge(logits, a + 1)
                if a >= 2:
                    dve.wait_ge(expd, a - 1)
                sa = S[:, a % 2, :]
                if kind == 0:
                    ins = stt(sa, Dm, float(2.0 ** (-8.0 * (a + 1) / H1)), LB[a % 2][:, 0:CAUSAL], ALU.mult, ALU.add)
                else:
                    ins = stt(sa, LB[a % 2][:, 0:CAUSAL], MOBA_SCALE if a < H1 + H2 else MLA_SCALE,
                              C("causal", CAUSAL), ALU.mult, ALU.add)
                ins.then_inc(biased, 1)
                dve.wait_ge(biased, a + 1)
                for tt, (c0, n) in enumerate(tiles):
                    last = v.reduce_max(stat[:, a % 2, 0, tt:tt + 1], S[:, a % 2, c0:c0 + n], axis=AX.X, negate=True)
                last.then_inc(maxed, 1)

            def normalise(a):
                dve.wait_ge(expd, a + 1)
                step(v.reciprocal(stat[:, a % 2, 2, :], stat[:, a % 2, 1, :]))
                for tt, (c0, n) in enumerate(tiles):
                    last = v.tensor_scalar(E[:, a % 2, c0:c0 + n], E[:, a % 2, c0:c0 + n],
                                           stat[:, a % 2, 2, tt:tt + 1], None, ALU.mult)
                last.then_inc(probs, 1)

            def silu2(f, stage, i, dst):
                bank = DB[(FILL0[stage] + i) % 2]
                dve.wait_ge(tanhd, f + 1)
                stt(dst[:, 2 * i:2 * i + 2, :], th[:, f % 2, :].rearrange("p (a b) -> p a b", a=2), 1.0,
                    bank[:, :].rearrange("p (a b) -> p a b", a=2), ALU.add, ALU.mult).then_inc(rel["dve"], 1)

            dve.wait_ge(mask_ready, 1)

            def lru(i):
                if i == 0:
                    dve.wait_ge(sq_a, 4)
                    stt(scr[:], scr[:], 1.0, ra, ALU.add, ALU.mult).then_inc(m_ready, 1)
                elif i == 1:
                    step(stt(ib, ib, 1.0, u, ALU.add, ALU.mult))
                elif i == 2:
                    dve.wait_ge(rt_m, 1)
                    step(stt(ib, scr[:], 0.5, ib))
                elif i < 7:
                    for c in range(2 * (i - 3), 2 * (i - 3) + 2):
                        last = v.tensor_tensor_scan(u[:, c, :], la[:, c, :], ib[:, c, :], 0.0, ALU.mult, ALU.add)
                    step(last)
                elif 8 <= i < 12:
                    c = 2 * (i - 8)
                    kept(dve, "grnn", i - 8)
                    stt(u[:, c:c + 2, :], u[:, c:c + 2, :], 0.5, sr[:, c:c + 2, :]).then_inc(h_ready, 1)

            for i in range(H1 + 2):
                if i < H1:
                    bias_max(i)
                    lru(i)
                    normalise(i)
                if 1 <= i <= H1:
                    a = i - 1
                    dve.wait_ge(pv_mm, a + 1)
                    if a >= 2:
                        dve.wait_ge(o_mm, a - 1)
                    v.tensor_copy(olat[:, a % 2, :], OB[:, 0:T]).then_inc(olat_ready, 1)
                if i >= 3 and i % 2:
                    m = (i - 3) // 2
                    dve.wait_ge(o_mm, 2 * m + 2)
                    kept(dve, "gattn", m // 2)
                    stt(oT[:, m, :], UB[:, 0:T], 0.5, sg[:, m, :]).then_inc(o_ready, 1)
                if i < 8:
                    silu2(i, "gattn" if i < 4 else "grnn", i % 4, sg if i < 4 else sr)

            def layer_end(proj_r, proj_a, gate_r, gate_a, out_stage, n_mixed):
                for stage, gate in ((proj_r, gate_r), (proj_a, gate_a)):
                    for i in range(4):
                        bank = filled(dve, stage, i)
                        g = gate[:, 2 * i:2 * i + 2, :]
                        stt(g, g, 1.0, bank[:, :].rearrange("p (a b) -> p a b", a=2), ALU.add,
                            ALU.mult).then_inc(rel["dve"], 1)
                        if gate is gate_a:
                            kept(dve, stage, i)
                            v.tensor_tensor(g, g, gate_r[:, 2 * i:2 * i + 2, :], ALU.add).then_inc(mixed, 1)
                for i in range(4):
                    bank = filled(dve, out_stage, i)
                    r = xT[:, 2 * i:2 * i + 2, :]
                    stt(r, bank[:, :].rearrange("p (a b) -> p a b", a=2), 0.5, r, ALU.mult,
                        ALU.add).then_inc(rel["dve"], 1)

            kept(dve, "merge", 7)
            layer_end("rproj", "aproj", tm[:, 8:16, :], tm[:, 0:8, :], "out1", 0)
            kept(dve, "out1", 3)
            norm(N_FIN1, lambda c: xT[:, c, :], lambda c: xT[:, c, :], "final_norm_gain")
            norm(N_ATT2, lambda c: xT[:, c, :], lambda c: hT[:, c, :], "attn_norm_2")

            kept(dve, "ckv2", 0)
            norm(N_CQ, lambda c: cqT[:, c, :], lambda c: cqT[:, c, :], "q_norm_2")
            dve.wait_ge(kr_mm, 1)
            step(v.tensor_tensor(rot[64:96, 0, 0:T], QB[0:32, 0:T], cst[0:32, CST["cos_mla"]:CST["cos_mla"] + T], ALU.mult))
            step(v.tensor_tensor(rot[64:96, 1, 0:T], QB[32:64, 0:T], cst[32:64, CST["sin_mla"]:CST["sin_mla"] + T], ALU.mult))
            v.tensor_tensor(kh[64:96, :, :], rot[64:96, 0:1, 0:T].to_broadcast([32, H2, T]),
                            rot[64:96, 1:2, 0:T].to_broadcast([32, H2, T]), ALU.add).then_inc(kr_ready, 1)
            norm(N_CKV2, lambda c: ckT[:, c, :], lambda c: ckT[:, c, :], "kv_norm_2")
            dve.wait_ge(kr_ready, 1)
            kept(dve, "kb", 1)
            cosb = C("cos_moba", T).unsqueeze(1).to_broadcast([P, 2, T])
            sinb = C("sin_moba", T).unsqueeze(1).to_broadcast([P, 2, T])
            for i in range(4):
                x2 = (qb if i < 2 else kb)[:, (i % 2) * 2:(i % 2) * 2 + 2, :]
                r = rot[:, 0, :].rearrange("p (a b) -> p a b", a=2)
                dve.wait_ge(swap_mm, i + 1)
                if i:
                    dve.wait_ge(rotated, i)
                step(v.tensor_tensor(r, LB[i % 2][:, :].rearrange("p (a b) -> p a b", a=2), sinb, ALU.mult))
                step(v.tensor_tensor(x2, x2, cosb, ALU.mult))
                v.tensor_tensor(x2, x2, r, ALU.add).then_inc(rotated, 1)
            dve.wait_ge(rotated, 4)
            for i in range(4):
                bank = filled(dve, "uq", i)
                if i:
                    kept(dve, "uq", i - 1)
                b3 = bank[:, :].rearrange("p (a b) -> p a b", a=2)
                h2 = slice(2 * i, 2 * i + 2)
                cosq = cst[64:96, CST["cos_mla"]:CST["cos_mla"] + T].unsqueeze(1).to_broadcast([32, 2, T])
                sinq = cst[96:128, CST["sin_mla"]:CST["sin_mla"] + T].unsqueeze(1).to_broadcast([32, 2, T])
                r = rot[64:96, :, :].rearrange("p r (a b) -> p r a b", a=2)
                v.tensor_copy(qh[0:64, h2, :], b3[0:64])
                step(v.tensor_tensor(r[:, 0], b3[64:96], cosq, ALU.mult))
                step(v.tensor_tensor(r[:, 1], b3[96:128], sinq, ALU.mult))
                v.tensor_tensor(qh[64:96, h2, :], r[:, 0], r[:, 1], ALU.add).then_inc(rel["dve"], 1)
            for i in range(2 * H2 + 1):
                a = H1 + i
                if i < 2 * H2:
                    bias_max(a)
                    normalise(a)
                if i >= 2 and i % 2 == 0:
                    m = (i - 2) // 2
                    dve.wait_ge(o_mm, H1 + 2 * m + 2)
                    dst = oB if m < 4 else oA
                    v.tensor_copy(dst[:, m % 4, :], UB[:, 0:T]).then_inc(o_ready, 1)
            kept(dve, "gates", 7)
            layer_end("omla", "omoba", tg2[:, 0:8, :], tg2[:, 8:16, :], "out2", 4)
            kept(dve, "out2", 3)
            norm(N_FFN, lambda c: xT[:, c, :], lambda c: hT[:, c, :], "ffn_norm_2")

            A = rt[:, 0:64].rearrange("p (a b) -> p a b", a=2)
            lg = rt[:, 64:192].rearrange("p (a b) -> p a b", a=2)
            iota = C("iota", SLOTS)
            gpad = rt[:, 192:208].rearrange("p (a b) -> p a b", a=2)
            m8 = rt[:, 208:216]
            i8 = rt[:, 216:224].bitcast(U32)
            f8 = rt[:, 224:232]
            oh = rt[:, 232:236]
            pen = rt[:, 236:240]
            em = rt[:, 280:312]
            negm, sums, diff, ex = rt[:, 272:274], rt[:, 274:276], rt[:, 276:278], rt[:, 278:280]
            eid = rt[:, 312:316].rearrange("p (a b) -> p a b", a=2)
            OH = rt[:, 320:448].rearrange("p (a e b) -> p a e b", a=2, e=2)
            pos = rt[:, 448:452].rearrange("p (a b) -> p a b", a=2)
            wgt = rt[:, 452:456].rearrange("p (a b) -> p a b", a=2)
            tmp = rt[:, 456:488]
            cnt, offx = rt[:, 560:592], rt[:, 592:624]
            incl = rt[:, 624:656]
            onesf = ones[:, 0:NE]
            step(v.memset(rt[:, 192:208], TAKEN))
            dve.wait_ge(rlog, 1)
            for tt in range(NT):
                step(v.tensor_copy(gpad[:, tt, 0:NG], lg[:, tt, 0:NG]))
                step(v.max(out=m8, in_=gpad[:, tt, :]))
                v.tensor_scalar(negm[:, tt:tt + 1], m8[:, 0:1], -1.0, None, ALU.mult).then_inc(gate_neg, 1)
                step(v.max_index(i8, m8, gpad[:, tt, :]))
                step(v.tensor_copy(f8, i8))
                step(v.tensor_scalar(oh, iota[:, 0:NG], f8[:, 0:1], None, ALU.is_equal))
                step(v.tensor_scalar(pen, oh, -1.0, BIG, ALU.add, ALU.mult))
                e3 = em.rearrange("p (a b) -> p a b", a=NG)
                step(v.tensor_tensor(e3, lg[:, tt, NG:NG + NE].rearrange("p (a b) -> p a b", a=NG),
                                     oh.unsqueeze(2).to_broadcast([P, NG, EPG]), ALU.mult))
                step(v.tensor_tensor(e3, e3, pen.unsqueeze(2).to_broadcast([P, NG, EPG]), ALU.add))
                step(v.max(out=m8, in_=em))
                step(v.max_index(i8, m8, em))
                step(v.tensor_copy(f8, i8))
                step(v.tensor_copy(eid[:, tt, :], f8[:, 0:2]))
                v.tensor_tensor(diff[:, tt:tt + 1], m8[:, 1:2], m8[:, 0:1], ALU.subtract).then_inc(topd, 1)
                for e in range(2):
                    step(v.tensor_scalar(OH[:, tt, e, :], iota[:, 0:NE], eid[:, tt, e:e + 1], None, ALU.is_equal))
                v.tensor_tensor(A[:, tt, :], OH[:, tt, 0, :], OH[:, tt, 1, :], ALU.add).then_inc(onehot, 1)
            dve.wait_ge(expg, 2)
            dve.wait_ge(expt, 1)
            step(v.tensor_scalar(tmp[:, 0:2], ex, 1.0, None, ALU.add))
            step(v.tensor_tensor(tmp[:, 0:2], tmp[:, 0:2], sums, ALU.mult))
            step(v.reciprocal(wgt[:, 0:2, 0:1].rearrange("p a b -> p (a b)"), tmp[:, 0:2]))
            step(v.tensor_tensor(wgt[:, :, 1:2].rearrange("p a b -> p (a b)"),
                                 wgt[:, :, 0:1].rearrange("p a b -> p (a b)"), ex, ALU.mult))
            dve.wait_ge(cnt_mm, 1)
            step(v.tensor_copy(cnt, OB[:, 2 * NE:3 * NE]))
            step(v.tensor_tensor_scan(incl, onesf, cnt, 0.0, ALU.mult, ALU.add))
            step(v.tensor_tensor(offx, incl, cnt, ALU.subtract))
            step(v.tensor_copy(rt[:, 512:544].bitcast(I32), offx))
            step(v.reduce_max(tmp[:, 0:1], cnt, axis=AX.X))
            step(v.tensor_scalar(tmp[:, 0:1], tmp[:, 0:1], float(WIN), None, ALU.is_gt))
            v.tensor_copy(rt[:, 544:545].bitcast(I32), tmp[:, 0:1]).then_inc(offs, 1)
            dve.wait_ge(offs, 1)
            for tt in range(NT):
                step(v.tensor_tensor(incl, OB[:, tt * NE:(tt + 1) * NE], offx, ALU.add))
                for e in range(2):
                    step(v.tensor_tensor(tmp, incl, OH[:, tt, e, :], ALU.mult))
                    step(v.reduce_sum(pos[:, tt, e:e + 1], tmp, axis=AX.X))
                step(v.tensor_scalar(sel[:, tt, :], iota, pos[:, tt, 0:1], None, ALU.is_equal))
                step(v.tensor_scalar(sw[:, tt, :], sel[:, tt, :], wgt[:, tt, 0:1], None, ALU.mult))
                step(v.tensor_scalar(ysm[:, 3, 0:SLOTS], iota, pos[:, tt, 1:2], None, ALU.is_equal))
                step(stt(sw[:, tt, :], ysm[:, 3, 0:SLOTS], wgt[:, tt, 1:2], sw[:, tt, :], ALU.mult, ALU.add))
                v.tensor_tensor(sel[:, tt, :], sel[:, tt, :], ysm[:, 3, 0:SLOTS], ALU.add).then_inc(selected, 1)
            v.memset(xs[:, :, SLOTS:SLOTS + T], 0.0).then_inc(padz, 1)
            for c in range(1, DC, 2):
                dve.wait_ge(xs_mm, c + 1)
                v.tensor_copy(xs[:, c, 0:SLOTS], DB[1][:, :]).then_inc(xs_ready2, 1)
            for n in range(2):
                v.memset(actT[:, n, 0:8], 0.0).then_inc(act_ready, 1)
                v.memset(ys[:, n, 0:8], 0.0).then_inc(ys_done, 1)

            def experts(n, slow):
                with dve.Fori(0, NE // 2) as it:
                    for b in range(2):
                        gate = (L0 if slow else DB[b])[:, 0:2 * n]
                        up = (L1 if slow else LB[b])[:, 0:2 * n]
                        dve.wait_ge(gate_t, it * 2 + (b + 1))
                        dve.wait_ge(moe_used, it * PAIR + (EXPERT_PANELS * b + 2))
                        stt(th[:, b, 0:2 * n], th[:, b, 0:2 * n], 1.0, gate, ALU.add, ALU.mult).then_inc(silu_e, 1)
                        dve.wait_ge(silu_e, it * 2 + (b + 1))
                        stt(actT[:, b, 0:2 * n], th[:, b, 0:2 * n], 0.5, up).then_inc(act_ready, 1)

            dve.wait_ge(offs, 1)
            crowded = dve.value_load(rt[0:1, 544:545].bitcast(I32), min_val=0, max_val=1)
            with dve.If(crowded):
                experts(T, True)
            with dve.Else():
                experts(WIN, False)
            for n in range(1, 8, 2):
                dve.wait_ge(ysm_mm, n + 1)
                v.tensor_copy(ysm[:, n // 2, 512:1024], L1[:, :]).then_inc(ysm_ready2, 1)
            for i in range(4):
                dve.wait_ge(comb_mm, i + 1)
                r = xT[:, 2 * i:2 * i + 2, :]
                v.tensor_tensor(r, DB[i % 2][:, :].rearrange("p (a b) -> p a b", a=2), r, ALU.add).then_inc(comb, 1)
            dve.wait_ge(comb, 4)
            norm(N_OUT, lambda c: xT[:, c, :], lambda c: hT[:, c, :], "final_norm_2")



def chunks_of(w):
    k, m = w.shape
    return w.reshape(k // P, P, m // P, P).transpose(2, 1, 0, 3).reshape(m // P, P, k)


def k_major(w):
    k, m = w.shape
    return w.reshape(k // P, P, m).transpose(1, 0, 2)


def by_chunk(v):
    return v.reshape(-1, P).T


def units_of(a):
    return a.reshape(P, -1, UNIT).transpose(1, 0, 2)


def constants():
    f = np.float32
    t = np.arange(T, dtype=f)
    i = np.arange(P)
    c = {}
    c["ident"] = np.eye(P)
    c["ones"] = np.ones((P, P))
    c["mean64"] = ((i[:, None] // 64) == (i[None, :] // 64)) / 64.0
    r = i % 64
    partner = np.where(r < 8, i + 8, np.where(r < 16, i - 8, -1))
    c["swap"] = (i[:, None] == partner[None, :])
    c["before"] = i[:, None] < i[None, :]
    tok = np.concatenate([np.tile(i[:, None], (1, P)), np.tile(i[:, None] + P, (1, T))], 1)
    key = np.concatenate([np.arange(P), np.arange(T)])[None, :]
    c["causal"] = np.where(key <= tok, 0.0, -BIG)
    c["dist"] = np.where(key <= tok, -(tok - key), -BIG)

    def tables(rot):
        half = rot // 2
        inv = np.power(f(500000.0), -np.arange(half, dtype=f) / f(half)).astype(f)
        ang = (t[:, None] * inv[None, :]).astype(f)
        return np.cos(ang).T, np.sin(ang).T

    cos, sin = tables(ROPE)
    rows = i % 16
    c["cos_mla"] = cos[rows]
    c["sin_mla"] = sin[rows] * np.where(i % 32 < 16, -1.0, 1.0)[:, None]
    cos, sin = tables(MROT)
    c["cos_moba"] = np.where((r < 16)[:, None], cos[r % 8], 1.0)
    c["sin_moba"] = sin[r % 8] * np.where(r < 8, -1.0, np.where(r < 16, 1.0, 0.0))[:, None]
    c["iota"] = np.tile(np.arange(SLOTS), (P, 1))
    return np.ascontiguousarray(np.concatenate([c[n] for n in CST], 1).astype(f))


def pack(g):
    w = g["w_in"][0]
    cut = np.cumsum([0, 1024, 128, 512, 64, 8, 1024, 1024, 1024, 2048])
    q, ckv, qi, ki, wi, ga, xr, gr, mg = [w[:, a:b] for a, b in zip(cut[:-1], cut[1:])]
    w2 = g["w_in_2"][0]
    cut = np.cumsum([0, QL, KL, ROPE, 512, 512, 512, D, D])
    cq, ck, kr, qb, kb, vb, gA, gB = [w2[:, a:b] for a, b in zip(cut[:-1], cut[1:])]
    half = ROPE // 2
    uq = g["w_uq_2"][0].reshape(QL, H2, HD2 + ROPE)
    uq = np.concatenate([uq, uq[:, :, HD2 + half:], uq[:, :, HD2:HD2 + half]], 2)
    uqu = np.pad(chunks_of(uq.reshape(QL, H2 * P)), ((0, 0), (0, 0), (0, UNIT - QL)))
    ukv = g["w_ukv_2"][0].reshape(KL, H2, 2 * HD2)
    uk = chunks_of(ukv[:, :, :HD2].reshape(KL, 512)).transpose(1, 0, 2).reshape(P, UNIT)
    uv = k_major(ukv[:, :, HD2:].reshape(KL, 512)).reshape(P, UNIT)
    parts = [chunks_of(a) for a in (np.concatenate([ckv, ki, ki], 1), qi, xr, q, ga, gr, mg,
                                    g["w_rnn_proj"][0], g["w_attn_proj"][0], g["w_out"][0], cq, ck, qb, kb)]
    parts.append(units_of(k_major(vb).reshape(P, 4 * UNIT)))
    parts += [uqu, uk[None], uv[None], chunks_of(np.concatenate([gA, gB], 1))]
    for name in ("w_o_mla_2", "w_o_moba_2"):
        parts.append(units_of(chunks_of(g[name][0]).transpose(1, 0, 2).reshape(P, 4 * UNIT)))
    parts.append(chunks_of(g["w_out_2"][0]))
    dense = np.concatenate(parts, 0)
    dense = dense.reshape(-1, 2, P, UNIT).transpose(0, 2, 1, 3).reshape(-1, P, 2 * UNIT)
    gate, up, down = (g[n][0] for n in ("w_exp_gate_2", "w_exp_up_2", "w_exp_down_2"))
    gu = [a.reshape(NE, DC, P, 2, P).transpose(0, 2, 3, 1, 4).reshape(NE, P, 2 * UNIT) for a in (gate, up)]
    dn = down.reshape(NE, 2, P, D).transpose(0, 2, 1, 3).reshape(NE, P, 2 * UNIT)
    expert = np.stack([gu[0], gu[1], dn], 1).reshape(NE * EXPERT_PANELS, P, 2 * UNIT)
    idx2 = lambda a: np.concatenate([a, a])
    cols = {"conv_w": g["conv_w"][0].reshape(CONV * 8, P).T, "idx_ln_gain": idx2(g["idx_ln_gain"][0])[:, None],
            "idx_ln_bias": idx2(g["idx_ln_bias"][0])[:, None], "final_norm_gain": by_chunk(g["final_norm_gain"]),
            "final_norm_2": by_chunk(g["final_norm_2"])}
    vecs = np.concatenate([cols[n] if n in cols else by_chunk(g[n][0]) for n in VEC], 1)
    rg = np.zeros((P, 2, 8, P), np.float32)
    for n, name in enumerate(("w_rg_a", "w_rg_x")):
        b = g[name][0].reshape(8, 2, 64, 64)
        for s in range(2):
            rg[64 * s:64 * s + 64, n, :, 64 * s:64 * s + 64] = b[:, s].transpose(1, 0, 2)
    wuk = g["w_uk"][0].reshape(8, 2, LAT, HD1).transpose(1, 3, 0, 2).reshape(P, 8 * LAT)
    wuv = g["w_uv"][0].transpose(1, 0, 2).reshape(LAT, H1 * HD1)
    wkr = k_major(np.concatenate([kr, kr[:, half:], kr[:, :half]], 1)).reshape(P, -1)
    wre = g["w_router_expert_2"][0].transpose(1, 0, 2).reshape(D, NE)
    wrt = k_major(np.concatenate([g["w_router_group_2"][0], wre], 1)).reshape(P, -1)
    brt = np.concatenate([g["b_router_group_2"][0], g["b_router_expert_2"][0].reshape(-1)])[None, :]
    x_t = g["x"][0].T.reshape(DC, P, T).transpose(1, 0, 2).reshape(P, DC * T)
    arrays = dict(x_t=x_t, vecs=vecs, consts=constants(), w_widx=k_major(wi).reshape(P, -1),
                  w_rg=rg.reshape(P, -1), w_uk=wuk, w_uv=wuv, w_kr=wkr, w_router=wrt, b_router=brt,
                  w_dense=dense, w_expert=expert)
    return {k: np.ascontiguousarray(v) for k, v in arrays.items()}


def kernel(**inputs):
    import concourse.bacc as bacc
    from concourse.bass_utils import run_bass_kernel_spmd

    arrays = pack({k: np.asarray(v) for k, v in inputs.items()})
    nc = bacc.Bacc("TRN2", target_bir_lowering=False, num_devices=1)
    aps = {n: nc.dram_tensor(f"{n}_dram", a.shape, mybir.dt.from_np(a.dtype), kind="ExternalInput").ap()
           for n, a in arrays.items()}
    out = nc.dram_tensor("out_dram", (P, DC * T), F32, kind="ExternalOutput").ap()
    build(nc, out=out, **aps)
    r = run_bass_kernel_spmd(nc, [{f"{n}_dram": a for n, a in arrays.items()}], core_ids=[0])
    y = r.results[0]["out_dram"].reshape(P, DC, T)
    return np.ascontiguousarray(y.transpose(2, 1, 0).reshape(1, T, D))
```

```python
import numpy as np
import concourse.bass as bass
from concourse import mybir
from contextlib import ExitStack

F32 = mybir.dt.float32
I32 = mybir.dt.int32
U32 = mybir.dt.uint32
ACT = mybir.ActivationFunctionType
ALU = mybir.AluOpType
AX = mybir.AxisListType

P = 128
T = 256
NT = T // P
D = 1024
DC = D // P
EPS = 1e-6
BIG = 1e30
TAKEN = -3e38

H1, HD1, LAT = 16, 64, 128
IDXH, IDXD = 8, 64
TOPK = min(256, T // 4)
CONV = 4
LRU_C = 8.0
H2, HD2 = 8, 64
ROPE, MROT = 32, 16
QL, KL = 768, 256
QC, KC = QL // P, KL // P
MLA_SCALE = float((HD2 + ROPE) ** -0.5)
MOBA_SCALE = float(HD2 ** -0.5)
NG, EPG = 4, 8
NE = NG * EPG
FF = 256
SLOTS = 2 * T
WIN = 64
CAUSAL = P + T

UNIT = 1024
RING = 6

PLAN = [
    ("ckv_kidx", [2], "act"), ("qidx", [2, 4], "act"), ("xrnn", [2, 4, 6, 8], "act"),
    ("q", [2, 4, 6, 8], "act"), ("gattn", [2, 4, 6, 8], "dve"), ("grnn", [2, 4, 6, 8], "dve"),
    ("merge", [2, 4, 6, 8, 10, 12, 14, 16], "act"), ("rproj", [2, 4, 6, 8], "dve"),
    ("aproj", [2, 4, 6, 8], "dve"), ("out1", [2, 4, 6, 8], "dve"),
    ("cq", [2, 4, 6], "act"), ("ckv2", [2], "act"), ("qb", [2, 4], "act"), ("kb", [2, 4], "act"),
    ("vb", [4, 4], "act"), ("uq", [2, 4, 6, 8], "dve"), ("ukvk", [1, 1], "act"),
    ("ukvv", [1, 1], "act"), ("gates", [2, 4, 6, 8, 10, 12, 14, 16], "act"),
    ("omla", [1, 2, 3, 4], "dve"), ("omoba", [1, 2, 3, 4], "dve"), ("out2", [2, 4, 6, 8], "dve"),
]
FILL0, UNIT0, UNITS_AT, RELEASE = {}, {}, [], []
_u = 0
for _name, _ends, _eng in PLAN:
    FILL0[_name], UNIT0[_name] = len(UNITS_AT), _u
    for _e in _ends:
        UNITS_AT.append(_u + _e)
        RELEASE.append(_eng)
    _u += _ends[-1]
DENSE_UNITS = _u
DENSE_PANELS = DENSE_UNITS // 2
UNUSED_PANEL = 2
WINDOWS = T // 64
RELEASED = [RELEASE[:f + 1].count(RELEASE[f]) for f in range(len(RELEASE))]

NORMS = [(8, D), (1, LAT), (1, 1), (8, D), (8, D), (6, QL), (2, KL), (8, D), (8, D)]
N_X, N_CKV, N_KIDX, N_FIN1, N_ATT2, N_CQ, N_CKV2, N_FFN, N_OUT = range(9)
SQ0 = [sum((c + 1) // 2 for c, _ in NORMS[:k]) for k in range(10)]
NM0 = [sum(c for c, _ in NORMS[:k]) for k in range(10)]

VEC = {}
_c = 0
for _name, _n in [("norm_gain", 8), ("b_merge", 16), ("b_rg_a", 8), ("b_rg_x", 8), ("kv_norm_gain", 1),
                  ("idx_ln_gain", 1), ("idx_ln_bias", 1), ("conv_w", 32), ("conv_b", 8), ("lru_lambda", 8),
                  ("final_norm_gain", 8), ("attn_norm_2", 8), ("q_norm_2", 6), ("kv_norm_2", 2),
                  ("ffn_norm_2", 8), ("final_norm_2", 8)]:
    VEC[_name] = _c
    _c += _n
NVEC = _c
CST = {}
_c = 0
for _name, _n in [("ident", P), ("ones", P), ("mean64", P), ("swap", P), ("before", P), ("dist", CAUSAL),
                  ("causal", CAUSAL), ("cos_mla", T), ("sin_mla", T), ("cos_moba", T), ("sin_moba", T),
                  ("iota", SLOTS)]:
    CST[_name] = _c
    _c += _n
NCST = _c


def build(nc, x_t, vecs, consts, w_widx, w_rg, w_uk, w_uv, w_kr, w_router, b_router, w_dense, w_expert, out):
    ctx = ExitStack()
    with ctx:
        def sb(name, shape, dt=F32):
            return ctx.enter_context(nc.sbuf_tensor(name, shape, dt))

        def sem(name):
            return ctx.enter_context(nc.semaphore(name))

        ring = sb("ring", [P, RING, 2 * UNIT])
        vec = sb("vec", [P, NVEC])
        cst = sb("cst", [P, NCST])
        xT = sb("xT", [P, DC, T])
        hT = sb("hT", [P, DC, T])
        scr = sb("scr", [P, DC, T])
        widx_w = sb("widx_w", [P, DC, IDXH])
        wkr = sb("wkr", [P, DC, 2 * ROPE])
        wrt = sb("wrt", [P, DC, NG + NE])
        brt = sb("brt", [1, NG + NE])
        wuk = sb("wuk", [P, H1 // 2, LAT])
        wuv = sb("wuv", [P, H1, HD1])
        root = sb("root", [P, T])
        rinv = sb("rinv", [P, T])
        halfb = sb("halfb", [P, 32])
        sp = sb("sp", [P, 10, 8])
        S = sb("S", [P, 2, CAUSAL])
        E = sb("E", [P, 2, CAUSAL])
        PT = sb("PT", [P, 2, CAUSAL])
        stat = sb("stat", [P, 2, 3, 2])
        th = sb("th", [P, 2, 2 * T])
        big = sb("big", [P, 19 * 1024])
        small = sb("small", [P, 5 * 1024])

        def at(region, off, *dims):
            n = 1
            for d in dims:
                n *= d
            v = region[:, off:off + n]
            if len(dims) == 2:
                v = v.rearrange("p (a b) -> p a b", a=dims[0])
            if len(dims) == 3:
                v = v.rearrange("p (a b c) -> p a b c", a=dims[0], b=dims[1])
            return v

        K = 1024
        qT = at(big, 0, 8, T)
        oT = qT
        xr = at(big, 2 * K, 8, T + CONV)
        la = at(big, 2 * K, 8, T)
        u = at(big, 5 * K - 512, 8, T)
        ra = at(big, 7 * K - 512, 8, T)
        ib = at(big, 9 * K - 512, 8, T)
        sg = at(big, 11 * K - 512, 8, T)
        sr = at(big, 13 * K - 512, 8, T)
        tm = at(big, 15 * K - 512, 16, T)
        wrg = at(big, 15 * K - 512, 2, 8, P)
        qi = at(small, 0, 4, T)
        zc = at(small, K, 2, T)
        kiT = at(small, K + 512, T)
        cT = at(small, K + 768, T)
        ctok = at(small, 2 * K, 2, LAT)
        widx = at(small, 2 * K + 256, 2, IDXH)
        qlat = at(small, 2 * K + 512, 2, T)
        olat = at(small, 3 * K, 2, T)
        score = at(small, 3 * K + 512, CAUSAL)
        Dm = at(small, 4 * K, CAUSAL)
        top8 = at(small, 4 * K + 512, 2, 8)
        cqT = at(big, 0, QC, T)
        ckT = at(big, 6 * 256, KC, T)
        qb = at(big, 2 * K, 4, T)
        kb = at(big, 3 * K, 4, T)
        vb = at(big, 4 * K, 2, 512)
        qh = at(big, 5 * K, H2, T)
        kh = at(big, 7 * K, H2, T)
        vh = at(big, 9 * K, 2, 512)
        tg2 = at(big, 10 * K, 16, T)
        oA = at(big, 14 * K, 4, T)
        oB = at(big, 15 * K, 4, T)
        krT = at(big, 16 * K, T)
        rot = at(big, 16 * K + 256, 2, 512)
        xs = at(big, 0, DC, SLOTS + WIN)
        ys = at(big, 4 * K + 512, DC, SLOTS + WIN)
        ysm = at(big, 9 * K, SLOTS // P, D)
        htok = at(big, 9 * K, 2, D)
        SWT = at(big, 13 * K, SLOTS // P, T)
        sel = at(big, 14 * K, 2, SLOTS)
        sw = at(big, 15 * K, 2, SLOTS)
        actT = at(small, 0, 2, 2, WIN)
        xe = at(small, 3 * K, 2, DC, WIN)
        ye = scr.rearrange("p (b c) t -> p b (c t)", b=4)
        rt = at(small, K, 2048)

        def V(name, i=0, n=1):
            return vec[:, VEC[name] + i:VEC[name] + i + n]

        def C(name, n, i=0):
            return cst[:, CST[name] + i:CST[name] + i + n]

        ident, ones = C("ident", P), C("ones", P)

        D0, D1, L0, L1, TB, QB, OB, UB = [ctx.enter_context(nc.psum_tensor(n, [P, 512], F32))
                                          for n in ("D0", "D1", "L0", "L1", "TB", "QB", "OB", "UB")]
        DB, LB = [D0, D1], [L0, L1]

        arrived = [sem(f"panel_arrived_{i}") for i in range(RING)]
        s_in = {n: sem(f"in_{n}") for n in ("x", "vec", "cst", "widx", "wrg", "wuk", "wuv", "wkr", "wrt", "brt")}
        unit_done, panel_used = sem("unit_done"), sem("expert_panel_used")
        rel = {"act": sem("bank_released_by_act"), "dve": sem("bank_released_by_dve")}
        sq, ssq, rooted, rinvd, normed = [sem(n) for n in ("squared", "sumsq_ready", "rooted", "rinv_ready", "normed")]
        tanhd = sem("tanh_ready")
        vstep, astep = sem("vector_step"), sem("scalar_step")
        mean_ready, centered, kidx_ready, widx_mm, widx_ready = [sem(n) for n in (
            "mean_ready", "centered", "kidx_ready", "widx_matmul", "widx_ready")]
        ctok_mm, ctok_ready = sem("ctok_transposed"), sem("ctok_ready")
        idx_mm, idx_relu, idx_acc = sem("idx_scores"), sem("idx_relu"), sem("idx_accumulated")
        mask_ready = sem("mask_ready")
        padded, conv_done, gate_mm, gates, decay, sq_a, m_ready, rt_m, h_ready = [sem(n) for n in (
            "conv_padded", "conv_done", "rg_gates_matmul", "rg_gates_ready", "decay_ready", "decay_squared",
            "m_ready", "m_rooted", "gated_h_ready")]
        sp_step, sp_act, sp_ready = sem("softplus_step"), sem("softplus_act"), sem("softplus_ready")
        qlat_mm, qlat_ready = sem("qlat_matmul"), sem("qlat_ready")
        logits, biased, maxed, expd, probs = [sem(n) for n in ("logits", "biased", "maxed", "expd", "probs")]
        pt_mm, pt_ready, pv_mm, olat_ready, o_mm, o_ready = [sem(n) for n in (
            "probs_transposed", "pt_ready", "pv_matmul", "olat_ready", "o_matmul", "o_ready")]
        mixed = sem("mixed_ready")
        kr_mm, kr_ready = sem("krope_matmul"), sem("krope_ready")
        swap_mm, rotated = sem("swap_matmul"), sem("moba_rotated")
        rlog_mm, rlog, gate_neg, expg, topd, expt, onehot, cnt_mm, selected, offs = [sem(n) for n in (
            "router_matmul", "router_logits", "group_max", "group_exp", "top2", "top2_exp", "onehot_ready",
            "rank_matmul", "selection_ready", "offsets_ready")]
        htok_mm, htok_ready, swt_mm, swt_ready, xs_mm, xs_ready, xs_ready2 = [sem(n) for n in (
            "htok_transposed", "htok_ready", "swt_transposed", "swt_ready", "gathered", "xs_by_act", "xs_by_dve")]
        padz = sem("pads_zero")
        xe_ready, gu_done, gate_t, silu_e, act_ready, at_mm, at_ready, y_mm, ye_ready, yt_mm, ys_done = [
            sem(n) for n in ("window_staged", "gate_up_done", "expert_gate_tanh", "expert_silu", "expert_act_ready",
                             "act_transposed", "act_t_ready", "down_done", "down_kept", "out_transposed",
                             "expert_out_kept")]
        ysm_mm, ysm_ready, ysm_ready2, comb_mm, comb = [sem(n) for n in (
            "ys_transposed", "ysm_by_act", "ysm_by_dve", "combined_matmul", "combined")]
        stored = sem("stored")

        def freed(eng, f):
            eng.wait_ge(rel[RELEASE[f]], RELEASED[f])

        def kept(eng, stage, i):
            freed(eng, FILL0[stage] + i)

        def filled(eng, stage, i):
            f = FILL0[stage] + i
            eng.wait_ge(unit_done, UNITS_AT[f])
            return DB[f % 2]

        def window_offset(eng, n):
            return eng.value_load(rt[0:1, 828:956].bitcast(I32)[0:1, bass.ds(n, 1)], min_val=0, max_val=SLOTS)

        def since(eng, s_, it, c):
            if it is not None or c >= 0:
                eng.wait_ge(s_, (0 if it is None else it * 2) + (c + 1))

        def expert_steps(eng, one):
            for e in range(3):
                one(None, e)
            with eng.Fori(1, NE // 2 - 1) as it:
                for c in (1, 2):
                    one(it, c)
            one(None, NE - 1)

        def expert_panel(eng, it, c, n):
            g = DENSE_PANELS + 3 * c + n
            lap = g // RING + 1 - (1 if g % RING == (DENSE_PANELS + UNUSED_PANEL) % RING else 0)
            eng.wait_ge(arrived[g % RING], (0 if it is None else it * 16) + 16 * lap)
            return ring[:, g % RING, :]

        def expert_banks(b):
            return (D0, D1)[b], (TB, L1)[b], (QB, L0)[b], (OB, UB)[b]

        def x1_src(eng, stage):
            def src(c, w):
                kept(eng, stage, c // 2)
                return xT[:, c:c + w, :]
            return src

        def x3_src(eng):
            def src(c, w):
                eng.wait_ge(comb, c // 2 + 1)
                return xT[:, c:c + w, :]
            return src

        block = ctx.enter_context(nc.Block())

        @block.sync
        def _(sp_):
            def panel(slot, src):
                return sp_.dma_start(ring[:, slot, :], src).then_inc(arrived[slot], 16)

            sp_.dma_start(xT[:], x_t.rearrange("p (c t) -> p c t", c=DC)).then_inc(s_in["x"], 16)
            sp_.dma_start(vec[:], vecs).then_inc(s_in["vec"], 16)
            sp_.dma_start(cst[:, 0:NCST], consts).then_inc(s_in["cst"], 16)
            panel(0, w_dense[0])
            sp_.dma_start(widx_w[:], w_widx.rearrange("p (c t) -> p c t", c=DC)).then_inc(s_in["widx"], 16)
            for p in range(1, RING):
                panel(p, w_dense[p])
            sp_.dma_start(wrg, w_rg.rearrange("p (a c t) -> p a c t", a=2, c=8)).then_inc(s_in["wrg"], 16)
            sp_.dma_start(wuk[:], w_uk.rearrange("p (c t) -> p c t", c=8)).then_inc(s_in["wuk"], 16)
            sp_.dma_start(wuv[:], w_uv.rearrange("p (c t) -> p c t", c=16)).then_inc(s_in["wuv"], 16)
            sp_.dma_start(wkr[:], w_kr.rearrange("p (c t) -> p c t", c=DC)).then_inc(s_in["wkr"], 16)
            sp_.dma_start(wrt[:], w_router.rearrange("p (c t) -> p c t", c=DC)).then_inc(s_in["wrt"], 16)
            sp_.dma_start(brt[:], b_router).then_inc(s_in["brt"], 16)
            laps = DENSE_PANELS // RING
            with sp_.Fori(1, laps) as lap:
                for slot in range(RING):
                    sp_.wait_ge(unit_done, lap * (2 * RING) + (2 * slot + 2 - 2 * RING))
                    sp_.dma_start(ring[:, slot, :], w_dense[bass.ds(lap * RING + slot, 1)].rearrange(
                        "a p n -> p (a n)")).then_inc(arrived[slot], 16)
            for p in range(laps * RING, DENSE_PANELS):
                sp_.wait_ge(unit_done, 2 * (p - RING) + 2)
                panel(p % RING, w_dense[p])
            def expert(p, it=None):
                slot = (DENSE_PANELS + p) % RING
                row = p - (p > UNUSED_PANEL) - 2 * (p > 3 * NE)
                src = w_expert[row] if it is None else w_expert[bass.ds(it * RING + (p - 1), 1)].rearrange(
                    "a p n -> p (a n)")
                sp_.dma_start(ring[:, slot, :], src).then_inc(arrived[slot], 16)

            for p in range(RING):
                if p != UNUSED_PANEL:
                    sp_.wait_ge(unit_done, 2 * (DENSE_PANELS + p - RING) + 2)
                    expert(p)
            with sp_.Fori(1, 3 * NE // RING) as lap:
                for p in range(RING):
                    sp_.wait_ge(panel_used, lap * RING + (p + 1 - RING))
                    expert(p, lap)
            sp_.wait_ge(panel_used, 3 * NE + 3 - RING)
            expert(3 * NE + 2)
            for c in range(0, DC, 2):
                sp_.wait_ge(normed, NM0[N_OUT] + c + 2)
                sp_.dma_start(out[:, c * T:(c + 2) * T].rearrange("p (c t) -> p c t", c=2),
                              hT[:, c:c + 2, :]).then_inc(stored, 16)
            sp_.wait_ge(stored, 16 * (DC // 2))

        @block.tensor
        def _(pe):
            mm = nc.tensor.matmul
            seen = [0]

            def unit(n):
                p = n // 2
                if p >= seen[0]:
                    pe.wait_ge(arrived[p % RING], 16 * (p // RING + 1))
                    seen[0] = p + 1
                return ring[:, p % RING, (n % 2) * UNIT:(n % 2 + 1) * UNIT]

            def open_bank(stage, i):
                f = FILL0[stage] + i
                if f >= 2:
                    freed(pe, f - 2)
                return DB[f % 2]

            def chunk(stage, c, src, kc=DC, ready=None):
                bank = open_bank(stage, c // 2) if c % 2 == 0 else DB[(FILL0[stage] + c // 2) % 2]
                w = unit(UNIT0[stage] + c)
                for k in range(kc):
                    if ready is not None:
                        pe.wait_ge(normed, ready + k + 1)
                    last = mm(bank[:, (c % 2) * T:(c % 2 + 1) * T], w[:, k * P:(k + 1) * P], src[:, k, :],
                              start=(k == 0), stop=(k == kc - 1))
                last.then_inc(unit_done, 1)

            def sumsq(n, lhs=None):
                nch = NORMS[n][0]
                if n:
                    pe.wait_ge(rooted, n)
                for c in range(nch):
                    pe.wait_ge(sq, SQ0[n] + c // 2 + 1)
                    last = mm(UB[:, 0:T], ones if lhs is None else lhs, scr[:, c, :],
                              start=(c == 0), stop=(c == nch - 1))
                last.then_inc(ssq, 1)

            pe.wait_ge(s_in["cst"], 16)
            sumsq(N_X)
            for c in range(2):
                chunk("ckv_kidx", c, hT, ready=NM0[N_X] if c == 0 else None)
            chunk("qidx", 0, hT)
            kept(pe, "ckv_kidx", 0)
            mm(OB[:, 0:T], C("mean64", P), zc[:, 1, :], start=True, stop=True).then_inc(mean_ready, 1)
            chunk("qidx", 1, hT)
            sumsq(N_CKV)
            pe.wait_ge(s_in["widx"], 16)
            for tt in range(NT):
                for k in range(DC):
                    last = mm(QB[:, tt * IDXH:(tt + 1) * IDXH], hT[:, k, tt * P:(tt + 1) * P], widx_w[:, k, :],
                              start=(k == 0), stop=(k == DC - 1))
            last.then_inc(widx_mm, 1)
            chunk("qidx", 2, hT)
            sumsq(N_KIDX, C("mean64", P))
            chunk("qidx", 3, hT)
            chunk("xrnn", 0, hT)
            pe.wait_ge(kidx_ready, 1)
            kept(pe, "qidx", 1)
            for j in range(IDXH):
                if j >= 2:
                    pe.wait_ge(idx_relu, j - 1)
                lo = IDXD * (j % 2)
                mm(LB[j % 2][:, 0:P], qi[lo:lo + IDXD, j // 2, 0:P], kiT[lo:lo + IDXD, 0:P], start=True, stop=True)
                mm(LB[j % 2][:, P:CAUSAL], qi[lo:lo + IDXD, j // 2, P:T], kiT[lo:lo + IDXD, 0:T],
                   start=True, stop=True).then_inc(idx_mm, 1)
            pe.wait_ge(normed, NM0[N_CKV] + 1)
            for s in range(2):
                last = nc.tensor.transpose(OB[:, 256 + s * P:256 + (s + 1) * P], cT[:, s * P:(s + 1) * P], ident)
            last.then_inc(ctok_mm, 1)
            for c in range(1, 8):
                chunk("xrnn", c, hT)
            for c in range(8):
                chunk("q", c, hT)
            pe.wait_ge(s_in["wrg"], 16)
            for c in range(8):
                pe.wait_ge(conv_done, c + 1)
                pe.wait_ge(idx_relu, IDXH)
                if c >= 2:
                    pe.wait_ge(gates, c - 1)
                for g in range(2):
                    last = mm(LB[c % 2][:, g * T:(g + 1) * T], wrg[:, g, c, :], u[:, c, :], start=True, stop=True)
                last.then_inc(gate_mm, 1)

            def scores(a, q_of, k_of):
                pe.wait_ge(biased, a - 1) if a >= 2 else pe.wait_ge(gates, 8)
                for tt in range(NT):
                    c0, n = (0, P) if tt == 0 else (P, T)
                    last = mm(LB[a % 2][:, c0:c0 + n], q_of(tt), k_of(n), start=True, stop=True)
                last.then_inc(logits, 1)

            def transposes(a):
                pe.wait_ge(probs, a + 1)
                if a >= 1:
                    pe.wait_ge(pt_ready, a)
                for b in range(3):
                    last = nc.tensor.transpose(TB[:, b * P:(b + 1) * P], E[:, a % 2, b * P:(b + 1) * P], ident)
                last.then_inc(pt_mm, 1)

            def pv(a, dst, v_of):
                pe.wait_ge(pt_ready, a + 1)
                mm(dst[:, 0:T], v_of(0), PT[:, a % 2, 0:T], start=True, stop=False, skip_group_check=True)
                return mm(dst[:, P:T], v_of(1), PT[:, a % 2, T:CAUSAL], start=False, stop=True, skip_group_check=True)

            todo = [("gattn", c) for c in range(8)] + [("grnn", c) for c in range(8)] + [("merge", c) for c in range(16)]

            def fill():
                if todo:
                    chunk(*todo.pop(0), hT)

            pe.wait_ge(s_in["wuk"], 16)
            pe.wait_ge(s_in["wuv"], 16)
            kept(pe, "q", 3)
            pe.wait_ge(ctok_ready, 1)
            pe.wait_ge(widx_ready, 1)
            for i in range(H1 + 2):
                if i < H1:
                    lo = HD1 * (i % 2)
                    if i >= 1:
                        pe.wait_ge(qlat_ready, i)
                    mm(QB[:, 0:T], wuk[lo:lo + HD1, i // 2, :], qT[lo:lo + HD1, i // 2, :],
                       start=True, stop=True).then_inc(qlat_mm, 1)
                fill()
                if i < H1:
                    pe.wait_ge(qlat_ready, i + 1)
                    scores(i, lambda tt: qlat[:, i % 2, tt * P:(tt + 1) * P], lambda n: cT[:, 0:n])
                if 1 <= i <= H1:
                    transposes(i - 1)
                fill()
                if 1 <= i <= H1:
                    if i >= 2:
                        pe.wait_ge(olat_ready, i - 1)
                    pv(i - 1, OB, lambda s: ctok[:, s, :]).then_inc(pv_mm, 1)
                if i >= 2:
                    a = i - 2
                    pe.wait_ge(olat_ready, a + 1)
                    if a % 2 == 0 and a >= 2:
                        pe.wait_ge(o_ready, a // 2)
                    lo = HD1 * (a % 2)
                    mm(UB[lo:lo + HD1, 0:T], wuv[:, a, :], olat[:, a % 2, :], start=True, stop=True).then_inc(o_mm, 1)
            while todo:
                fill()
            pe.wait_ge(h_ready, 4)
            for c in range(8):
                chunk("rproj", c, u)
            pe.wait_ge(o_ready, 8)
            for c in range(8):
                chunk("aproj", c, oT)
            pe.wait_ge(mixed, 4)
            for c in range(8):
                chunk("out1", c, tm)
            sumsq(N_FIN1)
            sumsq(N_ATT2)

            for c in range(6):
                chunk("cq", c, hT, ready=NM0[N_ATT2] if c == 0 else None)
            for c in range(2):
                chunk("ckv2", c, hT)
            for c in range(4):
                chunk("qb", c, hT)
            for c in range(4):
                chunk("kb", c, hT)
            for i in range(2):
                bank = open_bank("vb", i)
            vb_banks = [DB[(FILL0["vb"] + i) % 2] for i in range(2)]
            for k in range(DC):
                w = unit(UNIT0["vb"] + k // 2)[:, (k % 2) * 512:(k % 2 + 1) * 512]
                for tt in range(NT):
                    last = mm(vb_banks[tt][:, 0:512], hT[:, k, tt * P:(tt + 1) * P], w, start=(k == 0), stop=(k == DC - 1))
                if k % 2:
                    last.then_inc(unit_done, 1)
            sumsq(N_CQ)
            pe.wait_ge(s_in["wkr"], 16)
            for k in range(DC):
                last = mm(QB[0:2 * ROPE, 0:T], wkr[:, k, :], hT[:, k, :], start=(k == 0), stop=(k == DC - 1))
            last.then_inc(kr_mm, 1)
            sumsq(N_CKV2)
            kept(pe, "kb", 1)
            for i in range(4):
                if i >= 2:
                    pe.wait_ge(rotated, i - 1)
                src = (qb if i < 2 else kb)[:, (i % 2) * 2:(i % 2) * 2 + 2, :]
                mm(LB[i % 2][:, :], C("swap", P), src, start=True, stop=True).then_inc(swap_mm, 1)
            pe.wait_ge(normed, NM0[N_CQ] + 6)
            for h in range(H2):
                chunk("uq", h, cqT, kc=QC)
            pe.wait_ge(normed, NM0[N_CKV2] + 2)
            w = unit(UNIT0["ukvk"])
            for m in range(4):
                bank = open_bank("ukvk", m // 2) if m % 2 == 0 else DB[(FILL0["ukvk"] + m // 2) % 2]
                for k in range(KC):
                    last = mm(bank[:, (m % 2) * T:(m % 2 + 1) * T], w[:, (m * KC + k) * P:(m * KC + k + 1) * P],
                              ckT[:, k, :], start=(k == 0), stop=(k == KC - 1))
            last.then_inc(unit_done, 1)
            w = unit(UNIT0["ukvv"])
            for tt in range(NT):
                bank = open_bank("ukvv", tt)
                for k in range(KC):
                    last = mm(bank[:, 0:512], ckT[:, k, tt * P:(tt + 1) * P], w[:, k * 512:(k + 1) * 512],
                              start=(k == 0), stop=(k == KC - 1))
            last.then_inc(unit_done, 1)

            todo = [("gates", c) for c in range(16)]
            pe.wait_ge(rotated, 4)
            kept(pe, "vb", 1)
            for i in range(2 * H2 + 1):
                a = H1 + i
                if i < H2:
                    lo = HD2 * (i % 2)
                    scores(a, lambda tt: qb[lo:lo + HD2, i // 2, tt * P:(tt + 1) * P],
                           lambda n: kb[lo:lo + HD2, i // 2, 0:n])
                elif i < 2 * H2:
                    j = i - H2
                    if j == 0:
                        kept(pe, "uq", 3)
                        kept(pe, "ukvk", 1)
                        kept(pe, "ukvv", 1)
                        pe.wait_ge(kr_ready, 1)
                    scores(a, lambda tt: qh[0:HD2 + ROPE, j, tt * P:(tt + 1) * P], lambda n: kh[0:HD2 + ROPE, j, 0:n])
                if i >= 1:
                    transposes(a - 1)
                if todo:
                    chunk(*todo.pop(0), hT)
                if i >= 1:
                    j, v = ((i - 1) % H2), (vb if i - 1 < H2 else vh)
                    if (i - 1) % 2 == 0:
                        pe.wait_ge(o_ready, 8 + (i - 1) // 2)
                        pe.wait_ge(rooted, N_CKV2 + 1)
                    lo = HD2 * (j % 2)
                    pv(a - 1, UB[lo:lo + HD2], lambda s: v[:, s, j * HD2:(j + 1) * HD2]).then_inc(o_mm, 1)
            pe.wait_ge(o_ready, 16)

            def half_chunks(stage, src):
                for i in range(4):
                    bank, w = open_bank(stage, i), unit(UNIT0[stage] + i)
                    for m in range(2):
                        for k in range(4):
                            last = mm(bank[:, m * T:(m + 1) * T], w[:, (m * 4 + k) * P:(m * 4 + k + 1) * P],
                                      src[:, k, :], start=(k == 0), stop=(k == 3))
                    last.then_inc(unit_done, 1)

            half_chunks("omla", oA)
            half_chunks("omoba", oB)
            pe.wait_ge(mixed, 8)
            for c in range(8):
                chunk("out2", c, tg2[:, 8:16, :])
            sumsq(N_FFN)

            pe.wait_ge(s_in["wrt"], 16)
            pe.wait_ge(s_in["brt"], 16)
            pe.wait_ge(normed, NM0[N_FFN] + 8)
            for tt in range(NT):
                for k in range(DC):
                    mm(QB[:, tt * 64:tt * 64 + NG + NE], hT[:, k, tt * P:(tt + 1) * P], wrt[:, k, :],
                       start=(k == 0), stop=False)
                last = mm(QB[:, tt * 64:tt * 64 + NG + NE], ones[0:1, :], brt[0:1, :], start=False, stop=True)
            last.then_inc(rlog_mm, 1)
            for n in range(4):
                tt, half = n // 2, n % 2
                if n >= 2:
                    pe.wait_ge(htok_ready, n - 1)
                for c in range(4):
                    last = nc.tensor.transpose(LB[n % 2][:, c * P:(c + 1) * P],
                                               hT[:, half * 4 + c, tt * P:(tt + 1) * P], ident)
                last.then_inc(htok_mm, 1)
            pe.wait_ge(onehot, 2)
            A = rt[:, 0:64].rearrange("p (a b) -> p a b", a=2)
            before = C("before", P)
            mm(OB[:, 0:NE], before, A[:, 0, :], start=True, stop=True)
            mm(OB[:, NE:2 * NE], ones, A[:, 0, :], start=True, stop=False)
            mm(OB[:, NE:2 * NE], before, A[:, 1, :], start=False, stop=True)
            mm(OB[:, 2 * NE:3 * NE], ones, A[:, 0, :], start=True, stop=False)
            mm(OB[:, 2 * NE:3 * NE], ones, A[:, 1, :], start=False, stop=True).then_inc(cnt_mm, 1)
            pe.wait_ge(selected, 2)
            pe.wait_ge(htok_ready, 4)
            for c in range(DC):
                if c >= 2:
                    pe.wait_ge((xs_ready, xs_ready2)[c % 2], c // 2)
                elif c == 0:
                    kept(pe, "out2", 3)
                for tt in range(NT):
                    last = mm(DB[c % 2][:, :], htok[:, tt, c * P:(c + 1) * P], sel[:, tt, :],
                              start=(tt == 0), stop=(tt == NT - 1))
                last.then_inc(xs_mm, 1)
            for s2 in range(2):
                for b in range(4):
                    s, tt = s2 * 2 + b // 2, b % 2
                    last = nc.tensor.transpose(LB[s2][:, b * P:(b + 1) * P], sw[:, tt, s * P:(s + 1) * P], ident)
                last.then_inc(swt_mm, 1)

            pe.wait_ge(offs, 1)
            pe.wait_ge(swt_ready, 2)

            def gate_up(it, c, release=None):
                b = c % 2
                gu = expert_banks(b)[0]
                for h in range(2):
                    w = expert_panel(pe, it, c, h).rearrange("p (m k f) -> p m k f", m=2, k=4)
                    for k in range(4):
                        for m in range(2):
                            last = mm(gu[m * WIN:(m + 1) * WIN, 0:FF], xe[:, b, h * 4 + k, :], w[:, m, k, :],
                                      start=(h + k == 0), stop=(h * 4 + k == DC - 1))
                            if release and h + k + m == 0:
                                last.then_inc(panel_used, release)
                last.then_inc(gu_done, 1)

            def act_transposes(c, release):
                b = c % 2
                for k in range(2):
                    last = nc.tensor.transpose(expert_banks(b)[1][:, k * P:(k + 1) * P],
                                               th[:, b, FF + k * P:FF + (k + 1) * P], ident)
                    if k == 0 and release:
                        last.then_inc(panel_used, release)
                last.then_inc(at_mm, 1)

            def down(it, c):
                b = c % 2
                w = expert_panel(pe, it, c, 5).rearrange("p (k h f) -> p k h f", k=2, h=2)
                for k in range(2):
                    for h in range(2):
                        last = mm(expert_banks(b)[2][h * WIN:(h + 1) * WIN, :], actT[:, b, k, :], w[:, k, h, :],
                                  start=(k == 0), stop=(k == 1))
                last.then_inc(y_mm, 1)

            def out_transposes(c):
                b = c % 2
                for q in range(4):
                    last = nc.tensor.transpose(expert_banks(b)[3][:, q * P:(q + 1) * P],
                                               ye[:, b, q * P:(q + 1) * P], ident)
                last.then_inc(yt_mm, 1)

            def gate_up_step(it, c):
                since(pe, xe_ready, it, c)
                since(pe, act_ready, it, c - 2)
                first = it is None and c < 2
                gate_up(it, c, release=(3 if c else None) if first else 1)

            def expert_step(it, c):
                if it is not None or c < NE - 1:
                    gate_up_step(it, c + 1)
                since(pe, act_ready, it, c)
                since(pe, at_ready, it, c - 2)
                act_transposes(c, 2)
                since(pe, at_ready, it, c)
                since(pe, ye_ready, it, c - 2)
                down(it, c)
                if it is not None or c:
                    since(pe, ye_ready, it, c - 1)
                    since(pe, ys_done, it, c - 3)
                    out_transposes(c - 1)

            crowded = pe.value_load(rt[0:1, 544:545].bitcast(I32), min_val=0, max_val=1)
            with pe.If(crowded):
                with pe.Fori(0, NE // 2) as it:
                    for c in range(2):
                        for j in range(WINDOWS):
                            w = it * (2 * WINDOWS) + (c * WINDOWS + j + 1)
                            pe.wait_ge(xe_ready, w)
                            gate_up(it, c)
                            pe.wait_ge(act_ready, w)
                            act_transposes(c, 3 if j == WINDOWS - 1 else None)
                            pe.wait_ge(at_ready, w)
                            down(it, c)
                            pe.wait_ge(ye_ready, w)
                            out_transposes(c)
                            pe.wait_ge(ys_done, w)
            with pe.Else():
                gate_up_step(None, 0)
                expert_steps(pe, expert_step)
                since(pe, ye_ready, None, NE - 1)
                since(pe, ys_done, None, NE - 3)
                out_transposes(NE - 1)
                pe.wait_ge(ys_done, NE)
            for n in range(8):
                s, half = n // 2, n % 2
                if n >= 2:
                    pe.wait_ge((ysm_ready, ysm_ready2)[n % 2], n // 2)
                for c in range(4):
                    last = nc.tensor.transpose(LB[n % 2][:, c * P:(c + 1) * P],
                                               ys[:, half * 4 + c, s * P:(s + 1) * P], ident)
                last.then_inc(ysm_mm, 1)
            pe.wait_ge(ysm_ready, 4)
            pe.wait_ge(ysm_ready2, 4)
            for c in range(DC):
                if c % 2 == 0 and c >= 4:
                    pe.wait_ge(comb, c // 2 - 1)
                for s in range(SLOTS // P):
                    last = mm(DB[(c // 2) % 2][:, (c % 2) * T:(c % 2 + 1) * T], ysm[:, s, c * P:(c + 1) * P],
                              SWT[:, s, :], start=(s == 0), stop=(s == SLOTS // P - 1))
                if c % 2:
                    last.then_inc(comb_mm, 1)
            sumsq(N_OUT)

        @block.scalar
        def _(act):
            A_ = nc.scalar.activation

            def squares(n, src):
                nch = NORMS[n][0]
                if n:
                    act.wait_ge(ssq, n)
                for c in range(0, nch, 2):
                    w = min(2, nch - c)
                    A_(scr[:, c:c + w, :], src(c, w), ACT.Square).then_inc(sq, 1)

            def rootmean(n):
                act.wait_ge(ssq, n + 1)
                if n:
                    act.wait_ge(rinvd, n)
                act.wait_ge(vstep, 1)
                A_(root[:], UB[:, 0:T], ACT.Sqrt, bias=sp[:, 9, 0:1], scale=1.0 / NORMS[n][1]).then_inc(rooted, 1)

            act.wait_ge(s_in["x"], 16)
            squares(N_X, lambda c, w: xT[:, c:c + w, :])
            rootmean(N_X)
            act.wait_ge(sp_step, 2)
            A_(sp[:, 2, :], sp[:, 1, :], ACT.Exp, scale=-1.0).then_inc(sp_act, 1)
            act.wait_ge(sp_step, 3)
            A_(sp[:, 4, :], sp[:, 3, :], ACT.Ln).then_inc(sp_act, 1)
            bank = filled(act, "ckv_kidx", 0)
            A_(zc, bank[:, :].rearrange("p (a b) -> p a b", a=2), ACT.Copy).then_inc(rel["act"], 1)
            act.wait_ge(rel["act"], 1)
            squares(N_CKV, lambda c, w: zc[:, 0:1, :])
            rootmean(N_CKV)
            act.wait_ge(centered, 1)
            squares(N_KIDX, lambda c, w: zc[:, 1:2, :])
            act.wait_ge(widx_mm, 1)
            A_(widx, QB[:, 0:2 * IDXH].rearrange("p (a b) -> p a b", a=2), ACT.Copy,
               scale=float(IDXH ** -0.5)).then_inc(widx_ready, 1)
            rootmean(N_KIDX)
            for i in range(2):
                bank = filled(act, "qidx", i)
                A_(qi[:, 2 * i:2 * i + 2, :], bank[:, :].rearrange("p (a b) -> p a b", a=2), ACT.Copy,
                   scale=float(IDXD ** -0.5)).then_inc(rel["act"], 1)

            def conv_in(i):
                bank = filled(act, "xrnn", i)
                A_(xr[:, 2 * i:2 * i + 2, CONV:CONV + T], bank[:, :].rearrange("p (a b) -> p a b", a=2),
                   ACT.Copy).then_inc(rel["act"], 1)

            for j in range(IDXH):
                act.wait_ge(idx_mm, j + 1)
                if j >= 2:
                    act.wait_ge(idx_acc, j - 1)
                A_(S[:, j % 2, :], LB[j % 2][:, 0:CAUSAL], ACT.Relu).then_inc(idx_relu, 1)
            conv_in(0)
            act.wait_ge(ctok_mm, 1)
            A_(ctok, OB[:, 256:512].rearrange("p (a b) -> p a b", a=2), ACT.Copy).then_inc(ctok_ready, 1)
            for i in range(1, 4):
                conv_in(i)
            for i in range(4):
                bank = filled(act, "q", i)
                A_(qT[:, 2 * i:2 * i + 2, :], bank[:, :].rearrange("p (a b) -> p a b", a=2), ACT.Copy,
                   scale=float(HD1 ** -0.5)).then_inc(rel["act"], 1)
            for c in range(8):
                act.wait_ge(gate_mm, c + 1)
                A_(ra[:, c, :], LB[c % 2][:, 0:T], ACT.Tanh, bias=halfb[:, 16 + c:17 + c], scale=0.5)
                A_(ib[:, c, :], LB[c % 2][:, T:2 * T], ACT.Tanh, bias=halfb[:, 24 + c:25 + c],
                   scale=0.5).then_inc(gates, 1)
            act.wait_ge(gates, 8)
            act.wait_ge(sp_ready, 1)
            act.wait_ge(conv_done, 8)
            for c in range(8):
                A_(la[:, c, :], ra[:, c, :], ACT.Exp, bias=sp[:, 8, c:c + 1], scale=sp[:, 8, c:c + 1]).then_inc(decay, 1)
                act.wait_ge(decay, 2 * c + 1)
                A_(ra[:, c, :], ra[:, c, :], ACT.Tanh, bias=sp[:, 7, c:c + 1], scale=sp[:, 7, c:c + 1]).then_inc(decay, 1)
            act.wait_ge(ssq, 3)
            for i in range(4):
                A_(scr[:, 2 * i:2 * i + 2, :], la[:, 2 * i:2 * i + 2, :], ACT.Square).then_inc(sq_a, 1)
            def exps(a):
                act.wait_ge(maxed, a + 1)
                if a >= 2:
                    act.wait_ge(pt_mm, a - 1)
                for tt in range(NT):
                    c0, n = (0, P) if tt == 0 else (P, T)
                    last = A_(E[:, a % 2, c0:c0 + n], S[:, a % 2, c0:c0 + n], ACT.Exp,
                              bias=stat[:, a % 2, 0, tt:tt + 1], accum_out=stat[:, a % 2, 1, tt:tt + 1])
                last.then_inc(expd, 1)

            def ptcopy(a):
                act.wait_ge(pt_mm, a + 1)
                if a >= 2 and a <= H1:
                    act.wait_ge(pv_mm, a - 1)
                elif a > H1:
                    act.wait_ge(o_mm, a - 1)
                A_(PT[:, a % 2, :], TB[:, 0:CAUSAL], ACT.Copy).then_inc(pt_ready, 1)

            def half_tanh(f, stage, i):
                bank = filled(act, stage, i)
                if f >= 2:
                    act.wait_ge(rel["dve"], f - 1)
                A_(th[:, f % 2, :], bank[:, :], ACT.Tanh, scale=0.5).then_inc(tanhd, 1)

            def merge_gate(i):
                bank = filled(act, "merge", i)
                if i == 0:
                    act.wait_ge(gate_mm, 8)
                for m in range(2):
                    c = 2 * i + m
                    last = A_(tm[:, c, :], bank[:, m * T:(m + 1) * T], ACT.Tanh, bias=halfb[:, c:c + 1], scale=0.5)
                last.then_inc(rel["act"], 1)

            for i in range(H1 + 2):
                if i < H1:
                    act.wait_ge(qlat_mm, i + 1)
                    if i >= 2:
                        act.wait_ge(logits, i - 1)
                    A_(qlat[:, i % 2, :], QB[:, 0:T], ACT.Copy).then_inc(qlat_ready, 1)
                if 1 <= i <= H1:
                    ptcopy(i - 1)
                if i < H1:
                    exps(i)
                    if i == 1:
                        act.wait_ge(m_ready, 1)
                        A_(scr[:], scr[:], ACT.Sqrt).then_inc(rt_m, 1)
                    if i < 8:
                        half_tanh(i, "gattn" if i < 4 else "grnn", i % 4)
                    else:
                        merge_gate(i - 8)
            squares(N_FIN1, x1_src(act, "out1"))
            rootmean(N_FIN1)
            act.wait_ge(normed, NM0[N_FIN1] + 8)
            squares(N_ATT2, lambda c, w: xT[:, c:c + w, :])
            rootmean(N_ATT2)

            def keep(stage, i, dst, n=2):
                bank = filled(act, stage, i)
                A_(dst, bank[:, :].rearrange("p (a b) -> p a b", a=n), ACT.Copy).then_inc(rel["act"], 1)

            act.wait_ge(unit_done, UNITS_AT[FILL0["aproj"] + 3])
            for i in range(3):
                keep("cq", i, cqT[:, 2 * i:2 * i + 2, :])
            keep("ckv2", 0, ckT)
            for i in range(2):
                keep("qb", i, qb[:, 2 * i:2 * i + 2, :])
            act.wait_ge(rel["act"], RELEASED[FILL0["ckv2"]])
            squares(N_CQ, lambda c, w: cqT[:, c:c + w, :])
            for i in range(2):
                keep("kb", i, kb[:, 2 * i:2 * i + 2, :])
            rootmean(N_CQ)
            squares(N_CKV2, lambda c, w: ckT)
            rootmean(N_CKV2)
            for i in range(2):
                bank = filled(act, "vb", i)
                A_(vb[:, i, :], bank[:, :], ACT.Copy).then_inc(rel["act"], 1)
            for i in range(2):
                bank = filled(act, "ukvk", i)
                v = bank[:, :].rearrange("p (a b) -> p a b", a=2)
                A_(kh[0:64, 4 * i:4 * i + 4:2, :], v[0:64], ACT.Copy)
                A_(kh[0:64, 4 * i + 1:4 * i + 4:2, :], v[64:128], ACT.Copy).then_inc(rel["act"], 1)
            for i in range(2):
                bank = filled(act, "ukvv", i)
                A_(vh[:, i, :], bank[:, :], ACT.Copy).then_inc(rel["act"], 1)
            for i in range(2 * H2 + 1):
                a = H1 + i
                if i >= 1:
                    ptcopy(a - 1)
                if i < 2 * H2:
                    exps(a)
                    if i % 2:
                        g = i // 2
                        bank = filled(act, "gates", g)
                        A_(tg2[:, 2 * g:2 * g + 2, :], bank[:, :].rearrange("p (a b) -> p a b", a=2), ACT.Tanh,
                           scale=0.5).then_inc(rel["act"], 1)
            squares(N_FFN, x1_src(act, "out2"))
            rootmean(N_FFN)
            act.wait_ge(rlog_mm, 1)
            lg = rt[:, 64:192].rearrange("p (a b) -> p a b", a=2)
            A_(lg[:, :, 0:NG + NE], QB[:, 0:128].rearrange("p (a b) -> p a b", a=2)[:, :, 0:NG + NE],
               ACT.Copy).then_inc(rlog, 1)
            for n in range(4):
                act.wait_ge(htok_mm, n + 1)
                A_(htok[:, n // 2, (n % 2) * 512:(n % 2 + 1) * 512], LB[n % 2][:, :], ACT.Copy).then_inc(htok_ready, 1)
            for tt in range(NT):
                act.wait_ge(gate_neg, tt + 1)
                A_(rt[:, 256 + 8 * tt:260 + 8 * tt], lg[:, tt, 0:NG], ACT.Exp, bias=rt[:, 272 + tt:273 + tt],
                   accum_out=rt[:, 274 + tt:275 + tt]).then_inc(expg, 1)
            act.wait_ge(topd, 2)
            A_(rt[:, 278:280], rt[:, 276:278], ACT.Exp).then_inc(expt, 1)
            for c in range(0, DC, 2):
                act.wait_ge(xs_mm, c + 1)
                A_(xs[:, c, 0:SLOTS], DB[0][:, :], ACT.Copy).then_inc(xs_ready, 1)
            for s2 in range(2):
                act.wait_ge(swt_mm, s2 + 1)
                A_(SWT[:, 2 * s2:2 * s2 + 2, :], LB[s2][:, :].rearrange("p (a b) -> p a b", a=2),
                   ACT.Copy).then_inc(swt_ready, 1)
            act.wait_ge(offs, 1)

            def gate_tanh(c):
                b = c % 2
                A_(th[0:WIN, b, 0:FF], expert_banks(b)[0][0:WIN, 0:FF], ACT.Tanh, scale=0.5).then_inc(gate_t, 1)

            def act_t(c):
                b = c % 2
                A_(actT[:, b], expert_banks(b)[1][:, 0:2 * P].rearrange("p (a b) -> p a b", a=2)[:, :, 0:WIN],
                   ACT.Copy).then_inc(at_ready, 1)

            def down_keep(c):
                b = c % 2
                A_(ye[:, b, :], expert_banks(b)[2][:, :], ACT.Copy).then_inc(ye_ready, 1)

            def expert_step(it, c):
                if it is not None or c < NE - 1:
                    since(act, gu_done, it, c + 1)
                    since(act, act_ready, it, c - 1)
                    gate_tanh(c + 1)
                since(act, at_mm, it, c)
                since(act, y_mm, it, c - 2)
                act_t(c)
                since(act, y_mm, it, c)
                since(act, yt_mm, it, c - 2)
                down_keep(c)

            crowded = act.value_load(rt[0:1, 544:545].bitcast(I32), min_val=0, max_val=1)
            with act.If(crowded):
                with act.Fori(0, NE // 2) as it:
                    for c in range(2):
                        for j in range(WINDOWS):
                            w = it * (2 * WINDOWS) + (c * WINDOWS + j + 1)
                            act.wait_ge(gu_done, w)
                            gate_tanh(c)
                            act.wait_ge(at_mm, w)
                            act_t(c)
                            act.wait_ge(y_mm, w)
                            down_keep(c)
            with act.Else():
                since(act, gu_done, None, 0)
                gate_tanh(0)
                expert_steps(act, expert_step)
            for n in range(0, 8, 2):
                act.wait_ge(ysm_mm, n + 1)
                A_(ysm[:, n // 2, 0:512], L0[:, :], ACT.Copy).then_inc(ysm_ready, 1)
            squares(N_OUT, x3_src(act))
            rootmean(N_OUT)

        @block.gpsimd
        def _(pool):
            g = nc.gpsimd
            pool.wait_ge(offs, 1)
            pool.wait_ge(xs_ready, 4)
            pool.wait_ge(xs_ready2, 4)
            pool.wait_ge(padz, 1)

            def stage(c, off):
                g.tensor_copy(xe[:, c % 2], xs[:, :, bass.ds(off, WIN)]).then_inc(xe_ready, 1)

            def stage_step(it, c):
                off = window_offset(pool, (0 if it is None else it * (2 * WINDOWS)) + c * WINDOWS)
                since(pool, gu_done, it, c - 2)
                stage(c, off)

            crowded = pool.value_load(rt[0:1, 544:545].bitcast(I32), min_val=0, max_val=1)
            with pool.If(crowded):
                with pool.Fori(0, NE // 2) as it:
                    for c in range(2):
                        for j in range(WINDOWS):
                            n = c * WINDOWS + j
                            stage(c, window_offset(pool, it * (2 * WINDOWS) + n))
                            pool.wait_ge(gu_done, it * (2 * WINDOWS) + (n + 1))
            with pool.Else():
                expert_steps(pool, stage_step)

        @block.vector
        def _(dve):
            v = nc.vector
            count = [0]

            def step(ins):
                count[0] += 1
                ins.then_inc(vstep, 1)
                dve.wait_ge(vstep, count[0])

            def stt(out_, in0, scalar, in1, op0=ALU.mult, op1=ALU.mult):
                return v.scalar_tensor_tensor(out=out_, in0=in0, scalar=scalar, in1=in1, op0=op0, op1=op1)

            def norm(n, src, dst, gain):
                nch = NORMS[n][0]
                dve.wait_ge(rooted, n + 1)
                if n:
                    dve.wait_ge(normed, NM0[n])
                v.reciprocal(rinv[:], root[:]).then_inc(rinvd, 1)
                dve.wait_ge(rinvd, n + 1)
                for c in range(nch):
                    stt(dst(c), src(c), V(gain, c), rinv[:]).then_inc(normed, 1)

            step(v.memset(sp[:, 9, :], EPS))
            dve.wait_ge(s_in["vec"], 16)
            dve.wait_ge(s_in["x"], 16)
            norm(N_X, lambda c: xT[:, c, :], lambda c: hT[:, c, :], "norm_gain")
            v.memset(xr[:, :, 0:CONV], 0.0).then_inc(padded, 1)
            step(v.tensor_scalar(halfb[:], V("b_merge", 0, 32), 0.5, None, ALU.mult))
            v.tensor_scalar(sp[:, 0, :], V("lru_lambda", 0, 8), -1.0, None, ALU.mult).then_inc(sp_step, 1)
            dve.wait_ge(sp_step, 1)
            v.tensor_tensor(sp[:, 1, :], sp[:, 0, :], V("lru_lambda", 0, 8), ALU.max).then_inc(sp_step, 1)
            dve.wait_ge(sp_act, 1)
            v.tensor_scalar(sp[:, 3, :], sp[:, 2, :], 1.0, None, ALU.add).then_inc(sp_step, 1)
            dve.wait_ge(sp_step, 3)
            step(v.tensor_scalar(sp[:, 5, :], sp[:, 3, :], 1.0, None, ALU.is_equal))
            step(stt(sp[:, 6, :], sp[:, 3, :], -1.0, sp[:, 5, :], ALU.add, ALU.add))
            step(v.reciprocal(sp[:, 7, :], sp[:, 6, :]))
            dve.wait_ge(sp_act, 2)
            step(v.tensor_tensor(sp[:, 6, :], sp[:, 4, :], sp[:, 5, :], ALU.add))
            step(v.tensor_tensor(sp[:, 6, :], sp[:, 6, :], sp[:, 2, :], ALU.mult))
            step(v.tensor_tensor(sp[:, 6, :], sp[:, 6, :], sp[:, 7, :], ALU.mult))
            step(stt(sp[:, 6, :], sp[:, 0, :], 0.0, sp[:, 6, :], ALU.max, ALU.add))
            step(v.tensor_scalar(sp[:, 7, :], sp[:, 6, :], LRU_C / 2, None, ALU.mult))
            v.tensor_scalar(sp[:, 8, :], sp[:, 6, :], -LRU_C / 2, None, ALU.mult).then_inc(sp_ready, 1)

            dve.wait_ge(mean_ready, 1)
            v.tensor_tensor(zc[:, 1, :], zc[:, 1, :], OB[:, 0:T], ALU.subtract).then_inc(centered, 1)
            norm(N_CKV, lambda c: zc[:, 0, :], lambda c: cT, "kv_norm_gain")
            dve.wait_ge(centered, 1)
            norm(N_KIDX, lambda c: zc[:, 1, :], lambda c: kiT, "idx_ln_gain")
            dve.wait_ge(normed, NM0[N_KIDX] + 1)
            v.tensor_scalar(kiT, kiT, V("idx_ln_bias"), None, ALU.add).then_inc(kidx_ready, 1)
            dve.wait_ge(widx_ready, 1)
            dve.wait_ge(s_in["cst"], 16)
            tiles = [(0, P), (P, T)]
            for j in range(IDXH):
                dve.wait_ge(idx_relu, j + 1)
                if j:
                    dve.wait_ge(idx_acc, j)
                for tt, (c0, n) in enumerate(tiles):
                    acc = score[:, c0:c0 + n]
                    last = stt(acc, S[:, j % 2, c0:c0 + n], widx[:, tt, j:j + 1],
                               acc if j else C("causal", n, c0), ALU.mult, ALU.add)
                last.then_inc(idx_acc, 1)
            dve.wait_ge(idx_acc, IDXH)
            for tt, (c0, n) in enumerate(tiles):
                s = score[:, c0:c0 + n]
                for r in range(TOPK // 8):
                    step(v.max(out=top8[:, tt, :], in_=s))
                    step(v.match_replace(out=s, in_to_replace=top8[:, tt, :], in_values=s, imm_value=TAKEN))
            step(v.tensor_scalar(score, score, TAKEN / 2, -BIG, ALU.is_gt, ALU.mult))
            v.tensor_tensor(Dm, score, C("dist", CAUSAL), ALU.add).then_inc(mask_ready, 1)
            dve.wait_ge(padded, 1)
            for c in range(8):
                kept(dve, "xrnn", c // 2)
                step(v.tensor_scalar(u[:, c, :], xr[:, c, 4:4 + T], V("conv_w", 3 * 8 + c), V("conv_b", c),
                                     ALU.mult, ALU.add))
                for t in (2, 1, 0):
                    ins = stt(u[:, c, :], xr[:, c, 1 + t:1 + t + T], V("conv_w", t * 8 + c), u[:, c, :],
                              ALU.mult, ALU.add)
                    if t:
                        step(ins)
                ins.then_inc(conv_done, 1)

            def bias_max(a):
                kind = 0 if a < H1 else 1
                dve.wait_ge(logits, a + 1)
                if a >= 2:
                    dve.wait_ge(expd, a - 1)
                sa = S[:, a % 2, :]
                if kind == 0:
                    ins = stt(sa, Dm, float(2.0 ** (-8.0 * (a + 1) / H1)), LB[a % 2][:, 0:CAUSAL], ALU.mult, ALU.add)
                else:
                    ins = stt(sa, LB[a % 2][:, 0:CAUSAL], MOBA_SCALE if a < H1 + H2 else MLA_SCALE,
                              C("causal", CAUSAL), ALU.mult, ALU.add)
                ins.then_inc(biased, 1)
                dve.wait_ge(biased, a + 1)
                for tt, (c0, n) in enumerate(tiles):
                    last = v.reduce_max(stat[:, a % 2, 0, tt:tt + 1], S[:, a % 2, c0:c0 + n], axis=AX.X, negate=True)
                last.then_inc(maxed, 1)

            def normalise(a):
                dve.wait_ge(expd, a + 1)
                step(v.reciprocal(stat[:, a % 2, 2, :], stat[:, a % 2, 1, :]))
                for tt, (c0, n) in enumerate(tiles):
                    last = v.tensor_scalar(E[:, a % 2, c0:c0 + n], E[:, a % 2, c0:c0 + n],
                                           stat[:, a % 2, 2, tt:tt + 1], None, ALU.mult)
                last.then_inc(probs, 1)

            def silu2(f, stage, i, dst):
                bank = DB[(FILL0[stage] + i) % 2]
                dve.wait_ge(tanhd, f + 1)
                stt(dst[:, 2 * i:2 * i + 2, :], th[:, f % 2, :].rearrange("p (a b) -> p a b", a=2), 1.0,
                    bank[:, :].rearrange("p (a b) -> p a b", a=2), ALU.add, ALU.mult).then_inc(rel["dve"], 1)

            dve.wait_ge(mask_ready, 1)

            def lru(i):
                if i == 0:
                    dve.wait_ge(sq_a, 4)
                    stt(scr[:], scr[:], 1.0, ra, ALU.add, ALU.mult).then_inc(m_ready, 1)
                elif i == 1:
                    step(stt(ib, ib, 1.0, u, ALU.add, ALU.mult))
                elif i == 2:
                    dve.wait_ge(rt_m, 1)
                    step(stt(ib, scr[:], 0.5, ib))
                elif i < 7:
                    for c in range(2 * (i - 3), 2 * (i - 3) + 2):
                        last = v.tensor_tensor_scan(u[:, c, :], la[:, c, :], ib[:, c, :], 0.0, ALU.mult, ALU.add)
                    step(last)
                elif 8 <= i < 12:
                    c = 2 * (i - 8)
                    kept(dve, "grnn", i - 8)
                    stt(u[:, c:c + 2, :], u[:, c:c + 2, :], 0.5, sr[:, c:c + 2, :]).then_inc(h_ready, 1)

            for i in range(H1 + 2):
                if i < H1:
                    bias_max(i)
                    lru(i)
                    normalise(i)
                if 1 <= i <= H1:
                    a = i - 1
                    dve.wait_ge(pv_mm, a + 1)
                    if a >= 2:
                        dve.wait_ge(o_mm, a - 1)
                    v.tensor_copy(olat[:, a % 2, :], OB[:, 0:T]).then_inc(olat_ready, 1)
                if i >= 3 and i % 2:
                    m = (i - 3) // 2
                    dve.wait_ge(o_mm, 2 * m + 2)
                    kept(dve, "gattn", m // 2)
                    stt(oT[:, m, :], UB[:, 0:T], 0.5, sg[:, m, :]).then_inc(o_ready, 1)
                if i < 8:
                    silu2(i, "gattn" if i < 4 else "grnn", i % 4, sg if i < 4 else sr)

            def layer_end(proj_r, proj_a, gate_r, gate_a, out_stage, n_mixed):
                for stage, gate in ((proj_r, gate_r), (proj_a, gate_a)):
                    for i in range(4):
                        bank = filled(dve, stage, i)
                        g = gate[:, 2 * i:2 * i + 2, :]
                        stt(g, g, 1.0, bank[:, :].rearrange("p (a b) -> p a b", a=2), ALU.add,
                            ALU.mult).then_inc(rel["dve"], 1)
                        if gate is gate_a:
                            kept(dve, stage, i)
                            v.tensor_tensor(g, g, gate_r[:, 2 * i:2 * i + 2, :], ALU.add).then_inc(mixed, 1)
                for i in range(4):
                    bank = filled(dve, out_stage, i)
                    r = xT[:, 2 * i:2 * i + 2, :]
                    stt(r, bank[:, :].rearrange("p (a b) -> p a b", a=2), 0.5, r, ALU.mult,
                        ALU.add).then_inc(rel["dve"], 1)

            kept(dve, "merge", 7)
            layer_end("rproj", "aproj", tm[:, 8:16, :], tm[:, 0:8, :], "out1", 0)
            kept(dve, "out1", 3)
            norm(N_FIN1, lambda c: xT[:, c, :], lambda c: xT[:, c, :], "final_norm_gain")
            norm(N_ATT2, lambda c: xT[:, c, :], lambda c: hT[:, c, :], "attn_norm_2")

            kept(dve, "ckv2", 0)
            norm(N_CQ, lambda c: cqT[:, c, :], lambda c: cqT[:, c, :], "q_norm_2")
            dve.wait_ge(kr_mm, 1)
            step(v.tensor_tensor(rot[64:96, 0, 0:T], QB[0:32, 0:T], cst[0:32, CST["cos_mla"]:CST["cos_mla"] + T], ALU.mult))
            step(v.tensor_tensor(rot[64:96, 1, 0:T], QB[32:64, 0:T], cst[32:64, CST["sin_mla"]:CST["sin_mla"] + T], ALU.mult))
            v.tensor_tensor(kh[64:96, :, :], rot[64:96, 0:1, 0:T].to_broadcast([32, H2, T]),
                            rot[64:96, 1:2, 0:T].to_broadcast([32, H2, T]), ALU.add).then_inc(kr_ready, 1)
            norm(N_CKV2, lambda c: ckT[:, c, :], lambda c: ckT[:, c, :], "kv_norm_2")
            dve.wait_ge(kr_ready, 1)
            kept(dve, "kb", 1)
            cosb = C("cos_moba", T).unsqueeze(1).to_broadcast([P, 2, T])
            sinb = C("sin_moba", T).unsqueeze(1).to_broadcast([P, 2, T])
            for i in range(4):
                x2 = (qb if i < 2 else kb)[:, (i % 2) * 2:(i % 2) * 2 + 2, :]
                r = rot[:, 0, :].rearrange("p (a b) -> p a b", a=2)
                dve.wait_ge(swap_mm, i + 1)
                if i:
                    dve.wait_ge(rotated, i)
                step(v.tensor_tensor(r, LB[i % 2][:, :].rearrange("p (a b) -> p a b", a=2), sinb, ALU.mult))
                step(v.tensor_tensor(x2, x2, cosb, ALU.mult))
                v.tensor_tensor(x2, x2, r, ALU.add).then_inc(rotated, 1)
            dve.wait_ge(rotated, 4)
            for i in range(4):
                bank = filled(dve, "uq", i)
                if i:
                    kept(dve, "uq", i - 1)
                b3 = bank[:, :].rearrange("p (a b) -> p a b", a=2)
                h2 = slice(2 * i, 2 * i + 2)
                cosq = cst[64:96, CST["cos_mla"]:CST["cos_mla"] + T].unsqueeze(1).to_broadcast([32, 2, T])
                sinq = cst[96:128, CST["sin_mla"]:CST["sin_mla"] + T].unsqueeze(1).to_broadcast([32, 2, T])
                r = rot[64:96, :, :].rearrange("p r (a b) -> p r a b", a=2)
                v.tensor_copy(qh[0:64, h2, :], b3[0:64])
                step(v.tensor_tensor(r[:, 0], b3[64:96], cosq, ALU.mult))
                step(v.tensor_tensor(r[:, 1], b3[96:128], sinq, ALU.mult))
                v.tensor_tensor(qh[64:96, h2, :], r[:, 0], r[:, 1], ALU.add).then_inc(rel["dve"], 1)
            for i in range(2 * H2 + 1):
                a = H1 + i
                if i < 2 * H2:
                    bias_max(a)
                    normalise(a)
                if i >= 2 and i % 2 == 0:
                    m = (i - 2) // 2
                    dve.wait_ge(o_mm, H1 + 2 * m + 2)
                    dst = oB if m < 4 else oA
                    v.tensor_copy(dst[:, m % 4, :], UB[:, 0:T]).then_inc(o_ready, 1)
            kept(dve, "gates", 7)
            layer_end("omla", "omoba", tg2[:, 0:8, :], tg2[:, 8:16, :], "out2", 4)
            kept(dve, "out2", 3)
            norm(N_FFN, lambda c: xT[:, c, :], lambda c: hT[:, c, :], "ffn_norm_2")

            A = rt[:, 0:64].rearrange("p (a b) -> p a b", a=2)
            lg = rt[:, 64:192].rearrange("p (a b) -> p a b", a=2)
            iota = C("iota", SLOTS)
            gpad = rt[:, 192:208].rearrange("p (a b) -> p a b", a=2)
            m8 = rt[:, 208:216]
            i8 = rt[:, 216:224].bitcast(U32)
            f8 = rt[:, 224:232]
            oh = rt[:, 232:236]
            pen = rt[:, 236:240]
            em = rt[:, 280:312]
            negm, sums, diff, ex = rt[:, 272:274], rt[:, 274:276], rt[:, 276:278], rt[:, 278:280]
            eid = rt[:, 312:316].rearrange("p (a b) -> p a b", a=2)
            OH = rt[:, 320:448].rearrange("p (a e b) -> p a e b", a=2, e=2)
            pos = rt[:, 448:452].rearrange("p (a b) -> p a b", a=2)
            wgt = rt[:, 452:456].rearrange("p (a b) -> p a b", a=2)
            tmp = rt[:, 456:488]
            cnt, offx = rt[:, 560:592], rt[:, 592:624]
            incl = rt[:, 624:656]
            onesf = ones[:, 0:NE]
            step(v.memset(rt[:, 192:208], TAKEN))
            dve.wait_ge(rlog, 1)
            for tt in range(NT):
                step(v.tensor_copy(gpad[:, tt, 0:NG], lg[:, tt, 0:NG]))
                step(v.max(out=m8, in_=gpad[:, tt, :]))
                v.tensor_scalar(negm[:, tt:tt + 1], m8[:, 0:1], -1.0, None, ALU.mult).then_inc(gate_neg, 1)
                step(v.max_index(i8, m8, gpad[:, tt, :]))
                step(v.tensor_copy(f8, i8))
                step(v.tensor_scalar(oh, iota[:, 0:NG], f8[:, 0:1], None, ALU.is_equal))
                step(v.tensor_scalar(pen, oh, -1.0, BIG, ALU.add, ALU.mult))
                e3 = em.rearrange("p (a b) -> p a b", a=NG)
                step(v.tensor_tensor(e3, lg[:, tt, NG:NG + NE].rearrange("p (a b) -> p a b", a=NG),
                                     oh.unsqueeze(2).to_broadcast([P, NG, EPG]), ALU.mult))
                step(v.tensor_tensor(e3, e3, pen.unsqueeze(2).to_broadcast([P, NG, EPG]), ALU.add))
                step(v.max(out=m8, in_=em))
                step(v.max_index(i8, m8, em))
                step(v.tensor_copy(f8, i8))
                step(v.tensor_copy(eid[:, tt, :], f8[:, 0:2]))
                v.tensor_tensor(diff[:, tt:tt + 1], m8[:, 1:2], m8[:, 0:1], ALU.subtract).then_inc(topd, 1)
                for e in range(2):
                    step(v.tensor_scalar(OH[:, tt, e, :], iota[:, 0:NE], eid[:, tt, e:e + 1], None, ALU.is_equal))
                v.tensor_tensor(A[:, tt, :], OH[:, tt, 0, :], OH[:, tt, 1, :], ALU.add).then_inc(onehot, 1)
            dve.wait_ge(expg, 2)
            dve.wait_ge(expt, 1)
            step(v.tensor_scalar(tmp[:, 0:2], ex, 1.0, None, ALU.add))
            step(v.tensor_tensor(tmp[:, 0:2], tmp[:, 0:2], sums, ALU.mult))
            step(v.reciprocal(wgt[:, 0:2, 0:1].rearrange("p a b -> p (a b)"), tmp[:, 0:2]))
            step(v.tensor_tensor(wgt[:, :, 1:2].rearrange("p a b -> p (a b)"),
                                 wgt[:, :, 0:1].rearrange("p a b -> p (a b)"), ex, ALU.mult))
            dve.wait_ge(cnt_mm, 1)
            step(v.tensor_copy(cnt, OB[:, 2 * NE:3 * NE]))
            step(v.tensor_tensor_scan(incl, onesf, cnt, 0.0, ALU.mult, ALU.add))
            step(v.tensor_tensor(offx, incl, cnt, ALU.subtract))
            win = rt[:, 700:828].rearrange("p (e j) -> p e j", j=WINDOWS)
            step(v.tensor_tensor(win, offx.unsqueeze(2).to_broadcast([P, NE, WINDOWS]),
                                 iota[:, 0:WINDOWS * WIN:WIN].unsqueeze(1).to_broadcast([P, NE, WINDOWS]), ALU.add))
            step(v.tensor_scalar(rt[:, 700:828], rt[:, 700:828], float(SLOTS), None, ALU.min))
            step(v.tensor_copy(rt[:, 828:956].bitcast(I32), rt[:, 700:828]))
            step(v.reduce_max(tmp[:, 0:1], cnt, axis=AX.X))
            step(v.tensor_scalar(tmp[:, 0:1], tmp[:, 0:1], float(WIN), None, ALU.is_gt))
            v.tensor_copy(rt[:, 544:545].bitcast(I32), tmp[:, 0:1]).then_inc(offs, 1)
            dve.wait_ge(offs, 1)
            for tt in range(NT):
                step(v.tensor_tensor(incl, OB[:, tt * NE:(tt + 1) * NE], offx, ALU.add))
                for e in range(2):
                    step(v.tensor_tensor(tmp, incl, OH[:, tt, e, :], ALU.mult))
                    step(v.reduce_sum(pos[:, tt, e:e + 1], tmp, axis=AX.X))
                step(v.tensor_scalar(sel[:, tt, :], iota, pos[:, tt, 0:1], None, ALU.is_equal))
                step(v.tensor_scalar(sw[:, tt, :], sel[:, tt, :], wgt[:, tt, 0:1], None, ALU.mult))
                step(v.tensor_scalar(ysm[:, 3, 0:SLOTS], iota, pos[:, tt, 1:2], None, ALU.is_equal))
                step(stt(sw[:, tt, :], ysm[:, 3, 0:SLOTS], wgt[:, tt, 1:2], sw[:, tt, :], ALU.mult, ALU.add))
                v.tensor_tensor(sel[:, tt, :], sel[:, tt, :], ysm[:, 3, 0:SLOTS], ALU.add).then_inc(selected, 1)
            v.memset(xs[:, :, SLOTS:SLOTS + WIN], 0.0).then_inc(padz, 1)
            for c in range(1, DC, 2):
                dve.wait_ge(xs_mm, c + 1)
                v.tensor_copy(xs[:, c, 0:SLOTS], DB[1][:, :]).then_inc(xs_ready2, 1)

            def expert_act(it, c, w):
                b = c % 2
                gu = expert_banks(b)[0]
                t_ = th[0:WIN, b, 0:FF]
                stt(t_, t_, 1.0, gu[0:WIN, 0:FF], ALU.add, ALU.mult).then_inc(silu_e, 1)
                dve.wait_ge(silu_e, w)
                stt(th[0:WIN, b, FF:2 * FF], t_, 0.5, gu[WIN:2 * WIN, 0:FF]).then_inc(act_ready, 1)

            def out_keep(it, c, off):
                v.tensor_copy(ys[:, :, bass.ds(off, WIN)].rearrange("p (h q) s -> p h q s", h=2),
                              expert_banks(c % 2)[3][:, :].rearrange("p (q h s) -> p h q s", q=4, h=2)
                              ).then_inc(ys_done, 1)

            def expert_step(it, c):
                if it is not None or c < NE - 1:
                    since(dve, gate_t, it, c + 1)
                    since(dve, at_mm, it, c - 1)
                    expert_act(it, c + 1, (0 if it is None else it * 2) + (c + 2))
                if it is not None or c:
                    keep_step(it, c - 1)

            def keep_step(it, c):
                off = window_offset(dve, (0 if it is None else it * (2 * WINDOWS)) + c * WINDOWS)
                since(dve, yt_mm, it, c)
                since(dve, ys_done, it, c - 1)
                out_keep(it, c, off)

            dve.wait_ge(padz, 1)
            crowded = dve.value_load(rt[0:1, 544:545].bitcast(I32), min_val=0, max_val=1)
            with dve.If(crowded):
                with dve.Fori(0, NE // 2) as it:
                    for c in range(2):
                        for j in range(WINDOWS):
                            n = c * WINDOWS + j
                            w = it * (2 * WINDOWS) + (n + 1)
                            off = window_offset(dve, it * (2 * WINDOWS) + n)
                            dve.wait_ge(gate_t, w)
                            expert_act(it, c, w)
                            dve.wait_ge(yt_mm, w)
                            out_keep(it, c, off)
                            dve.wait_ge(ys_done, w)
            with dve.Else():
                since(dve, gate_t, None, 0)
                expert_act(None, 0, 1)
                expert_steps(dve, expert_step)
                keep_step(None, NE - 1)
            for n in range(1, 8, 2):
                dve.wait_ge(ysm_mm, n + 1)
                v.tensor_copy(ysm[:, n // 2, 512:1024], L1[:, :]).then_inc(ysm_ready2, 1)
            for i in range(4):
                dve.wait_ge(comb_mm, i + 1)
                r = xT[:, 2 * i:2 * i + 2, :]
                v.tensor_tensor(r, DB[i % 2][:, :].rearrange("p (a b) -> p a b", a=2), r, ALU.add).then_inc(comb, 1)
            dve.wait_ge(comb, 4)
            norm(N_OUT, lambda c: xT[:, c, :], lambda c: hT[:, c, :], "final_norm_2")



def chunks_of(w):
    k, m = w.shape
    return w.reshape(k // P, P, m // P, P).transpose(2, 1, 0, 3).reshape(m // P, P, k)


def k_major(w):
    k, m = w.shape
    return w.reshape(k // P, P, m).transpose(1, 0, 2)


def by_chunk(v):
    return v.reshape(-1, P).T


def units_of(a):
    return a.reshape(P, -1, UNIT).transpose(1, 0, 2)


def constants():
    f = np.float32
    t = np.arange(T, dtype=f)
    i = np.arange(P)
    c = {}
    c["ident"] = np.eye(P)
    c["ones"] = np.ones((P, P))
    c["mean64"] = ((i[:, None] // 64) == (i[None, :] // 64)) / 64.0
    r = i % 64
    partner = np.where(r < 8, i + 8, np.where(r < 16, i - 8, -1))
    c["swap"] = (i[:, None] == partner[None, :])
    c["before"] = i[:, None] < i[None, :]
    tok = np.concatenate([np.tile(i[:, None], (1, P)), np.tile(i[:, None] + P, (1, T))], 1)
    key = np.concatenate([np.arange(P), np.arange(T)])[None, :]
    c["causal"] = np.where(key <= tok, 0.0, -BIG)
    c["dist"] = np.where(key <= tok, -(tok - key), -BIG)

    def tables(rot):
        half = rot // 2
        inv = np.power(f(500000.0), -np.arange(half, dtype=f) / f(half)).astype(f)
        ang = (t[:, None] * inv[None, :]).astype(f)
        return np.cos(ang).T, np.sin(ang).T

    cos, sin = tables(ROPE)
    rows = i % 16
    c["cos_mla"] = cos[rows]
    c["sin_mla"] = sin[rows] * np.where(i % 32 < 16, -1.0, 1.0)[:, None]
    cos, sin = tables(MROT)
    c["cos_moba"] = np.where((r < 16)[:, None], cos[r % 8], 1.0)
    c["sin_moba"] = sin[r % 8] * np.where(r < 8, -1.0, np.where(r < 16, 1.0, 0.0))[:, None]
    c["iota"] = np.tile(np.arange(SLOTS), (P, 1))
    return np.ascontiguousarray(np.concatenate([c[n] for n in CST], 1).astype(f))


def pack(g):
    w = g["w_in"][0]
    cut = np.cumsum([0, 1024, 128, 512, 64, 8, 1024, 1024, 1024, 2048])
    q, ckv, qi, ki, wi, ga, xr, gr, mg = [w[:, a:b] for a, b in zip(cut[:-1], cut[1:])]
    w2 = g["w_in_2"][0]
    cut = np.cumsum([0, QL, KL, ROPE, 512, 512, 512, D, D])
    cq, ck, kr, qb, kb, vb, gA, gB = [w2[:, a:b] for a, b in zip(cut[:-1], cut[1:])]
    half = ROPE // 2
    uq = g["w_uq_2"][0].reshape(QL, H2, HD2 + ROPE)
    uq = np.concatenate([uq, uq[:, :, HD2 + half:], uq[:, :, HD2:HD2 + half]], 2)
    uqu = np.pad(chunks_of(uq.reshape(QL, H2 * P)), ((0, 0), (0, 0), (0, UNIT - QL)))
    ukv = g["w_ukv_2"][0].reshape(KL, H2, 2 * HD2)
    uk = chunks_of(ukv[:, :, :HD2].reshape(KL, 512)).transpose(1, 0, 2).reshape(P, UNIT)
    uv = k_major(ukv[:, :, HD2:].reshape(KL, 512)).reshape(P, UNIT)
    parts = [chunks_of(a) for a in (np.concatenate([ckv, ki, ki], 1), qi, xr, q, ga, gr, mg,
                                    g["w_rnn_proj"][0], g["w_attn_proj"][0], g["w_out"][0], cq, ck, qb, kb)]
    parts.append(units_of(k_major(vb).reshape(P, 4 * UNIT)))
    parts += [uqu, uk[None], uv[None], chunks_of(np.concatenate([gA, gB], 1))]
    for name in ("w_o_mla_2", "w_o_moba_2"):
        parts.append(units_of(chunks_of(g[name][0]).transpose(1, 0, 2).reshape(P, 4 * UNIT)))
    parts.append(chunks_of(g["w_out_2"][0]))
    dense = np.concatenate(parts, 0)
    dense = dense.reshape(-1, 2, P, UNIT).transpose(0, 2, 1, 3).reshape(-1, P, 2 * UNIT)
    gate, up, down = (g[n][0] for n in ("w_exp_gate_2", "w_exp_up_2", "w_exp_down_2"))
    gu = np.stack([gate, up], 1).reshape(NE, 2, 2, 4, P, FF).transpose(0, 2, 4, 1, 3, 5).reshape(NE, 2, P, 2 * UNIT)
    dn = down.reshape(NE, 2, P, D).transpose(0, 2, 1, 3).reshape(NE, P, 2 * UNIT)
    order = [gu[0, 0], gu[0, 1]]
    for e in range(NE - 1):
        order += [gu[e + 1, 0], gu[e + 1, 1], dn[e]]
    expert = np.stack(order + [dn[NE - 1]])
    idx2 = lambda a: np.concatenate([a, a])
    cols = {"conv_w": g["conv_w"][0].reshape(CONV * 8, P).T, "idx_ln_gain": idx2(g["idx_ln_gain"][0])[:, None],
            "idx_ln_bias": idx2(g["idx_ln_bias"][0])[:, None], "final_norm_gain": by_chunk(g["final_norm_gain"]),
            "final_norm_2": by_chunk(g["final_norm_2"])}
    vecs = np.concatenate([cols[n] if n in cols else by_chunk(g[n][0]) for n in VEC], 1)
    rg = np.zeros((P, 2, 8, P), np.float32)
    for n, name in enumerate(("w_rg_a", "w_rg_x")):
        b = g[name][0].reshape(8, 2, 64, 64)
        for s in range(2):
            rg[64 * s:64 * s + 64, n, :, 64 * s:64 * s + 64] = b[:, s].transpose(1, 0, 2)
    wuk = g["w_uk"][0].reshape(8, 2, LAT, HD1).transpose(1, 3, 0, 2).reshape(P, 8 * LAT)
    wuv = g["w_uv"][0].transpose(1, 0, 2).reshape(LAT, H1 * HD1)
    wkr = k_major(np.concatenate([kr, kr[:, half:], kr[:, :half]], 1)).reshape(P, -1)
    wre = g["w_router_expert_2"][0].transpose(1, 0, 2).reshape(D, NE)
    wrt = k_major(np.concatenate([g["w_router_group_2"][0], wre], 1)).reshape(P, -1)
    brt = np.concatenate([g["b_router_group_2"][0], g["b_router_expert_2"][0].reshape(-1)])[None, :]
    x_t = g["x"][0].T.reshape(DC, P, T).transpose(1, 0, 2).reshape(P, DC * T)
    arrays = dict(x_t=x_t, vecs=vecs, consts=constants(), w_widx=k_major(wi).reshape(P, -1),
                  w_rg=rg.reshape(P, -1), w_uk=wuk, w_uv=wuv, w_kr=wkr, w_router=wrt, b_router=brt,
                  w_dense=dense, w_expert=expert)
    return {k: np.ascontiguousarray(v) for k, v in arrays.items()}


def kernel(**inputs):
    import concourse.bacc as bacc
    from concourse.bass_utils import run_bass_kernel_spmd

    arrays = pack({k: np.asarray(v) for k, v in inputs.items()})
    nc = bacc.Bacc("TRN2", target_bir_lowering=False, num_devices=1)
    aps = {n: nc.dram_tensor(f"{n}_dram", a.shape, mybir.dt.from_np(a.dtype), kind="ExternalInput").ap()
           for n, a in arrays.items()}
    out = nc.dram_tensor("out_dram", (P, DC * T), F32, kind="ExternalOutput").ap()
    build(nc, out=out, **aps)
    r = run_bass_kernel_spmd(nc, [{f"{n}_dram": a for n, a in arrays.items()}], core_ids=[0])
    y = r.results[0]["out_dram"].reshape(P, DC, T)
    return np.ascontiguousarray(y.transpose(2, 1, 0).reshape(1, T, D))
```

```python
import numpy as np
import concourse.bass as bass
from concourse import mybir
from contextlib import ExitStack

F32 = mybir.dt.float32
F32R = mybir.dt.float32r
I32 = mybir.dt.int32
U32 = mybir.dt.uint32
ACT = mybir.ActivationFunctionType
ALU = mybir.AluOpType
AX = mybir.AxisListType

P = 128
T = 256
NT = T // P
D = 1024
DC = D // P
EPS = 1e-6
BIG = 1e30
TAKEN = -3e38

H1, HD1, LAT = 16, 64, 128
IDXH, IDXD = 8, 64
TOPK = min(256, T // 4)
CONV = 4
LRU_C = 8.0
H2, HD2 = 8, 64
ROPE, MROT = 32, 16
QL, KL = 768, 256
QC, KC = QL // P, KL // P
MLA_SCALE = float((HD2 + ROPE) ** -0.5)
MOBA_SCALE = float(HD2 ** -0.5)
NG, EPG = 4, 8
NE = NG * EPG
FF = 256
SLOTS = 2 * T
WIN = 64
CAUSAL = P + T

UNIT = 1024
RING = 6
DRING = 4
HI_UNITS = 2 * (RING - DRING)

PLAN = [
    ("ckv_kidx", [2], "act"), ("qidx", [2, 4], "act"), ("xrnn", [2, 4, 6, 8], "act"),
    ("q", [2, 4, 6, 8], "act"), ("gattn", [2, 4, 6, 8], "dve"), ("grnn", [2, 4, 6, 8], "dve"),
    ("merge", [2, 4, 6, 8, 10, 12, 14, 16], "act"), ("rproj", [2, 4, 6, 8], "dve"),
    ("aproj", [2, 4, 6, 8], "dve"), ("out1", [2, 4, 6, 8], "dve"),
    ("cq", [2, 4, 6], "act"), ("ckv2", [2], "act"), ("qb", [2, 4], "act"), ("kb", [2, 4], "act"),
    ("vb", [4, 4], "act"), ("uq", [2, 4, 6, 8], "dve"), ("ukvk", [1, 1], "act"),
    ("ukvv", [1, 1], "act"), ("gates", [2, 4, 6, 8, 10, 12, 14, 16], "act"),
    ("omoba", [1, 2, 3, 4], "dve"), ("omla", [1, 2, 3, 4], "dve"), ("out2", [2, 4, 6, 8], "dve"),
]
FILL0, UNIT0, UNITS_AT, RELEASE = {}, {}, [], []
_u = 0
for _name, _ends, _eng in PLAN:
    FILL0[_name], UNIT0[_name] = len(UNITS_AT), _u
    for _e in _ends:
        UNITS_AT.append(_u + _e)
        RELEASE.append(_eng)
    _u += _ends[-1]
DENSE_UNITS = _u
DENSE_PANELS = DENSE_UNITS // 2
UNUSED_PANEL = 2
WINDOWS = T // 64
RELEASED = [RELEASE[:f + 1].count(RELEASE[f]) for f in range(len(RELEASE))]

NORMS = [(8, D), (1, LAT), (1, 1), (8, D), (8, D), (6, QL), (2, KL), (8, D), (8, D)]
N_X, N_CKV, N_KIDX, N_FIN1, N_ATT2, N_CQ, N_CKV2, N_FFN, N_OUT = range(9)
SQ0 = [sum((c + 1) // 2 for c, _ in NORMS[:k]) for k in range(10)]
NM0 = [sum(c for c, _ in NORMS[:k]) for k in range(10)]

VEC = {}
_c = 0
for _name, _n in [("norm_gain", 8), ("b_merge", 16), ("b_rg_a", 8), ("b_rg_x", 8), ("kv_norm_gain", 1),
                  ("idx_ln_gain", 1), ("idx_ln_bias", 1), ("conv_w", 32), ("conv_b", 8), ("lru_lambda", 8),
                  ("final_norm_gain", 8), ("attn_norm_2", 8), ("q_norm_2", 6), ("kv_norm_2", 2),
                  ("ffn_norm_2", 8), ("final_norm_2", 8), ("ones", P), ("b_router", 1)]:
    VEC[_name] = _c
    _c += _n
NVEC = _c
CST = {}
_c = 0
for _name, _n in [("ident", P), ("mean64", P), ("swap", P), ("before", P), ("dist", CAUSAL),
                  ("causal", CAUSAL), ("cos_mla", T), ("sin_mla", T), ("cos_moba", T), ("sin_moba", T),
                  ("iota", SLOTS)]:
    CST[_name] = _c
    _c += _n
NCST = _c


def build(nc, x_t, vecs, consts, w_widx, w_rg, w_uk, w_uv, w_kr, w_router, w_dense, w_expert, out):
    ctx = ExitStack()
    with ctx:
        def sb(name, shape, dt=F32):
            return ctx.enter_context(nc.sbuf_tensor(name, shape, dt))

        def sem(name):
            return ctx.enter_context(nc.semaphore(name))

        rounded = {}

        def sb2(name, shape):
            offset = -(-nc.sbuf_base // 32) * 32
            t = sb(name, shape)
            rounded[name] = nc.alloc_sbuf_tensor_at(f"{name}_r", shape, F32R, offset=offset)
            return t

        ring = sb2("ring", [P, RING, 2 * UNIT])
        hT = sb2("hT", [P, DC, T])
        scr = sb2("scr", [P, DC, T])
        widx_w = sb2("widx_w", [P, DC, IDXH])
        widx_hi = sb2("widx_hi", [P, DC, IDXH])
        wkr = sb2("wkr", [P, DC, 2 * ROPE])
        big = sb2("big", [P, 18 * 1024 + 512])
        vec = sb("vec", [P, NVEC])
        cst = sb("cst", [P, NCST])
        xT = sb("xT", [P, DC, T])
        wrt = sb("wrt", [P, DC, NG + NE])
        wu = sb("wu", [P, 2 * UNIT])
        root = sb("root", [P, T])
        rinv = sb("rinv", [P, T])
        halfb = sb("halfb", [P, 32])
        both_gains = sb("both_gains", [P, 8])
        sp = sb("sp", [P, 10, 8])
        attn = sb("attn", [P, 6 * CAUSAL])
        stat = sb("stat", [P, 2, 3, 2])
        th = sb("th", [P, 2, 2 * T])
        small = sb2("small", [P, 5 * 1024])

        def at(region, off, *dims):
            n = 1
            for d in dims:
                n *= d
            v = region[:, off:off + n]
            if len(dims) == 2:
                v = v.rearrange("p (a b) -> p a b", a=dims[0])
            if len(dims) == 3:
                v = v.rearrange("p (a b c) -> p a b c", a=dims[0], b=dims[1])
            return v

        K = 1024
        wuk = at(wu, 0, H1 // 2, 2 * HD1)
        wuv = at(wu, K, H1, HD1)
        S = at(attn, 0, 2, CAUSAL)
        E = at(attn, 2 * CAUSAL, 2, CAUSAL)
        PT = at(attn, 4 * CAUSAL, 2, CAUSAL)
        qT = at(big, 0, 8, T)
        oT = qT
        xr = at(big, 2 * K, 8, T + CONV)
        la = at(big, 2 * K, 8, T)
        u = at(big, 5 * K - 512, 8, T)
        ra = at(big, 7 * K - 512, 8, T)
        ib = at(big, 9 * K - 512, 8, T)
        sg = at(big, 11 * K - 512, 8, T)
        sr = at(big, 13 * K - 512, 8, T)
        lru_m = at(big, 16 * K + 512, 8, T)
        u_hi, o_hi, m_hi = la, ra, ib
        tm = at(big, 15 * K - 512, 16, T)
        wrg = at(big, 15 * K - 512, 2, 8, P)
        qi = at(small, 0, 4, T)
        zc = at(small, K, 2, T)
        kiT = at(small, K + 512, T)
        cT = at(small, K + 768, T)
        widx = at(small, 2 * K + 256, 2, IDXH)
        kk = at(small, K, 2, T)
        v1 = [at(small, 0, H1 * HD1), at(small, 2 * K + 512, H1 * HD1)]
        score = at(small, 3 * K + 512, CAUSAL)
        Dm = at(small, 4 * K, CAUSAL)
        top8 = at(small, 4 * K + 512, 2, 8)
        sq1 = at(small, 2 * K + 512, 2, T)
        cqT = at(big, 0, QC, T)
        ckT = at(big, 6 * 256, KC, T)
        qb = at(big, 2 * K, 4, T)
        kb = at(big, 3 * K, 4, T)
        vb = at(big, 4 * K, 2, 512)
        qh = at(big, 5 * K, H2, T)
        kh = at(big, 7 * K, H2, T)
        vh = at(big, 9 * K, 2, 512)
        tg2 = at(big, 10 * K, 16, T)
        oA = at(big, 14 * K, 4, T)
        oB = at(big, 15 * K, 4, T)
        cq_hi = at(big, 10 * K, QC, T)
        ck_hi = at(big, 11 * K + 512, KC, T)
        wkr_hi = at(big, 12 * K, DC, 2 * ROPE)
        ob_hi, oa_hi = at(big, 0, 4, T), at(big, K, 4, T)
        m2_hi = at(big, 2 * K, 8, T)
        ss2 = at(small, 4 * K + 256, T)
        cq_sq = at(big, 14 * K, QC, T)
        ck_sq = at(big, 15 * K + 512, KC, T)
        rot = at(big, 16 * K + 256, 2, 512)
        xs = at(big, 0, DC, SLOTS + WIN)
        ys = at(big, 4 * K + 512, DC, SLOTS + WIN)
        ysm_hi = at(big, 9 * K, SLOTS // P, D)
        ysm_lo = at(big, 14 * K + 512, SLOTS // P, D)
        SWT_hi = at(small, 2 * K, SLOTS // P, T)
        htok = at(big, 9 * K, 2, D)
        htok_hi = at(big, 11 * K, 2, D)
        rlogT = at(small, 4 * K, T)
        SWT = at(big, 13 * K, SLOTS // P, T)
        sel = at(big, 14 * K, 2, SLOTS)
        sw2 = at(big, 16 * K, SLOTS)
        sw = at(big, 15 * K, 2, SLOTS)
        actT = at(small, 0, 2, 2, WIN)
        xe = at(small, 3 * K, 2, DC, WIN)
        ye = at(small, 4 * K, 2, 512)
        early = {6: wu[:], 7: attn[:, 0:2 * UNIT], 8: big[:, 16 * K + 512:18 * K + 512],
                 9: scr.rearrange("p c t -> p (c t)"), 10: hT.rearrange("p c t -> p (c t)"),
                 11: big[:, 9 * K:11 * K]}
        rt = at(small, K, 1024)

        def V(name, i=0, n=1):
            return vec[:, VEC[name] + i:VEC[name] + i + n]

        def C(name, n, i=0):
            return cst[:, CST[name] + i:CST[name] + i + n]

        ident, ones = C("ident", P), V("ones", 0, P)

        D0, D1, L0, L1, TB, QB, OB, UB = [ctx.enter_context(nc.psum_tensor(n, [P, 512], F32))
                                          for n in ("D0", "D1", "L0", "L1", "TB", "QB", "OB", "UB")]
        DB, LB = [D0, D1], [L0, L1]

        arrived = [sem(f"panel_arrived_{i}") for i in range(DRING)]
        earrived = [sem(f"expert_panel_arrived_{i}") for i in range(RING)]
        early_arrived = {p: sem(f"early_panel_arrived_{p}") for p in early}
        hi_ready, lo_ready = sem("unit_rounded"), sem("unit_rest_ready")
        SPLITS = ("x", "widx", "u", "o", "m1", "att2", "wkr", "cq", "ck", "ob", "oa", "m2", "ysm", "swt")
        hi_of = {n: sem(f"{n}_rounded") for n in SPLITS}
        lo_of = {n: sem(f"{n}_rest_ready") for n in SPLITS}
        s_in = {n: sem(f"in_{n}") for n in ("x0", "x1", "vec", "cst", "widx", "wrg", "wuk", "wuv", "wkr", "wrt")}
        unit_done, panel_used = sem("unit_done"), sem("expert_panel_used")
        rel = {"act": sem("bank_released_by_act"), "dve": sem("bank_released_by_dve")}
        sq, ssq, rooted, rinvd, normed = [sem(n) for n in ("squared", "sumsq_ready", "rooted", "rinv_ready", "normed")]
        tanhd = sem("tanh_ready")
        vstep, astep = sem("vector_step"), sem("scalar_step")
        mean_ready, centered, kidx_ready, widx_mm, widx_ready = [sem(n) for n in (
            "mean_ready", "centered", "kidx_ready", "widx_matmul", "widx_ready")]
        idx_mm, idx_relu, idx_acc = sem("idx_scores"), sem("idx_relu"), sem("idx_accumulated")
        mask_ready = sem("mask_ready")
        padded, conv_done, gate_mm, gates, decay, sq_a, m_ready, rt_m, h_ready = [sem(n) for n in (
            "conv_padded", "conv_done", "rg_gates_matmul", "rg_gates_ready", "decay_ready", "decay_squared",
            "m_ready", "m_rooted", "gated_h_ready")]
        sp_step, sp_act, sp_ready = sem("softplus_step"), sem("softplus_act"), sem("softplus_ready")
        kk_mm, kk_ready = sem("keys_matmul"), sem("keys_ready")
        v1_mm, v1_ready = sem("values_matmul"), sem("values_ready")
        logits, biased, maxed, expd, probs = [sem(n) for n in ("logits", "biased", "maxed", "expd", "probs")]
        pt_mm, pt_ready, o_mm, o_ready = [sem(n) for n in ("probs_transposed", "pt_ready", "o_matmul", "o_ready")]
        mixed = sem("mixed_ready")
        kr_mm, kr_ready = sem("krope_matmul"), sem("krope_ready")
        swap_mm, rotated = sem("swap_matmul"), sem("moba_rotated")
        rlog_mm, rlog_kept, rlog, gate_neg, expg, topd, expt, onehot, cnt_mm, selected, weighted, offs = [
            sem(n) for n in ("router_matmul", "router_logits_kept", "router_logits", "group_max", "group_exp", "top2",
                             "top2_exp", "onehot_ready", "rank_matmul", "selection_ready", "slot_weights_ready",
                             "offsets_ready")]
        htok_mm, htok_ready, swt_mm, swt_ready, xs_mm, xs_ready = [sem(n) for n in (
            "htok_transposed", "htok_ready", "swt_transposed", "swt_ready", "gathered", "xs_ready")]
        hi_of["htok"], lo_of["htok"] = sem("htok_rounded"), sem("htok_rest_ready")
        ms2_ready = sem("second_mean_square_ready")
        padz = sem("pads_zero")
        xe_ready, gu_done, gate_t, silu_e, act_ready, at_mm, at_ready, y_mm, ye_ready, yt_mm, ys_done = [
            sem(n) for n in ("window_staged", "gate_up_done", "expert_gate_tanh", "expert_silu", "expert_act_ready",
                             "act_transposed", "act_t_ready", "down_done", "down_kept", "out_transposed",
                             "expert_out_kept")]
        ysm_mm, comb_mm, comb = [sem(n) for n in ("ys_transposed", "combined_matmul", "combined")]
        stored = sem("stored")

        def r32(ap):
            return bass.AP(rounded[ap.tensor.name], ap.offset, ap.ap)

        def dense_unit(n):
            return ring[:, (n // 2) % DRING, (n % 2) * UNIT:(n % 2 + 1) * UNIT]

        def hi_unit(n):
            return ring[:, DRING + (n % HI_UNITS) // 2, (n % 2) * UNIT:(n % 2 + 1) * UNIT]

        def expert_slot(p):
            return (p + DRING - 2) % RING

        def freed(eng, f):
            eng.wait_ge(rel[RELEASE[f]], RELEASED[f])

        def kept(eng, stage, i):
            freed(eng, FILL0[stage] + i)

        def filled(eng, stage, i):
            f = FILL0[stage] + i
            if eng is rounding["engine"]:
                rounding["advance"](UNITS_AT[f] + HI_UNITS)
            eng.wait_ge(unit_done, UNITS_AT[f])
            return DB[f % 2]

        def window_offset(eng, n):
            return eng.value_load(rt[0:1, 880:1008].bitcast(I32)[0:1, bass.ds(n, 1)], min_val=0, max_val=SLOTS)

        def since(eng, s_, it, c):
            if it is not None or c >= 0:
                eng.wait_ge(s_, (0 if it is None else it * 2) + (c + 1))

        def expert_steps(eng, one):
            for e in range(3):
                one(None, e)
            with eng.Fori(1, NE // 2 - 1) as it:
                for c in (1, 2):
                    one(it, c)
            one(None, NE - 1)

        def expert_panel(eng, it, c, n):
            g = 3 * c + n
            if it is None and g in early:
                eng.wait_ge(early_arrived[g], 16)
                return early[g]
            lap = g // RING + (1 if it is None and g < RING else 0) - (1 if g % RING == UNUSED_PANEL else 0)
            eng.wait_ge(earrived[expert_slot(g)], (0 if it is None else it * 16) + 16 * lap)
            return ring[:, expert_slot(g), :]

        def expert_banks(b):
            return (D0, D1)[b], (TB, L1)[b], (QB, L0)[b], (OB, UB)[b]

        def o_bank(m):
            return (UB, OB)[m % 2]

        rounding = {"engine": None, "advance": None}

        def x1_src(eng, stage):
            def src(c, w):
                kept(eng, stage, c // 2)
                return xT[:, c:c + w, :]
            return src

        def x3_src(eng):
            def src(c, w):
                eng.wait_ge(comb, c // 2 + 1)
                return xT[:, c:c + w, :]
            return src

        block = ctx.enter_context(nc.Block())

        @block.sync
        def _(sp_):
            def panel(slot, src):
                return sp_.dma_start(ring[:, slot, :], src).then_inc(arrived[slot], 16)

            for h in range(2):
                sp_.dma_start(xT[:, 4 * h:4 * h + 4, :], x_t[:, 4 * h * T:4 * (h + 1) * T].rearrange(
                    "p (c t) -> p c t", c=4)).then_inc(s_in[f"x{h}"], 16)
            sp_.dma_start(vec[:], vecs).then_inc(s_in["vec"], 16)
            panel(0, w_dense[0])
            sp_.dma_start(widx_w[:], w_widx.rearrange("p (c t) -> p c t", c=DC)).then_inc(s_in["widx"], 16)
            sp_.dma_start(cst[:, 0:NCST], consts).then_inc(s_in["cst"], 16)
            for p in range(1, DRING):
                panel(p, w_dense[p])
            sp_.dma_start(wrg, w_rg.rearrange("p (a c t) -> p a c t", a=2, c=8)).then_inc(s_in["wrg"], 16)
            sp_.dma_start(wuk, w_uk.rearrange("p (c t) -> p c t", c=8)).then_inc(s_in["wuk"], 16)
            sp_.dma_start(wuv, w_uv.rearrange("p (c t) -> p c t", c=16)).then_inc(s_in["wuv"], 16)
            sp_.dma_start(wkr[:], w_kr.rearrange("p (c t) -> p c t", c=DC)).then_inc(s_in["wkr"], 16)
            sp_.dma_start(wrt[:], w_router.rearrange("p (c t) -> p c t", c=DC)).then_inc(s_in["wrt"], 16)
            laps = DENSE_PANELS // DRING
            with sp_.Fori(1, laps) as lap:
                for slot in range(DRING):
                    sp_.wait_ge(unit_done, lap * (2 * DRING) + (2 * slot + 2 - 2 * DRING))
                    sp_.dma_start(ring[:, slot, :], w_dense[bass.ds(lap * DRING + slot, 1)].rearrange(
                        "a p n -> p (a n)")).then_inc(arrived[slot], 16)
            for p in range(laps * DRING, DENSE_PANELS):
                sp_.wait_ge(unit_done, 2 * (p - DRING) + 2)
                panel(p % DRING, w_dense[p])
            def early_panel(p):
                sp_.dma_start(early[p], w_expert[p - 1]).then_inc(early_arrived[p], 16)

            def expert(p, it=None):
                row = p - (p > UNUSED_PANEL) - 2 * (p > 3 * NE)
                src = w_expert[row] if it is None else w_expert[bass.ds(it * RING + (p - 1), 1)].rearrange(
                    "a p n -> p (a n)")
                sp_.dma_start(ring[:, expert_slot(p), :], src).then_inc(earrived[expert_slot(p)], 16)

            sp_.wait_ge(o_mm, H1 + 2 * H2)
            for p in (6, 7, 8):
                early_panel(p)
            for p in range(RING):
                if p != UNUSED_PANEL:
                    slot = expert_slot(p)
                    if slot < DRING:
                        last = max(q for q in range(DENSE_PANELS) if q % DRING == slot)
                    else:
                        last = max(q for q in range(DENSE_PANELS) if q % (RING - DRING) == slot - DRING)
                    sp_.wait_ge(unit_done, 2 * last + 2)
                    expert(p)
            sp_.wait_ge(ssq, N_FFN + 1)
            early_panel(9)
            sp_.wait_ge(htok_mm, 4)
            early_panel(10)
            sp_.wait_ge(xs_mm, DC)
            early_panel(11)
            for p in range(2 * RING, 3 * RING):
                sp_.wait_ge(panel_used, p + 1 - 2 * RING)
                expert(p)
            with sp_.Fori(3, 3 * NE // RING) as lap:
                for p in range(RING):
                    sp_.wait_ge(panel_used, lap * RING + (p + 1 - RING))
                    expert(p, lap)
            sp_.wait_ge(panel_used, 3 * NE + 3 - RING)
            expert(3 * NE + 2)
            for c in range(0, DC, 2):
                sp_.wait_ge(normed, NM0[N_OUT] + c + 2)
                sp_.dma_start(out[:, c * T:(c + 2) * T].rearrange("p (c t) -> p c t", c=2),
                              hT[:, c:c + 2, :]).then_inc(stored, 16)
            sp_.wait_ge(stored, 16 * (DC // 2))

        @block.tensor
        def _(pe):
            mm = nc.tensor.matmul
            seen = [0]

            def unit(n):
                if n >= seen[0]:
                    pe.wait_ge(lo_ready, n + 1)
                    seen[0] = n + 1
                return hi_unit(n), dense_unit(n)

            def mm3(out_, w, x, ws, xs_, start, stop):
                for m, (i, j) in enumerate(((0, 0), (0, 1), (1, 0))):
                    last = mm(out_, r32(w[i][ws]), r32(x[j][xs_]), start=start and m == 0, stop=stop and m == 2)
                return last

            def open_bank(stage, i):
                f = FILL0[stage] + i
                if f >= 2:
                    freed(pe, f - 2)
                return DB[f % 2]

            def chunk(stage, c, src, kc=DC, split=None, per=2):
                bank = open_bank(stage, c // 2) if c % 2 == 0 else DB[(FILL0[stage] + c // 2) % 2]
                w = unit(UNIT0[stage] + c)
                dst = bank[:, (c % 2) * T:(c % 2 + 1) * T]
                if split is None:
                    for k in range(kc):
                        last = mm3(dst, w, src, np.s_[:, k * P:(k + 1) * P], np.s_[:, k, :], k == 0, k == kc - 1)
                else:
                    for k in range(kc):
                        if k % per == 0:
                            pe.wait_ge(hi_of[split], k // per + 1)
                        for i in range(2):
                            mm(dst, r32(w[i][:, k * P:(k + 1) * P]), r32(src[0][:, k, :]),
                               start=(k + i == 0), stop=False)
                    for k in range(kc):
                        if k % per == 0:
                            pe.wait_ge(lo_of[split], k // per + 1)
                        last = mm(dst, r32(w[0][:, k * P:(k + 1) * P]), r32(src[1][:, k, :]),
                                  start=False, stop=(k == kc - 1))
                last.then_inc(unit_done, 1)

            h2 = (scr, hT)

            def sumsq(n, lhs=None, src=scr):
                nch = NORMS[n][0]
                if n:
                    pe.wait_ge(rooted, n)
                for c in range(nch):
                    pe.wait_ge(sq, SQ0[n] + c // 2 + 1)
                    last = mm(UB[:, 0:T], ones if lhs is None else lhs, src[:, c, :],
                              start=(c == 0), stop=(c == nch - 1))
                last.then_inc(ssq, 1)

            pe.wait_ge(s_in["vec"], 16)
            sumsq(N_X)
            for c in range(2):
                chunk("ckv_kidx", c, h2, split="x" if c == 0 else None)
            chunk("qidx", 0, h2)
            pe.wait_ge(s_in["cst"], 16)
            kept(pe, "ckv_kidx", 0)
            mm(OB[:, 0:T], C("mean64", P), zc[:, 1, :], start=True, stop=True).then_inc(mean_ready, 1)
            chunk("qidx", 1, h2)
            sumsq(N_CKV, src=sq1)
            pe.wait_ge(lo_of["widx"], 1)
            for tt in range(NT):
                for k in range(DC):
                    last = mm3(QB[:, tt * IDXH:(tt + 1) * IDXH], h2, (widx_hi, widx_w),
                               np.s_[:, k, tt * P:(tt + 1) * P], np.s_[:, k, :], k == 0, k == DC - 1)
            last.then_inc(widx_mm, 1)
            chunk("qidx", 2, h2)
            sumsq(N_KIDX, C("mean64", P), src=sq1[:, 1:2, :])
            chunk("qidx", 3, h2)
            chunk("xrnn", 0, h2)
            pe.wait_ge(kidx_ready, 1)
            kept(pe, "qidx", 1)
            for j in range(IDXH):
                if j >= 2:
                    pe.wait_ge(idx_relu, j - 1)
                lo = IDXD * (j % 2)
                mm(LB[j % 2][:, 0:P], qi[lo:lo + IDXD, j // 2, 0:P], kiT[lo:lo + IDXD, 0:P], start=True, stop=True)
                mm(LB[j % 2][:, P:CAUSAL], qi[lo:lo + IDXD, j // 2, P:T], kiT[lo:lo + IDXD, 0:T],
                   start=True, stop=True).then_inc(idx_mm, 1)
            for c in range(1, 8):
                chunk("xrnn", c, h2)
            def rg_gates(c):
                pe.wait_ge(conv_done, c + 1)
                pe.wait_ge(idx_relu, IDXH)
                if c >= 2:
                    pe.wait_ge(gates, c - 1)
                for g in range(2):
                    last = mm(LB[c % 2][:, g * T:(g + 1) * T], wrg[:, g, c, :], u[:, c, :], start=True, stop=True)
                last.then_inc(gate_mm, 1)

            def values(n):
                if n >= 2:
                    pe.wait_ge(v1_ready, n - 1)
                mm((OB, TB)[n % 2][:, :], cT[:, (n // 2) * P:(n // 2 + 1) * P],
                   wu[:, UNIT + (n % 2) * 512:UNIT + (n % 2 + 1) * 512], start=True, stop=True).then_inc(v1_mm, 1)

            pe.wait_ge(s_in["wrg"], 16)
            pe.wait_ge(s_in["wuv"], 16)
            pe.wait_ge(normed, NM0[N_CKV] + 1)
            for c in range(8):
                chunk("q", c, h2)
                if 2 <= c < 6:
                    values(c - 2)
                if c >= 6:
                    for i in range(4 * (c - 6), 4 * (c - 6) + 4):
                        rg_gates(i)

            def scores(a, q_of, k_of):
                pe.wait_ge(biased, a - 1) if a >= 2 else pe.wait_ge(gates, 8)
                for tt in range(NT):
                    c0, n = (0, P) if tt == 0 else (P, T)
                    last = mm(LB[a % 2][:, c0:c0 + n], q_of(tt), k_of(n), start=True, stop=True)
                last.then_inc(logits, 1)

            def transposes(a):
                pe.wait_ge(probs, a + 1)
                if a >= 1:
                    pe.wait_ge(pt_ready, a)
                for b in range(3):
                    last = nc.tensor.transpose(TB[:, b * P:(b + 1) * P], E[:, a % 2, b * P:(b + 1) * P], ident)
                last.then_inc(pt_mm, 1)

            def pv(a, v_of):
                pe.wait_ge(pt_ready, a + 1)
                if a % 2 == 0 and a >= 4:
                    pe.wait_ge(o_ready, a // 2 - 1)
                dst = o_bank(a // 2)[HD1 * (a % 2):HD1 * (a % 2 + 1)]
                mm(dst[:, 0:T], v_of(0), PT[:, a % 2, 0:T], start=True, stop=False, skip_group_check=True)
                mm(dst[:, P:T], v_of(1), PT[:, a % 2, T:CAUSAL], start=False, stop=True,
                   skip_group_check=True).then_inc(o_mm, 1)

            todo = [("gattn", c) for c in range(8)] + [("grnn", c) for c in range(8)] + [("merge", c) for c in range(16)]

            def fill():
                if todo:
                    chunk(*todo.pop(0), h2)

            pe.wait_ge(s_in["wuk"], 16)
            kept(pe, "q", 3)
            pe.wait_ge(v1_ready, 4)
            pe.wait_ge(widx_ready, 1)
            for i in range(H1 + 1):
                m, lo = i // 2, HD1 * (i % 2)
                if i < H1 and i % 2 == 0:
                    if m:
                        pe.wait_ge(kk_ready, m)
                    mm(QB[:, 0:T], wuk[:, m, :], cT, start=True, stop=True).then_inc(kk_mm, 1)
                fill()
                if i < H1:
                    pe.wait_ge(kk_ready, m + 1)
                    scores(i, lambda tt: qT[lo:lo + HD1, m, tt * P:(tt + 1) * P], lambda n: kk[lo:lo + HD1, m % 2, 0:n])
                if i >= 1:
                    transposes(i - 1)
                fill()
                if i >= 1:
                    pv(i - 1, lambda s: v1[s][:, (i - 1) * HD1:i * HD1])
            while todo:
                fill()
            pe.wait_ge(lo_of["u"], 4)
            for c in range(8):
                chunk("rproj", c, (u_hi, u))
            for c in range(8):
                chunk("aproj", c, (o_hi, oT), split="o" if c == 0 else None, per=1)
            for c in range(8):
                chunk("out1", c, (m_hi, tm), split="m1" if c == 0 else None)
            sumsq(N_FIN1)
            pe.wait_ge(o_ready, 8)
            for c in range(DC):
                pe.wait_ge(sq, SQ0[N_ATT2] + c // 2 + 1)
                last = mm(QB[:, 0:T], ones, m_hi[:, c, :], start=(c == 0), stop=(c == DC - 1))
            last.then_inc(ssq, 1)

            for c in range(6):
                chunk("cq", c, h2, split="att2" if c == 0 else None)
            for c in range(2):
                chunk("ckv2", c, h2)
            for c in range(4):
                chunk("qb", c, h2)
            for c in range(4):
                chunk("kb", c, h2)
            def swap(i):
                if i >= 2:
                    pe.wait_ge(rotated, i - 1)
                src = (qb if i < 2 else kb)[:, (i % 2) * 2:(i % 2) * 2 + 2, :]
                mm(LB[i % 2][:, :], C("swap", P), src, start=True, stop=True).then_inc(swap_mm, 1)

            sumsq(N_CQ, src=cq_sq)
            sumsq(N_CKV2, src=ck_sq)
            kept(pe, "qb", 1)
            swap(0)
            swap(1)
            for i in range(2):
                bank = open_bank("vb", i)
            vb_banks = [DB[(FILL0["vb"] + i) % 2] for i in range(2)]
            for k in range(DC):
                w = unit(UNIT0["vb"] + k // 2)
                for tt in range(NT):
                    last = mm3(vb_banks[tt][:, 0:512], h2, w, np.s_[:, k, tt * P:(tt + 1) * P],
                               np.s_[:, (k % 2) * 512:(k % 2 + 1) * 512], k == 0, k == DC - 1)
                if k % 2:
                    last.then_inc(unit_done, 1)
            pe.wait_ge(lo_of["wkr"], 1)
            for k in range(DC):
                last = mm3(QB[0:2 * ROPE, 0:T], (wkr_hi, wkr), h2, np.s_[:, k, :], np.s_[:, k, :], k == 0, k == DC - 1)
            last.then_inc(kr_mm, 1)
            swap(2)
            swap(3)
            for h in range(H2):
                chunk("uq", h, (cq_hi, cqT), kc=QC, split="cq" if h == 0 else None)
            pe.wait_ge(lo_of["ck"], 1)
            w = unit(UNIT0["ukvk"])
            for m in range(4):
                bank = open_bank("ukvk", m // 2) if m % 2 == 0 else DB[(FILL0["ukvk"] + m // 2) % 2]
                for k in range(KC):
                    last = mm3(bank[:, (m % 2) * T:(m % 2 + 1) * T], w, (ck_hi, ckT),
                               np.s_[:, (m * KC + k) * P:(m * KC + k + 1) * P], np.s_[:, k, :], k == 0, k == KC - 1)
            last.then_inc(unit_done, 1)
            w = unit(UNIT0["ukvv"])
            for tt in range(NT):
                bank = open_bank("ukvv", tt)
                for k in range(KC):
                    last = mm3(bank[:, 0:512], (ck_hi, ckT), w, np.s_[:, k, tt * P:(tt + 1) * P],
                               np.s_[:, k * 512:(k + 1) * 512], k == 0, k == KC - 1)
            last.then_inc(unit_done, 1)

            todo = [("gates", c) for c in range(16)]
            pe.wait_ge(rotated, 4)
            kept(pe, "vb", 1)
            for i in range(2 * H2 + 1):
                a = H1 + i
                if i < H2:
                    lo = HD2 * (i % 2)
                    scores(a, lambda tt: qb[lo:lo + HD2, i // 2, tt * P:(tt + 1) * P],
                           lambda n: kb[lo:lo + HD2, i // 2, 0:n])
                elif i < 2 * H2:
                    j = i - H2
                    if j == 0:
                        kept(pe, "uq", 3)
                        kept(pe, "ukvk", 1)
                        kept(pe, "ukvv", 1)
                        pe.wait_ge(kr_ready, 1)
                    scores(a, lambda tt: qh[0:HD2 + ROPE, j, tt * P:(tt + 1) * P], lambda n: kh[0:HD2 + ROPE, j, 0:n])
                if i >= 1:
                    transposes(a - 1)
                if todo:
                    chunk(*todo.pop(0), h2)
                if i >= 1:
                    j, v = ((i - 1) % H2), (vb if i - 1 < H2 else vh)
                    pe.wait_ge(rooted, N_CKV2 + 1)
                    pv(a - 1, lambda s: v[:, s, j * HD2:(j + 1) * HD2])

            def half_chunks(stage, src):
                for i in range(4):
                    bank, w = open_bank(stage, i), unit(UNIT0[stage] + i)
                    for m in range(2):
                        for k in range(4):
                            last = mm3(bank[:, m * T:(m + 1) * T], w, src,
                                       np.s_[:, (m * 4 + k) * P:(m * 4 + k + 1) * P], np.s_[:, k, :], k == 0, k == 3)
                    last.then_inc(unit_done, 1)

            pe.wait_ge(lo_of["ob"], 4)
            half_chunks("omoba", (ob_hi, oB))
            pe.wait_ge(lo_of["oa"], 4)
            half_chunks("omla", (oa_hi, oA))
            for c in range(8):
                chunk("out2", c, (m2_hi, tg2), split="m2" if c == 0 else None)
            sumsq(N_FFN)

            pe.wait_ge(s_in["wrt"], 16)
            for k in range(DC):
                pe.wait_ge(normed, NM0[N_FFN] + k + 1)
                last = mm(QB[0:NG + NE, 0:T], wrt[:, k, :], hT[:, k, :], start=(k == 0), stop=(k == DC - 1))
            last.then_inc(rlog_mm, 1)

            def htok_transposes(n):
                if n >= 2:
                    pe.wait_ge(hi_of["htok"], n - 1)
                for c in range(4):
                    last = nc.tensor.transpose(LB[n % 2][:, c * P:(c + 1) * P],
                                               hT[:, (n % 2) * 4 + c, (n // 2) * P:(n // 2 + 1) * P], ident)
                last.then_inc(htok_mm, 1)

            htok_transposes(0)
            pe.wait_ge(rlog_kept, 1)
            for tt in range(NT):
                last = nc.tensor.transpose(OB[:, tt * P:(tt + 1) * P], rlogT[:, tt * P:(tt + 1) * P], ident)
            last.then_inc(rlog, 1)
            for n in range(1, 4):
                htok_transposes(n)
            pe.wait_ge(onehot, 1)
            A = rt[:, 320:384]
            mm(QB[:, 0:2 * NE], C("before", P), A, start=True, stop=True)
            mm(QB[:, 2 * NE:4 * NE], ones, A, start=True, stop=True).then_inc(cnt_mm, 1)
            for c in range(DC):
                if c >= 2:
                    pe.wait_ge(xs_ready, c - 1)
                for tt in range(NT):
                    if c == 0:
                        pe.wait_ge(selected, tt + 1)
                        pe.wait_ge(lo_of["htok"], 2 * tt + 2)
                    for m, part in enumerate((htok_hi, htok)):
                        last = mm(DB[c % 2][:, :], r32(part[:, tt, c * P:(c + 1) * P]), r32(sel[:, tt, :]),
                                  start=(tt + m == 0), stop=(tt + m == NT))
                last.then_inc(xs_mm, 1)
            pe.wait_ge(weighted, 2)
            for s2 in range(2):
                for b in range(4):
                    s, tt = s2 * 2 + b // 2, b % 2
                    last = nc.tensor.transpose(LB[s2][:, b * P:(b + 1) * P], sw[:, tt, s * P:(s + 1) * P], ident)
                last.then_inc(swt_mm, 1)

            pe.wait_ge(offs, 1)
            pe.wait_ge(swt_ready, 2)

            def gate_up(it, c, release=None):
                b = c % 2
                gu = expert_banks(b)[0]
                for h in range(2):
                    w = expert_panel(pe, it, c, h).rearrange("p (m k f) -> p m k f", m=2, k=4)
                    for k in range(4):
                        for m in range(2):
                            last = mm(gu[m * WIN:(m + 1) * WIN, 0:FF], xe[:, b, h * 4 + k, :], w[:, m, k, :],
                                      start=(h + k == 0), stop=(h * 4 + k == DC - 1))
                            if release and h + k + m == 0:
                                last.then_inc(panel_used, release)
                last.then_inc(gu_done, 1)

            def act_transposes(c, release):
                b = c % 2
                for k in range(2):
                    last = nc.tensor.transpose(expert_banks(b)[1][:, k * P:(k + 1) * P],
                                               th[:, b, FF + k * P:FF + (k + 1) * P], ident)
                    if k == 0 and release:
                        last.then_inc(panel_used, release)
                last.then_inc(at_mm, 1)

            def down(it, c):
                b = c % 2
                w = expert_panel(pe, it, c, 5).rearrange("p (k h f) -> p k h f", k=2, h=2)
                for k in range(2):
                    for h in range(2):
                        last = mm(expert_banks(b)[2][h * WIN:(h + 1) * WIN, :], actT[:, b, k, :], w[:, k, h, :],
                                  start=(k == 0), stop=(k == 1))
                last.then_inc(y_mm, 1)

            def out_transposes(c):
                b = c % 2
                for q in range(4):
                    last = nc.tensor.transpose(expert_banks(b)[3][:, q * P:(q + 1) * P],
                                               ye[:, b, q * P:(q + 1) * P], ident)
                last.then_inc(yt_mm, 1)

            def gate_up_step(it, c):
                since(pe, xe_ready, it, c)
                since(pe, act_ready, it, c - 2)
                first = it is None and c < 2
                gate_up(it, c, release=(3 if c else None) if first else 1)

            def expert_step(it, c):
                if it is not None or c < NE - 1:
                    gate_up_step(it, c + 1)
                since(pe, act_ready, it, c)
                since(pe, at_ready, it, c - 2)
                act_transposes(c, 2)
                if it is not None or c:
                    since(pe, ye_ready, it, c - 1)
                    since(pe, ys_done, it, c - 3)
                    out_transposes(c - 1)
                since(pe, at_ready, it, c)
                since(pe, ye_ready, it, c - 2)
                down(it, c)

            crowded = pe.value_load(rt[0:1, 544:545].bitcast(I32), min_val=0, max_val=1)
            with pe.If(crowded):
                def one(it, c):
                    for j in range(WINDOWS):
                        w = (0 if it is None else it * (2 * WINDOWS)) + (c * WINDOWS + j + 1)
                        pe.wait_ge(xe_ready, w)
                        gate_up(it, c)
                        pe.wait_ge(act_ready, w)
                        act_transposes(c, 3 if j == WINDOWS - 1 else None)
                        pe.wait_ge(at_ready, w)
                        down(it, c)
                        pe.wait_ge(ye_ready, w)
                        out_transposes(c)
                        pe.wait_ge(ys_done, w)

                for c in range(4):
                    one(None, c)
                with pe.Fori(2, NE // 2) as it:
                    for c in range(2):
                        one(it, c)
            with pe.Else():
                gate_up_step(None, 0)
                expert_steps(pe, expert_step)
                since(pe, ye_ready, None, NE - 1)
                since(pe, ys_done, None, NE - 3)
                out_transposes(NE - 1)
                pe.wait_ge(ys_done, NE)
            def ysm_transposes(n):
                if n >= 2:
                    pe.wait_ge(lo_of["ysm"], n - 1)
                for c in range(4):
                    last = nc.tensor.transpose(LB[n % 2][:, c * P:(c + 1) * P],
                                               ys[:, (n // 4) * 4 + c, (n % 4) * P:(n % 4 + 1) * P], ident)
                last.then_inc(ysm_mm, 1)

            def combine(c):
                if c % 2 == 0 and c >= 4:
                    pe.wait_ge(comb, c // 2 - 1)
                for s in range(SLOTS // P):
                    if c % 4 == 0:
                        pe.wait_ge(lo_of["ysm"], c + s + 1)
                    last = mm3(DB[(c // 2) % 2][:, (c % 2) * T:(c % 2 + 1) * T], (ysm_hi, ysm_lo), (SWT_hi, SWT),
                               np.s_[:, s, c * P:(c + 1) * P], np.s_[:, s, :], s == 0, s == SLOTS // P - 1)
                if c % 2:
                    last.then_inc(comb_mm, 1)

            for n in range(4):
                ysm_transposes(n)
            pe.wait_ge(lo_of["swt"], 1)
            for c in range(DC):
                combine(c)
                if c < 4:
                    ysm_transposes(4 + c)
            sumsq(N_OUT)

        @block.scalar
        def _(act):
            A_ = nc.scalar.activation

            taken = [0]

            def advance(n):
                while taken[0] < min(n, DENSE_UNITS):
                    j = taken[0]
                    if j % 2 == 0:
                        act.wait_ge(arrived[(j // 2) % DRING], 16 * (j // 2 // DRING + 1))
                    if j >= HI_UNITS:
                        act.wait_ge(unit_done, j - HI_UNITS + 1)
                    A_(r32(hi_unit(j)), dense_unit(j), ACT.Copy).then_inc(hi_ready, 1)
                    taken[0] += 1

            rounding["engine"], rounding["advance"] = act, advance

            def round_pieces(name, full, hi, wait, pieces=4, per=2):
                for i in range(pieces):
                    wait(i)
                    A_(r32(hi[:, per * i:per * i + per, :]), full[:, per * i:per * i + per, :],
                       ACT.Copy).then_inc(hi_of[name], 1)

            def squares(n, src, dst=scr):
                nch = NORMS[n][0]
                if n and dst is scr:
                    act.wait_ge(ssq, n)
                for c in range(0, nch, 2):
                    w = min(2, nch - c)
                    A_(dst[:, c:c + w, :], src(c, w), ACT.Square).then_inc(sq, 1)

            def rootmean(n):
                act.wait_ge(ssq, n + 1)
                if n:
                    act.wait_ge(rinvd, n)
                act.wait_ge(vstep, 1)
                A_(root[:], UB[:, 0:T], ACT.Sqrt, bias=sp[:, 9, 0:1], scale=1.0 / NORMS[n][1]).then_inc(rooted, 1)

            def x_in(c, w):
                act.wait_ge(s_in["x0" if c < 4 else "x1"], 16)
                return xT[:, c:c + w, :]

            squares(N_X, x_in)
            rootmean(N_X)
            advance(2)
            round_pieces("x", hT, scr, lambda i: act.wait_ge(normed, 2 * i + 2))
            advance(HI_UNITS)
            act.wait_ge(sp_step, 2)
            A_(sp[:, 2, :], sp[:, 1, :], ACT.Exp, scale=-1.0).then_inc(sp_act, 1)
            act.wait_ge(sp_step, 3)
            A_(sp[:, 4, :], sp[:, 3, :], ACT.Ln).then_inc(sp_act, 1)
            bank = filled(act, "ckv_kidx", 0)
            A_(zc, bank[:, :].rearrange("p (a b) -> p a b", a=2), ACT.Copy).then_inc(rel["act"], 1)
            act.wait_ge(rel["act"], 1)
            squares(N_CKV, lambda c, w: zc[:, 0:1, :], sq1)
            rootmean(N_CKV)
            act.wait_ge(centered, 1)
            squares(N_KIDX, lambda c, w: zc[:, 1:2, :], sq1[:, 1:2, :])
            act.wait_ge(widx_mm, 1)
            A_(widx, QB[:, 0:2 * IDXH].rearrange("p (a b) -> p a b", a=2), ACT.Copy,
               scale=float(IDXH ** -0.5)).then_inc(widx_ready, 1)
            rootmean(N_KIDX)
            for i in range(2):
                bank = filled(act, "qidx", i)
                A_(qi[:, 2 * i:2 * i + 2, :], bank[:, :].rearrange("p (a b) -> p a b", a=2), ACT.Copy,
                   scale=float(IDXD ** -0.5)).then_inc(rel["act"], 1)

            def conv_in(i):
                bank = filled(act, "xrnn", i)
                A_(xr[:, 2 * i:2 * i + 2, CONV:CONV + T], bank[:, :].rearrange("p (a b) -> p a b", a=2),
                   ACT.Copy).then_inc(rel["act"], 1)

            for j in range(IDXH):
                act.wait_ge(idx_mm, j + 1)
                if j >= 2:
                    act.wait_ge(idx_acc, j - 1)
                A_(S[:, j % 2, :], LB[j % 2][:, 0:CAUSAL], ACT.Relu).then_inc(idx_relu, 1)
            conv_in(0)
            for i in range(1, 4):
                conv_in(i)
            def q_in(i):
                bank = filled(act, "q", i)
                A_(qT[:, 2 * i:2 * i + 2, :], bank[:, :].rearrange("p (a b) -> p a b", a=2), ACT.Copy,
                   scale=float(HD1 ** -0.5)).then_inc(rel["act"], 1)

            def rg_tanh(c):
                act.wait_ge(gate_mm, c + 1)
                A_(ra[:, c, :], LB[c % 2][:, 0:T], ACT.Tanh, bias=halfb[:, 16 + c:17 + c], scale=0.5)
                A_(ib[:, c, :], LB[c % 2][:, T:2 * T], ACT.Tanh, bias=halfb[:, 24 + c:25 + c],
                   scale=0.5).then_inc(gates, 1)

            def v1_in(n):
                act.wait_ge(v1_mm, n + 1)
                A_(v1[n // 2][:, (n % 2) * 512:(n % 2 + 1) * 512], (OB, TB)[n % 2][:, :], ACT.Copy).then_inc(v1_ready, 1)

            q_in(0)
            v1_in(0)
            q_in(1)
            v1_in(1)
            v1_in(2)
            q_in(2)
            v1_in(3)
            for c in range(4):
                rg_tanh(c)
            q_in(3)
            for c in range(4, 8):
                rg_tanh(c)
            act.wait_ge(gates, 8)
            act.wait_ge(sp_ready, 1)
            act.wait_ge(conv_done, 8)

            def decays(c0, c1):
                for c in range(c0, c1):
                    A_(la[:, c, :], ra[:, c, :], ACT.Exp, bias=sp[:, 8, c:c + 1], scale=sp[:, 8, c:c + 1]).then_inc(decay, 1)
                    act.wait_ge(decay, 2 * c + 1)
                    A_(ra[:, c, :], ra[:, c, :], ACT.Tanh, bias=sp[:, 7, c:c + 1], scale=sp[:, 7, c:c + 1]).then_inc(decay, 1)
                if c1 == 8:
                    for i in range(4):
                        A_(lru_m[:, 2 * i:2 * i + 2, :], la[:, 2 * i:2 * i + 2, :], ACT.Square).then_inc(sq_a, 1)

            def exps(a):
                act.wait_ge(maxed, a + 1)
                if a >= 2:
                    act.wait_ge(pt_mm, a - 1)
                for tt in range(NT):
                    c0, n = (0, P) if tt == 0 else (P, T)
                    last = A_(E[:, a % 2, c0:c0 + n], S[:, a % 2, c0:c0 + n], ACT.Exp,
                              bias=stat[:, a % 2, 0, tt:tt + 1], accum_out=stat[:, a % 2, 1, tt:tt + 1])
                last.then_inc(expd, 1)

            def ptcopy(a):
                act.wait_ge(pt_mm, a + 1)
                if a >= 2:
                    act.wait_ge(o_mm, a - 1)
                A_(PT[:, a % 2, :], TB[:, 0:CAUSAL], ACT.Copy).then_inc(pt_ready, 1)

            def half_tanh(f, stage, i):
                bank = filled(act, stage, i)
                if f >= 2:
                    act.wait_ge(rel["dve"], f - 1)
                A_(th[:, f % 2, :], bank[:, :], ACT.Tanh, scale=0.5).then_inc(tanhd, 1)

            def merge_gate(i):
                bank = filled(act, "merge", i)
                if i == 0:
                    act.wait_ge(gate_mm, 8)
                for m in range(2):
                    c = 2 * i + m
                    last = A_(tm[:, c, :], bank[:, m * T:(m + 1) * T], ACT.Tanh, bias=halfb[:, c:c + 1], scale=0.5)
                last.then_inc(rel["act"], 1)

            for i in range(H1 + 2):
                if i < H1 and i % 2 == 0:
                    m = i // 2
                    act.wait_ge(kk_mm, m + 1)
                    if m >= 2:
                        act.wait_ge(logits, 2 * m - 2)
                    A_(kk[:, m % 2, :], QB[:, 0:T], ACT.Copy).then_inc(kk_ready, 1)
                if 1 <= i <= H1:
                    ptcopy(i - 1)
                if i < H1:
                    exps(i)
                    if i < 8:
                        half_tanh(i, "gattn" if i < 4 else "grnn", i % 4)
                    else:
                        merge_gate(i - 8)
                    if i < 4:
                        decays(2 * i, 2 * i + 2)
                    if i == 5:
                        act.wait_ge(m_ready, 1)
                        A_(lru_m, lru_m, ACT.Sqrt).then_inc(rt_m, 1)
            advance(UNITS_AT[FILL0["aproj"] + 3] + HI_UNITS)
            round_pieces("m1", tm, m_hi, lambda i: act.wait_ge(mixed, i + 1))
            advance(UNITS_AT[FILL0["out1"] + 3] + HI_UNITS)
            squares(N_FIN1, x1_src(act, "out1"))
            act.wait_ge(unit_done, UNITS_AT[FILL0["out1"] + 3])
            for c in range(DC):
                last = A_(m_hi[:, c, :], xT[:, c, :], ACT.Square, scale=V("final_norm_gain", c))
                if c % 2:
                    last.then_inc(sq, 1)
            rootmean(N_FIN1)
            act.wait_ge(ms2_ready, 1)
            act.wait_ge(rinvd, N_ATT2)
            A_(root[:], ss2, ACT.Sqrt, bias=sp[:, 9, 0:1], scale=1.0 / D).then_inc(rooted, 1)
            round_pieces("att2", hT, scr, lambda i: act.wait_ge(normed, NM0[N_FIN1] + 2 * i + 2))

            def keep(stage, i, dst, n=2):
                bank = filled(act, stage, i)
                A_(dst, bank[:, :].rearrange("p (a b) -> p a b", a=n), ACT.Copy).then_inc(rel["act"], 1)

            act.wait_ge(unit_done, UNITS_AT[FILL0["aproj"] + 3])
            for i in range(3):
                keep("cq", i, cqT[:, 2 * i:2 * i + 2, :])
            keep("ckv2", 0, ckT)
            for i in range(2):
                keep("qb", i, qb[:, 2 * i:2 * i + 2, :])
            act.wait_ge(rel["act"], RELEASED[FILL0["ckv2"]])
            squares(N_CQ, lambda c, w: cqT[:, c:c + w, :], cq_sq)
            squares(N_CKV2, lambda c, w: ckT, ck_sq)
            for i in range(2):
                keep("kb", i, kb[:, 2 * i:2 * i + 2, :])
            rootmean(N_CQ)
            rootmean(N_CKV2)
            round_pieces("cq", cqT, cq_hi, lambda i: act.wait_ge(normed, NM0[N_CQ] + 2 * i + 2), 3)
            round_pieces("ck", ckT, ck_hi, lambda i: act.wait_ge(normed, NM0[N_CKV2] + 2), 1)
            for i in range(2):
                bank = filled(act, "vb", i)
                A_(vb[:, i, :], bank[:, :], ACT.Copy).then_inc(rel["act"], 1)
            advance(UNITS_AT[FILL0["uq"] + 3] + HI_UNITS)
            for i in range(2):
                bank = filled(act, "ukvk", i)
                v = bank[:, :].rearrange("p (a b) -> p a b", a=2)
                A_(kh[0:64, 4 * i:4 * i + 4:2, :], v[0:64], ACT.Copy)
                A_(kh[0:64, 4 * i + 1:4 * i + 4:2, :], v[64:128], ACT.Copy).then_inc(rel["act"], 1)
            for i in range(2):
                bank = filled(act, "ukvv", i)
                A_(vh[:, i, :], bank[:, :], ACT.Copy).then_inc(rel["act"], 1)
            for i in range(2 * H2 + 1):
                a = H1 + i
                if i >= 1:
                    ptcopy(a - 1)
                if i < 2 * H2:
                    exps(a)
                    if i % 2:
                        g = i // 2
                        bank = filled(act, "gates", g)
                        A_(tg2[:, 2 * g:2 * g + 2, :], bank[:, :].rearrange("p (a b) -> p a b", a=2), ACT.Tanh,
                           scale=0.5).then_inc(rel["act"], 1)
            advance(UNITS_AT[FILL0["omla"] + 3] + HI_UNITS)
            round_pieces("m2", tg2, m2_hi, lambda i: act.wait_ge(mixed, 4 + i + 1))
            advance(DENSE_UNITS)
            squares(N_FFN, x1_src(act, "out2"))
            rootmean(N_FFN)
            for n in range(4):
                act.wait_ge(htok_mm, n + 1)
                piece = np.s_[:, n // 2, (n % 2) * 512:(n % 2 + 1) * 512]
                A_(htok[piece], LB[n % 2][:, :], ACT.Copy).then_inc(htok_ready, 1)
                A_(r32(htok_hi[piece]), LB[n % 2][:, :], ACT.Copy).then_inc(hi_of["htok"], 1)
            for tt in range(NT):
                act.wait_ge(gate_neg, 1)
                A_(rt[:, 392 + 4 * tt:396 + 4 * tt], OB[:, tt * P:tt * P + NG], ACT.Exp,
                   bias=rt[:, 384 + tt:385 + tt], accum_out=rt[:, 386 + tt:387 + tt]).then_inc(expg, 1)
            act.wait_ge(topd, 1)
            A_(rt[:, 388:390], rt[:, 390:392], ACT.Exp).then_inc(expt, 1)
            for c in range(DC):
                act.wait_ge(xs_mm, c + 1)
                A_(xs[:, c, 0:SLOTS], DB[c % 2][:, :], ACT.Copy).then_inc(xs_ready, 1)
            for s2 in range(2):
                act.wait_ge(swt_mm, s2 + 1)
                A_(SWT[:, 2 * s2:2 * s2 + 2, :], LB[s2][:, :].rearrange("p (a b) -> p a b", a=2),
                   ACT.Copy).then_inc(swt_ready, 1)
            act.wait_ge(offs, 1)

            def gate_tanh(c):
                b = c % 2
                A_(th[0:WIN, b, 0:FF], expert_banks(b)[0][0:WIN, 0:FF], ACT.Tanh, scale=0.5).then_inc(gate_t, 1)

            def act_t(c):
                b = c % 2
                A_(actT[:, b], expert_banks(b)[1][:, 0:2 * P].rearrange("p (a b) -> p a b", a=2)[:, :, 0:WIN],
                   ACT.Copy).then_inc(at_ready, 1)

            def down_keep(c):
                b = c % 2
                A_(ye[:, b, :], expert_banks(b)[2][:, :], ACT.Copy).then_inc(ye_ready, 1)

            def expert_step(it, c):
                if it is not None or c < NE - 1:
                    since(act, gu_done, it, c + 1)
                    since(act, act_ready, it, c - 1)
                    gate_tanh(c + 1)
                since(act, at_mm, it, c)
                since(act, y_mm, it, c - 2)
                act_t(c)
                since(act, y_mm, it, c)
                since(act, yt_mm, it, c - 2)
                down_keep(c)

            crowded = act.value_load(rt[0:1, 544:545].bitcast(I32), min_val=0, max_val=1)
            with act.If(crowded):
                with act.Fori(0, NE // 2) as it:
                    for c in range(2):
                        for j in range(WINDOWS):
                            w = it * (2 * WINDOWS) + (c * WINDOWS + j + 1)
                            act.wait_ge(gu_done, w)
                            gate_tanh(c)
                            act.wait_ge(at_mm, w)
                            act_t(c)
                            act.wait_ge(y_mm, w)
                            down_keep(c)
            with act.Else():
                since(act, gu_done, None, 0)
                gate_tanh(0)
                expert_steps(act, expert_step)
            for n in range(8):
                act.wait_ge(ysm_mm, n + 1)
                A_(r32(ysm_hi[:, n % 4, (n // 4) * 512:(n // 4 + 1) * 512]), LB[n % 2][:, :],
                   ACT.Copy).then_inc(hi_of["ysm"], 1)
            squares(N_OUT, x3_src(act))
            rootmean(N_OUT)

        @block.gpsimd
        def _(pool):
            g = nc.gpsimd
            for n in range(DENSE_UNITS):
                pool.wait_ge(hi_ready, n + 1)
                w = dense_unit(n)
                g.tensor_tensor(r32(w), w, r32(hi_unit(n)).bitcast(F32), ALU.subtract).then_inc(lo_ready, 1)

            for n in range(4):
                pool.wait_ge(hi_of["htok"], n + 1)
                f, h = [a[:, n // 2, (n % 2) * 512:(n % 2 + 1) * 512] for a in (htok, htok_hi)]
                g.tensor_tensor(r32(f), f, r32(h).bitcast(F32), ALU.subtract).then_inc(lo_of["htok"], 1)

            pool.wait_ge(offs, 1)
            pool.wait_ge(padz, 3)

            def stage(c, off):
                g.tensor_copy(xe[:, c % 2], xs[:, :, bass.ds(off, WIN)]).then_inc(xe_ready, 1)

            def stage_step(it, c):
                if it is None and c == 0:
                    return
                off = window_offset(pool, (0 if it is None else it * (2 * WINDOWS)) + c * WINDOWS)
                since(pool, gu_done, it, c - 2)
                stage(c, off)

            crowded = pool.value_load(rt[0:1, 544:545].bitcast(I32), min_val=0, max_val=1)
            with pool.If(crowded):
                pool.wait_ge(xs_ready, DC)
                with pool.Fori(0, NE // 2) as it:
                    for c in range(2):
                        for j in range(WINDOWS):
                            n = c * WINDOWS + j
                            stage(c, window_offset(pool, it * (2 * WINDOWS) + n))
                            pool.wait_ge(gu_done, it * (2 * WINDOWS) + (n + 1))
            with pool.Else():
                pool.wait_ge(xs_ready, DC)
                pool.wait_ge(xe_ready, 1)
                expert_steps(pool, stage_step)

        @block.vector
        def _(dve):
            v = nc.vector
            count = [0]

            def step(ins):
                count[0] += 1
                ins.then_inc(vstep, 1)
                dve.wait_ge(vstep, count[0])

            def stt(out_, in0, scalar, in1, op0=ALU.mult, op1=ALU.mult):
                return v.scalar_tensor_tensor(out=out_, in0=in0, scalar=scalar, in1=in1, op0=op0, op1=op1)

            def norm(n, src, dst, gain):
                nch = NORMS[n][0]
                dve.wait_ge(rooted, n + 1)
                if n:
                    dve.wait_ge(normed, NM0[n])
                v.reciprocal(rinv[:], root[:]).then_inc(rinvd, 1)
                dve.wait_ge(rinvd, n + 1)
                for c in range(nch):
                    stt(dst(c), src(c), V(gain, c), rinv[:]).then_inc(normed, 1)

            def rest_of(name, full, hi, pieces=4, per=2, first=0):
                for i in range(first, first + pieces):
                    dve.wait_ge(hi_of[name], i + 1)
                    f = full[:, per * i:per * i + per, :]
                    v.tensor_tensor(r32(f), f, r32(hi[:, per * i:per * i + per, :]).bitcast(F32),
                                    ALU.subtract).then_inc(lo_of[name], 1)

            def split(name, full, hi, i, per=1):
                v.tensor_copy(r32(hi[:, per * i:per * i + per, :]), full[:, per * i:per * i + per, :]).then_inc(hi_of[name], 1)
                rest_of(name, full, hi, 1, per, i)

            step(v.memset(sp[:, 9, :], EPS))
            dve.wait_ge(s_in["vec"], 16)
            dve.wait_ge(s_in["x0"], 16)
            dve.wait_ge(s_in["x1"], 16)
            norm(N_X, lambda c: xT[:, c, :], lambda c: hT[:, c, :], "norm_gain")
            rest_of("x", hT, scr)
            dve.wait_ge(s_in["widx"], 16)
            split("widx", widx_w, widx_hi, 0, DC)
            v.memset(xr[:, :, 0:CONV], 0.0).then_inc(padded, 1)
            step(v.tensor_tensor(both_gains[:], V("final_norm_gain", 0, 8), V("attn_norm_2", 0, 8), ALU.mult))
            step(v.tensor_scalar(halfb[:], V("b_merge", 0, 32), 0.5, None, ALU.mult))
            v.tensor_scalar(sp[:, 0, :], V("lru_lambda", 0, 8), -1.0, None, ALU.mult).then_inc(sp_step, 1)
            dve.wait_ge(sp_step, 1)
            v.tensor_tensor(sp[:, 1, :], sp[:, 0, :], V("lru_lambda", 0, 8), ALU.max).then_inc(sp_step, 1)
            dve.wait_ge(sp_act, 1)
            v.tensor_scalar(sp[:, 3, :], sp[:, 2, :], 1.0, None, ALU.add).then_inc(sp_step, 1)
            dve.wait_ge(sp_step, 3)
            step(v.tensor_scalar(sp[:, 5, :], sp[:, 3, :], 1.0, None, ALU.is_equal))
            step(stt(sp[:, 6, :], sp[:, 3, :], -1.0, sp[:, 5, :], ALU.add, ALU.add))
            step(v.reciprocal(sp[:, 7, :], sp[:, 6, :]))
            dve.wait_ge(sp_act, 2)
            step(v.tensor_tensor(sp[:, 6, :], sp[:, 4, :], sp[:, 5, :], ALU.add))
            step(v.tensor_tensor(sp[:, 6, :], sp[:, 6, :], sp[:, 2, :], ALU.mult))
            step(v.tensor_tensor(sp[:, 6, :], sp[:, 6, :], sp[:, 7, :], ALU.mult))
            step(stt(sp[:, 6, :], sp[:, 0, :], 0.0, sp[:, 6, :], ALU.max, ALU.add))
            step(v.tensor_scalar(sp[:, 7, :], sp[:, 6, :], LRU_C / 2, None, ALU.mult))
            v.tensor_scalar(sp[:, 8, :], sp[:, 6, :], -LRU_C / 2, None, ALU.mult).then_inc(sp_ready, 1)

            dve.wait_ge(mean_ready, 1)
            v.tensor_tensor(zc[:, 1, :], zc[:, 1, :], OB[:, 0:T], ALU.subtract).then_inc(centered, 1)
            norm(N_CKV, lambda c: zc[:, 0, :], lambda c: cT, "kv_norm_gain")
            dve.wait_ge(centered, 1)
            norm(N_KIDX, lambda c: zc[:, 1, :], lambda c: kiT, "idx_ln_gain")
            dve.wait_ge(normed, NM0[N_KIDX] + 1)
            v.tensor_scalar(kiT, kiT, V("idx_ln_bias"), None, ALU.add).then_inc(kidx_ready, 1)
            dve.wait_ge(widx_ready, 1)
            dve.wait_ge(s_in["cst"], 16)
            tiles = [(0, P), (P, T)]
            for j in range(IDXH):
                dve.wait_ge(idx_relu, j + 1)
                if j:
                    dve.wait_ge(idx_acc, j)
                for tt, (c0, n) in enumerate(tiles):
                    acc = score[:, c0:c0 + n]
                    last = stt(acc, S[:, j % 2, c0:c0 + n], widx[:, tt, j:j + 1],
                               acc if j else C("causal", n, c0), ALU.mult, ALU.add)
                last.then_inc(idx_acc, 1)
            dve.wait_ge(idx_acc, IDXH)
            for tt, (c0, n) in enumerate(tiles):
                s = score[:, c0:c0 + n]
                for r in range(TOPK // 8):
                    step(v.max(out=top8[:, tt, :], in_=s))
                    step(v.match_replace(out=s, in_to_replace=top8[:, tt, :], in_values=s, imm_value=TAKEN))
            step(v.tensor_scalar(score, score, TAKEN / 2, -BIG, ALU.is_gt, ALU.mult))
            v.tensor_tensor(Dm, score, C("dist", CAUSAL), ALU.add).then_inc(mask_ready, 1)
            dve.wait_ge(padded, 1)
            for c in range(8):
                kept(dve, "xrnn", c // 2)
                step(v.tensor_scalar(u[:, c, :], xr[:, c, 4:4 + T], V("conv_w", 3 * 8 + c), V("conv_b", c),
                                     ALU.mult, ALU.add))
                for t in (2, 1, 0):
                    ins = stt(u[:, c, :], xr[:, c, 1 + t:1 + t + T], V("conv_w", t * 8 + c), u[:, c, :],
                              ALU.mult, ALU.add)
                    if t:
                        step(ins)
                ins.then_inc(conv_done, 1)

            def bias_max(a):
                kind = 0 if a < H1 else 1
                dve.wait_ge(logits, a + 1)
                if a >= 2:
                    dve.wait_ge(expd, a - 1)
                sa = S[:, a % 2, :]
                if kind == 0:
                    ins = stt(sa, Dm, float(2.0 ** (-8.0 * (a + 1) / H1)), LB[a % 2][:, 0:CAUSAL], ALU.mult, ALU.add)
                else:
                    ins = stt(sa, LB[a % 2][:, 0:CAUSAL], MOBA_SCALE if a < H1 + H2 else MLA_SCALE,
                              C("causal", CAUSAL), ALU.mult, ALU.add)
                ins.then_inc(biased, 1)
                dve.wait_ge(biased, a + 1)
                for tt, (c0, n) in enumerate(tiles):
                    last = v.reduce_max(stat[:, a % 2, 0, tt:tt + 1], S[:, a % 2, c0:c0 + n], axis=AX.X, negate=True)
                last.then_inc(maxed, 1)

            def normalise(a):
                dve.wait_ge(expd, a + 1)
                step(v.reciprocal(stat[:, a % 2, 2, :], stat[:, a % 2, 1, :]))
                for tt, (c0, n) in enumerate(tiles):
                    last = v.tensor_scalar(E[:, a % 2, c0:c0 + n], E[:, a % 2, c0:c0 + n],
                                           stat[:, a % 2, 2, tt:tt + 1], None, ALU.mult)
                last.then_inc(probs, 1)

            def silu2(f, stage, i, dst):
                bank = DB[(FILL0[stage] + i) % 2]
                dve.wait_ge(tanhd, f + 1)
                stt(dst[:, 2 * i:2 * i + 2, :], th[:, f % 2, :].rearrange("p (a b) -> p a b", a=2), 1.0,
                    bank[:, :].rearrange("p (a b) -> p a b", a=2), ALU.add, ALU.mult).then_inc(rel["dve"], 1)

            dve.wait_ge(mask_ready, 1)

            def lru(i):
                if i == 0:
                    dve.wait_ge(sq_a, 4)
                    stt(lru_m, lru_m, 1.0, ra, ALU.add, ALU.mult).then_inc(m_ready, 1)
                elif i == 1:
                    step(stt(ib, ib, 1.0, u, ALU.add, ALU.mult))
                elif i == 2:
                    dve.wait_ge(rt_m, 1)
                    step(stt(ib, lru_m, 0.5, ib))
                elif i < 7:
                    for c in range(2 * (i - 3), 2 * (i - 3) + 2):
                        last = v.tensor_tensor_scan(u[:, c, :], la[:, c, :], ib[:, c, :], 0.0, ALU.mult, ALU.add)
                    step(last)
                elif 8 <= i < 12:
                    c = 2 * (i - 8)
                    kept(dve, "grnn", i - 8)
                    stt(u[:, c:c + 2, :], u[:, c:c + 2, :], 0.5, sr[:, c:c + 2, :]).then_inc(h_ready, 1)
                    dve.wait_ge(h_ready, i - 7)
                    split("u", u, u_hi, i - 8, 2)

            for i in range(H1 + 2):
                if i < H1:
                    bias_max(i)
                    normalise(i)
                    if i >= 4:
                        lru(i - 4)
                if i >= 3 and i % 2:
                    m = (i - 3) // 2
                    dve.wait_ge(o_mm, 2 * m + 2)
                    kept(dve, "gattn", m // 2)
                    stt(oT[:, m, :], o_bank(m)[:, 0:T], 0.5, sg[:, m, :]).then_inc(o_ready, 1)
                    if m:
                        dve.wait_ge(o_ready, m)
                        split("o", oT, o_hi, m - 1)
                if i < 8:
                    silu2(i, "gattn" if i < 4 else "grnn", i % 4, sg if i < 4 else sr)

            dve.wait_ge(o_ready, 8)
            split("o", oT, o_hi, 7)

            def layer_end(proj_r, proj_a, gate_r, gate_a, out_stage, cut, hi):
                for stage, gate in ((proj_r, gate_r), (proj_a, gate_a)):
                    for i in range(4):
                        bank = filled(dve, stage, i)
                        g = gate[:, 2 * i:2 * i + 2, :]
                        stt(g, g, 1.0, bank[:, :].rearrange("p (a b) -> p a b", a=2), ALU.add,
                            ALU.mult).then_inc(rel["dve"], 1)
                        if gate is gate_a:
                            kept(dve, stage, i)
                            v.tensor_tensor(g, g, gate_r[:, 2 * i:2 * i + 2, :], ALU.add).then_inc(mixed, 1)
                    if gate is gate_a:
                        rest_of(cut, gate_a, hi)
                for i in range(4):
                    bank = filled(dve, out_stage, i)
                    r = xT[:, 2 * i:2 * i + 2, :]
                    stt(r, bank[:, :].rearrange("p (a b) -> p a b", a=2), 0.5, r, ALU.mult,
                        ALU.add).then_inc(rel["dve"], 1)

            kept(dve, "merge", 7)
            layer_end("rproj", "aproj", tm[:, 8:16, :], tm[:, 0:8, :], "out1", "m1", m_hi)
            kept(dve, "out1", 3)
            dve.wait_ge(rooted, N_FIN1 + 1)
            dve.wait_ge(normed, NM0[N_FIN1])
            v.reciprocal(rinv[:], root[:]).then_inc(rinvd, 1)
            dve.wait_ge(rinvd, N_FIN1 + 1)
            dve.wait_ge(ssq, N_ATT2 + 1)
            step(v.tensor_tensor(ss2, QB[:, 0:T], rinv[:], ALU.mult))
            v.tensor_tensor(ss2, ss2, rinv[:], ALU.mult).then_inc(ms2_ready, 1)
            dve.wait_ge(ms2_ready, 1)
            dve.wait_ge(rooted, N_ATT2 + 1)
            v.reciprocal(ss2, root[:]).then_inc(rinvd, 1)
            dve.wait_ge(rinvd, N_ATT2 + 1)
            step(v.tensor_tensor(ss2, ss2, rinv[:], ALU.mult))
            for c in range(DC):
                stt(hT[:, c, :], xT[:, c, :], both_gains[:, c:c + 1], ss2).then_inc(normed, 1)
            rest_of("att2", hT, scr)
            for c in range(DC):
                stt(xT[:, c, :], xT[:, c, :], V("final_norm_gain", c), rinv[:]).then_inc(normed, 1)
            dve.wait_ge(s_in["wkr"], 16)
            split("wkr", wkr, wkr_hi, 0, DC)

            kept(dve, "ckv2", 0)
            norm(N_CQ, lambda c: cqT[:, c, :], lambda c: cqT[:, c, :], "q_norm_2")
            norm(N_CKV2, lambda c: ckT[:, c, :], lambda c: ckT[:, c, :], "kv_norm_2")
            rest_of("cq", cqT, cq_hi, 3)
            rest_of("ck", ckT, ck_hi, 1)
            cosb = C("cos_moba", T).unsqueeze(1).to_broadcast([P, 2, T])
            sinb = C("sin_moba", T).unsqueeze(1).to_broadcast([P, 2, T])

            def rotate(i):
                x2 = (qb if i < 2 else kb)[:, (i % 2) * 2:(i % 2) * 2 + 2, :]
                r = rot[:, 0, :].rearrange("p (a b) -> p a b", a=2)
                dve.wait_ge(swap_mm, i + 1)
                step(v.tensor_tensor(r, LB[i % 2][:, :].rearrange("p (a b) -> p a b", a=2), sinb, ALU.mult))
                step(v.tensor_tensor(x2, x2, cosb, ALU.mult))
                v.tensor_tensor(x2, x2, r, ALU.add).then_inc(rotated, 1)
                dve.wait_ge(rotated, i + 1)

            rotate(0)
            rotate(1)
            dve.wait_ge(kr_mm, 1)
            step(v.tensor_tensor(rot[64:96, 0, 0:T], QB[0:32, 0:T], cst[0:32, CST["cos_mla"]:CST["cos_mla"] + T], ALU.mult))
            step(v.tensor_tensor(rot[64:96, 1, 0:T], QB[32:64, 0:T], cst[32:64, CST["sin_mla"]:CST["sin_mla"] + T], ALU.mult))
            v.tensor_tensor(kh[64:96, :, :], rot[64:96, 0:1, 0:T].to_broadcast([32, H2, T]),
                            rot[64:96, 1:2, 0:T].to_broadcast([32, H2, T]), ALU.add).then_inc(kr_ready, 1)
            dve.wait_ge(kr_ready, 1)
            kept(dve, "kb", 1)
            rotate(2)
            rotate(3)
            for i in range(4):
                bank = filled(dve, "uq", i)
                if i:
                    kept(dve, "uq", i - 1)
                b3 = bank[:, :].rearrange("p (a b) -> p a b", a=2)
                h2 = slice(2 * i, 2 * i + 2)
                cosq = cst[64:96, CST["cos_mla"]:CST["cos_mla"] + T].unsqueeze(1).to_broadcast([32, 2, T])
                sinq = cst[96:128, CST["sin_mla"]:CST["sin_mla"] + T].unsqueeze(1).to_broadcast([32, 2, T])
                r = rot[64:96, :, :].rearrange("p r (a b) -> p r a b", a=2)
                v.tensor_copy(qh[0:64, h2, :], b3[0:64])
                step(v.tensor_tensor(r[:, 0], b3[64:96], cosq, ALU.mult))
                step(v.tensor_tensor(r[:, 1], b3[96:128], sinq, ALU.mult))
                v.tensor_tensor(qh[64:96, h2, :], r[:, 0], r[:, 1], ALU.add).then_inc(rel["dve"], 1)
            for i in range(2 * H2 + 1):
                a = H1 + i
                if i < 2 * H2:
                    bias_max(a)
                    normalise(a)
                if i >= 2 and i % 2 == 0:
                    m = (i - 2) // 2
                    dve.wait_ge(o_mm, H1 + 2 * m + 2)
                    dst = oB if m < 4 else oA
                    v.tensor_copy(dst[:, m % 4, :], o_bank(m)[:, 0:T]).then_inc(o_ready, 1)
                    dve.wait_ge(o_ready, 8 + m + 1)
                    split(*(("ob", oB, ob_hi) if m < 4 else ("oa", oA, oa_hi)), m % 4)
            kept(dve, "gates", 7)
            layer_end("omoba", "omla", tg2[:, 8:16, :], tg2[:, 0:8, :], "out2", "m2", m2_hi)
            kept(dve, "out2", 3)
            v.memset(xs[:, :, SLOTS:SLOTS + WIN], 0.0).then_inc(padz, 1)
            v.memset(rlogT, 0.0).then_inc(padz, 1)
            gpad = rt[:, 0:16].rearrange("p (a b) -> p a b", a=2)
            v.memset(rt[:, 0:16], TAKEN).then_inc(padz, 1)
            norm(N_FFN, lambda c: xT[:, c, :], lambda c: hT[:, c, :], "ffn_norm_2")

            def pair(a, n):
                return rt[:, a:a + 2 * n].rearrange("p (a b) -> p a b", a=2)

            iota = C("iota", SLOTS)
            lg = OB[:, 0:2 * P].rearrange("p (a b) -> p a b", a=2)
            gtop, gidx, gsel = pair(16, 8), pair(32, 8), pair(48, 8)
            oh, pen, em = pair(64, NG), pair(72, NG), pair(80, NE)
            etop, eidx, esel = pair(144, 8), pair(160, 8), pair(176, 8)
            OH = rt[:, 192:320].rearrange("p (a e b) -> p a e b", a=2, e=2)
            negm, sums, ex, diff = rt[:, 384:386], rt[:, 386:388], rt[:, 388:390], rt[:, 390:392]
            wgt, pos, tmp = pair(400, 2), pair(404, 2), rt[:, 408:410]
            cnt, offx, incl = rt[:, 416:448], rt[:, 448:480], rt[:, 480:512]
            rank = pair(560, NE)
            prod = rt[:, 624:752].rearrange("p (a e b) -> p a e b", a=2, e=2)
            dve.wait_ge(padz, 3)
            dve.wait_ge(rlog_mm, 1)
            v.tensor_scalar(rlogT[0:NG + NE, :], QB[0:NG + NE, 0:T], V("b_router")[0:NG + NE], None,
                            ALU.add).then_inc(rlog_kept, 1)
            dve.wait_ge(rlog, 1)
            step(v.tensor_copy(gpad[:, :, 0:NG], lg[:, :, 0:NG]))
            for tt in range(NT):
                last = v.max(out=gtop[:, tt, :], in_=gpad[:, tt, :])
            step(last)
            for tt in range(NT):
                last = v.max_index(gidx[:, tt, :].bitcast(U32), gtop[:, tt, :], gpad[:, tt, :])
            step(last)
            step(v.tensor_copy(gsel[:, :, 0:1], gidx[:, :, 0:1].bitcast(U32)))
            step(v.tensor_tensor(oh, iota[:, 0:NG].unsqueeze(1).to_broadcast([P, 2, NG]),
                                 gsel[:, :, 0:1].to_broadcast([P, 2, NG]), ALU.is_equal))
            e4 = em.rearrange("p t (a b) -> p t a b", a=NG)
            v.tensor_scalar(pen, oh, -1.0, BIG, ALU.add, ALU.mult)
            step(v.tensor_tensor(e4, lg[:, :, NG:NG + NE].rearrange("p t (a b) -> p t a b", a=NG),
                                 oh.unsqueeze(3).to_broadcast([P, 2, NG, EPG]), ALU.mult))
            step(v.tensor_tensor(e4, e4, pen.unsqueeze(3).to_broadcast([P, 2, NG, EPG]), ALU.add))
            for tt in range(NT):
                last = v.max(out=etop[:, tt, :], in_=em[:, tt, :])
            step(last)
            for tt in range(NT):
                last = v.max_index(eidx[:, tt, :].bitcast(U32), etop[:, tt, :], em[:, tt, :])
            step(last)
            step(v.tensor_copy(esel[:, :, 0:2], eidx[:, :, 0:2].bitcast(U32)))
            step(v.tensor_tensor(OH, iota[:, 0:NE].unsqueeze(1).unsqueeze(1).to_broadcast([P, 2, 2, NE]),
                                 esel[:, :, 0:2].unsqueeze(3).to_broadcast([P, 2, 2, NE]), ALU.is_equal))
            v.tensor_tensor(pair(320, NE), OH[:, :, 0, :], OH[:, :, 1, :], ALU.add).then_inc(onehot, 1)
            v.tensor_scalar(negm, gtop[:, :, 0], -1.0, None, ALU.mult).then_inc(gate_neg, 1)
            v.tensor_tensor(diff, etop[:, :, 1], etop[:, :, 0], ALU.subtract).then_inc(topd, 1)
            dve.wait_ge(cnt_mm, 1)
            before = QB[:, 0:2 * NE].rearrange("p (a b) -> p a b", a=2)
            step(v.reduce_sum(cnt, QB[:, 2 * NE:4 * NE].rearrange("p (a b) -> p b a", a=2), axis=AX.X))
            step(v.tensor_tensor_scan(incl, ones[:, 0:NE], cnt, 0.0, ALU.mult, ALU.add))
            step(v.tensor_tensor(offx, incl, cnt, ALU.subtract))
            step(v.tensor_tensor(rank, before, offx.unsqueeze(1).to_broadcast([P, 2, NE]), ALU.add))
            step(v.tensor_tensor(rank[:, 1, :], rank[:, 1, :], QB[:, 2 * NE:3 * NE], ALU.add))
            step(v.tensor_tensor(prod, OH, rank.unsqueeze(2).to_broadcast([P, 2, 2, NE]), ALU.mult))
            step(v.reduce_sum(pos, prod, axis=AX.X))
            for tt in range(NT):
                step(v.tensor_scalar(r32(sel[:, tt, :]), iota, pos[:, tt, 0:1], None, ALU.is_equal))
                stt(r32(sel[:, tt, :]), iota, pos[:, tt, 1:2], r32(sel[:, tt, :]).bitcast(F32),
                    ALU.is_equal, ALU.add).then_inc(selected, 1)
            win = rt[:, 752:880].rearrange("p (e j) -> p e j", j=WINDOWS)
            v.reduce_max(tmp[:, 0:1], cnt, axis=AX.X)
            step(v.tensor_tensor(win, offx.unsqueeze(2).to_broadcast([P, NE, WINDOWS]),
                                 iota[:, 0:WINDOWS * WIN:WIN].unsqueeze(1).to_broadcast([P, NE, WINDOWS]), ALU.add))
            step(v.tensor_scalar(rt[:, 752:880], rt[:, 752:880], float(SLOTS), None, ALU.min))
            v.tensor_copy(rt[:, 880:1008].bitcast(I32), rt[:, 752:880])
            step(v.tensor_scalar(tmp[:, 0:1], tmp[:, 0:1], float(WIN), None, ALU.is_gt))
            v.tensor_copy(rt[:, 544:545].bitcast(I32), tmp[:, 0:1]).then_inc(offs, 1)
            dve.wait_ge(offs, 1)
            dve.wait_ge(expg, 2)
            dve.wait_ge(expt, 1)
            step(v.tensor_scalar(tmp, ex, 1.0, None, ALU.add))
            step(v.tensor_tensor(tmp, tmp, sums, ALU.mult))
            step(v.reciprocal(wgt[:, :, 0], tmp))
            step(v.tensor_tensor(wgt[:, :, 1], wgt[:, :, 0], ex, ALU.mult))
            for tt in range(NT):
                v.tensor_scalar(sw[:, tt, :], iota, pos[:, tt, 0:1], wgt[:, tt, 0:1], ALU.is_equal, ALU.mult)
                step(v.tensor_scalar(sw2, iota, pos[:, tt, 1:2], wgt[:, tt, 1:2], ALU.is_equal, ALU.mult))
                v.tensor_tensor(sw[:, tt, :], sw[:, tt, :], sw2, ALU.add).then_inc(weighted, 1)
                dve.wait_ge(weighted, tt + 1)
            def expert_act(it, c, w):
                b = c % 2
                gu = expert_banks(b)[0]
                t_ = th[0:WIN, b, 0:FF]
                stt(t_, t_, 1.0, gu[0:WIN, 0:FF], ALU.add, ALU.mult).then_inc(silu_e, 1)
                dve.wait_ge(silu_e, w)
                stt(th[0:WIN, b, FF:2 * FF], t_, 0.5, gu[WIN:2 * WIN, 0:FF]).then_inc(act_ready, 1)

            def out_keep(it, c, off):
                v.tensor_copy(ys[:, :, bass.ds(off, WIN)].rearrange("p (h q) s -> p h q s", h=2),
                              expert_banks(c % 2)[3][:, :].rearrange("p (q h s) -> p h q s", q=4, h=2)
                              ).then_inc(ys_done, 1)

            def expert_step(it, c):
                if it is not None or c < NE - 1:
                    since(dve, gate_t, it, c + 1)
                    since(dve, at_mm, it, c - 1)
                    expert_act(it, c + 1, (0 if it is None else it * 2) + (c + 2))
                if it is not None or c:
                    keep_step(it, c - 1)

            def keep_step(it, c):
                off = window_offset(dve, (0 if it is None else it * (2 * WINDOWS)) + c * WINDOWS)
                since(dve, yt_mm, it, c)
                since(dve, ys_done, it, c - 1)
                out_keep(it, c, off)

            crowded = dve.value_load(rt[0:1, 544:545].bitcast(I32), min_val=0, max_val=1)
            with dve.If(crowded):
                dve.wait_ge(swt_ready, 2)
                split("swt", SWT, SWT_hi, 0, 4)
                with dve.Fori(0, NE // 2) as it:
                    for c in range(2):
                        for j in range(WINDOWS):
                            n = c * WINDOWS + j
                            w = it * (2 * WINDOWS) + (n + 1)
                            off = window_offset(dve, it * (2 * WINDOWS) + n)
                            dve.wait_ge(gate_t, w)
                            expert_act(it, c, w)
                            dve.wait_ge(yt_mm, w)
                            out_keep(it, c, off)
                            dve.wait_ge(ys_done, w)
            with dve.Else():
                dve.wait_ge(xs_ready, DC)
                v.tensor_copy(xe[:, 0], xs[:, :, 0:WIN]).then_inc(xe_ready, 1)
                dve.wait_ge(swt_ready, 2)
                split("swt", SWT, SWT_hi, 0, 4)
                since(dve, gate_t, None, 0)
                expert_act(None, 0, 1)
                expert_steps(dve, expert_step)
                keep_step(None, NE - 1)
            def ysm_rest(n):
                dve.wait_ge(hi_of["ysm"], n + 1)
                piece = np.s_[:, n % 4, (n // 4) * 512:(n // 4 + 1) * 512]
                v.tensor_tensor(r32(ysm_lo[piece]), LB[n % 2][:, :], r32(ysm_hi[piece]).bitcast(F32),
                                ALU.subtract).then_inc(lo_of["ysm"], 1)

            def add_experts(i):
                dve.wait_ge(comb_mm, i + 1)
                r = xT[:, 2 * i:2 * i + 2, :]
                v.tensor_tensor(r, DB[i % 2][:, :].rearrange("p (a b) -> p a b", a=2), r, ALU.add).then_inc(comb, 1)

            for n in range(6):
                ysm_rest(n)
            add_experts(0)
            ysm_rest(6)
            add_experts(1)
            ysm_rest(7)
            add_experts(2)
            add_experts(3)
            dve.wait_ge(comb, 4)
            norm(N_OUT, lambda c: xT[:, c, :], lambda c: hT[:, c, :], "final_norm_2")



def chunks_of(w):
    k, m = w.shape
    return w.reshape(k // P, P, m // P, P).transpose(2, 1, 0, 3).reshape(m // P, P, k)


def k_major(w):
    k, m = w.shape
    return w.reshape(k // P, P, m).transpose(1, 0, 2)


def by_chunk(v):
    return v.reshape(-1, P).T


def units_of(a):
    return a.reshape(P, -1, UNIT).transpose(1, 0, 2)


def constants():
    f = np.float32
    t = np.arange(T, dtype=f)
    i = np.arange(P)
    c = {}
    c["ident"] = np.eye(P)
    c["mean64"] = ((i[:, None] // 64) == (i[None, :] // 64)) / 64.0
    r = i % 64
    partner = np.where(r < 8, i + 8, np.where(r < 16, i - 8, -1))
    c["swap"] = (i[:, None] == partner[None, :])
    c["before"] = i[:, None] < i[None, :]
    tok = np.concatenate([np.tile(i[:, None], (1, P)), np.tile(i[:, None] + P, (1, T))], 1)
    key = np.concatenate([np.arange(P), np.arange(T)])[None, :]
    c["causal"] = np.where(key <= tok, 0.0, -BIG)
    c["dist"] = np.where(key <= tok, -(tok - key), -BIG)

    def tables(rot):
        half = rot // 2
        inv = np.power(f(500000.0), -np.arange(half, dtype=f) / f(half)).astype(f)
        ang = (t[:, None] * inv[None, :]).astype(f)
        return np.cos(ang).T, np.sin(ang).T

    cos, sin = tables(ROPE)
    rows = i % 16
    c["cos_mla"] = cos[rows]
    c["sin_mla"] = sin[rows] * np.where(i % 32 < 16, -1.0, 1.0)[:, None]
    cos, sin = tables(MROT)
    c["cos_moba"] = np.where((r < 16)[:, None], cos[r % 8], 1.0)
    c["sin_moba"] = sin[r % 8] * np.where(r < 8, -1.0, np.where(r < 16, 1.0, 0.0))[:, None]
    c["iota"] = np.tile(np.arange(SLOTS), (P, 1))
    return np.ascontiguousarray(np.concatenate([c[n] for n in CST], 1).astype(f))


def pack(g):
    w = g["w_in"][0]
    cut = np.cumsum([0, 1024, 128, 512, 64, 8, 1024, 1024, 1024, 2048])
    q, ckv, qi, ki, wi, ga, xr, gr, mg = [w[:, a:b] for a, b in zip(cut[:-1], cut[1:])]
    w2 = g["w_in_2"][0]
    cut = np.cumsum([0, QL, KL, ROPE, 512, 512, 512, D, D])
    cq, ck, kr, qb, kb, vb, gA, gB = [w2[:, a:b] for a, b in zip(cut[:-1], cut[1:])]
    half = ROPE // 2
    uq = g["w_uq_2"][0].reshape(QL, H2, HD2 + ROPE)
    uq = np.concatenate([uq, uq[:, :, HD2 + half:], uq[:, :, HD2:HD2 + half]], 2)
    uqu = np.pad(chunks_of(uq.reshape(QL, H2 * P)), ((0, 0), (0, 0), (0, UNIT - QL)))
    ukv = g["w_ukv_2"][0].reshape(KL, H2, 2 * HD2)
    uk = chunks_of(ukv[:, :, :HD2].reshape(KL, 512)).transpose(1, 0, 2).reshape(P, UNIT)
    uv = k_major(ukv[:, :, HD2:].reshape(KL, 512)).reshape(P, UNIT)
    parts = [chunks_of(a) for a in (np.concatenate([ckv, ki, ki], 1), qi, xr, q, ga, gr, mg,
                                    g["w_rnn_proj"][0], g["w_attn_proj"][0], g["w_out"][0], cq, ck, qb, kb)]
    parts.append(units_of(k_major(vb).reshape(P, 4 * UNIT)))
    parts += [uqu, uk[None], uv[None], chunks_of(np.concatenate([gA, gB], 1))]
    for name in ("w_o_moba_2", "w_o_mla_2"):
        parts.append(units_of(chunks_of(g[name][0]).transpose(1, 0, 2).reshape(P, 4 * UNIT)))
    parts.append(chunks_of(g["w_out_2"][0]))
    dense = np.concatenate(parts, 0)
    dense = dense.reshape(-1, 2, P, UNIT).transpose(0, 2, 1, 3).reshape(-1, P, 2 * UNIT)
    gate, up, down = (g[n][0] for n in ("w_exp_gate_2", "w_exp_up_2", "w_exp_down_2"))
    gu = np.stack([gate, up], 1).reshape(NE, 2, 2, 4, P, FF).transpose(0, 2, 4, 1, 3, 5).reshape(NE, 2, P, 2 * UNIT)
    dn = down.reshape(NE, 2, P, D).transpose(0, 2, 1, 3).reshape(NE, P, 2 * UNIT)
    order = [gu[0, 0], gu[0, 1]]
    for e in range(NE - 1):
        order += [gu[e + 1, 0], gu[e + 1, 1], dn[e]]
    expert = np.stack(order + [dn[NE - 1]])
    idx2 = lambda a: np.concatenate([a, a])
    cols = {"conv_w": g["conv_w"][0].reshape(CONV * 8, P).T, "idx_ln_gain": idx2(g["idx_ln_gain"][0])[:, None],
            "idx_ln_bias": idx2(g["idx_ln_bias"][0])[:, None], "final_norm_gain": by_chunk(g["final_norm_gain"]),
            "final_norm_2": by_chunk(g["final_norm_2"]), "ones": np.ones((P, P), np.float32),
            "b_router": np.pad(np.concatenate([g["b_router_group_2"][0], g["b_router_expert_2"][0].reshape(-1)]),
                               (0, P - NG - NE))[:, None]}
    vecs = np.concatenate([cols[n] if n in cols else by_chunk(g[n][0]) for n in VEC], 1)
    rg = np.zeros((P, 2, 8, P), np.float32)
    for n, name in enumerate(("w_rg_a", "w_rg_x")):
        b = g[name][0].reshape(8, 2, 64, 64)
        for s in range(2):
            rg[64 * s:64 * s + 64, n, :, 64 * s:64 * s + 64] = b[:, s].transpose(1, 0, 2)
    wuk = g["w_uk"][0].transpose(1, 0, 2).reshape(LAT, H1 * HD1)
    wuv = g["w_uv"][0].transpose(1, 0, 2).reshape(LAT, H1 * HD1)
    wkr = k_major(np.concatenate([kr, kr[:, half:], kr[:, :half]], 1)).reshape(P, -1)
    wre = g["w_router_expert_2"][0].transpose(1, 0, 2).reshape(D, NE)
    wrt = k_major(np.concatenate([g["w_router_group_2"][0], wre], 1)).reshape(P, -1)
    x_t = g["x"][0].T.reshape(DC, P, T).transpose(1, 0, 2).reshape(P, DC * T)
    arrays = dict(x_t=x_t, vecs=vecs, consts=constants(), w_widx=k_major(wi).reshape(P, -1),
                  w_rg=rg.reshape(P, -1), w_uk=wuk, w_uv=wuv, w_kr=wkr, w_router=wrt,
                  w_dense=dense, w_expert=expert)
    return {k: np.ascontiguousarray(v) for k, v in arrays.items()}


def kernel(**inputs):
    import concourse.bacc as bacc
    from concourse.bass_utils import run_bass_kernel_spmd

    arrays = pack({k: np.asarray(v) for k, v in inputs.items()})
    nc = bacc.Bacc("TRN2", target_bir_lowering=False, num_devices=1)
    aps = {n: nc.dram_tensor(f"{n}_dram", a.shape, mybir.dt.from_np(a.dtype), kind="ExternalInput").ap()
           for n, a in arrays.items()}
    out = nc.dram_tensor("out_dram", (P, DC * T), F32, kind="ExternalOutput").ap()
    build(nc, out=out, **aps)
    r = run_bass_kernel_spmd(nc, [{f"{n}_dram": a for n, a in arrays.items()}], core_ids=[0])
    y = r.results[0]["out_dram"].reshape(P, DC, T)
    return np.ascontiguousarray(y.transpose(2, 1, 0).reshape(1, T, D))
```
